# Optimizing a Trainium2 kernel written in Bass

```python
import jax, jax.numpy as jnp
from jax import lax
import numpy as np

D_MODEL = 2048
BATCH = 1
SEQ = 256
DEPTH = 1

CHUNK = 64
EPS = 1e-6

GLA_HEADS = 4
GLA_WIDTH = D_MODEL // 2
GLA_DV = GLA_WIDTH // GLA_HEADS
GLA_DK = GLA_DV // 2
GLA_QK = GLA_HEADS * GLA_DK
GLA_GATE_RANK = 16
GLA_TAU = 16.0

MLSTM_HEADS = 4
MLSTM_WIDTH = D_MODEL - GLA_WIDTH
MLSTM_DV = MLSTM_WIDTH // MLSTM_HEADS
MLSTM_DK = MLSTM_DV // 2
MLSTM_QK = MLSTM_HEADS * MLSTM_DK
CONV_WIDTH = 4

IN_SPLITS = (GLA_QK, GLA_QK, GLA_WIDTH, GLA_WIDTH, GLA_GATE_RANK,
             MLSTM_QK, MLSTM_QK, MLSTM_WIDTH, MLSTM_WIDTH, MLSTM_HEADS, MLSTM_HEADS)
IN_COLS = sum(IN_SPLITS)

PEER_HEADS = 8
N_KEYS = 128
N_EXPERTS = N_KEYS * N_KEYS
PEER_QDIM = 256
PEER_TOPK = 16
PEER_BLOCK = 128

PLE_DIM = 256

kernel_name = "hybrid_gla_mlstm_peer_ple"

def rmsnorm(x, g):
    xf = x.astype(jnp.float32)
    y = xf * lax.rsqrt(jnp.mean(xf * xf, axis=-1, keepdims=True) + EPS)
    return (y * g.astype(jnp.float32)).astype(x.dtype)

def head_rmsnorm(h, g, n_heads):
    b, s, w = h.shape
    hh = h.reshape(b, s, n_heads, w // n_heads)
    hh = hh * lax.rsqrt(jnp.mean(hh * hh, axis=-1, keepdims=True) + EPS)
    return hh.reshape(b, s, w) * g.astype(jnp.float32)

def split_cols(proj):
    out, start = [], 0
    for n in IN_SPLITS:
        out.append(proj[..., start:start + n])
        start += n
    return out

def to_chunks(t, n_heads):
    b, s, w = t.shape
    t = t.reshape(b, s // CHUNK, CHUNK, n_heads, w // n_heads)
    return t.transpose(1, 0, 3, 2, 4).astype(jnp.float32)

def from_chunks(t):
    nc, b, h, l, d = t.shape
    return t.transpose(1, 0, 3, 2, 4).reshape(b, nc * l, h * d)

def gates_to_chunks(t):
    b, s, h = t.shape
    return t.reshape(b, s // CHUNK, CHUNK, h).transpose(1, 0, 3, 2).astype(jnp.float32)

def causal_dwconv(x, w, bias):
    out = lax.conv_general_dilated(
        x, w[:, None, :].astype(x.dtype), window_strides=(1,),
        padding=[(CONV_WIDTH - 1, 0)],
        dimension_numbers=('NWC', 'WIO', 'NWC'),
        feature_group_count=x.shape[-1])
    return out + bias.astype(x.dtype)

def gla_chunked(q, k, v, log_a):
    mask = jnp.tril(jnp.ones((CHUNK, CHUNK), dtype=bool))
    nb, nh = q.shape[1], q.shape[2]

    def step(state, inp):
        qc, kc, vc, gc = inp
        b = jnp.cumsum(gc, axis=2)
        diff = b[:, :, :, None, :] - b[:, :, None, :, :]
        decay = jnp.exp(jnp.where(mask[:, :, None], diff, -jnp.inf))
        scores = jnp.sum(qc[:, :, :, None, :] * kc[:, :, None, :, :] * decay, axis=-1)
        o = scores @ vc + jnp.einsum('bhid,bhdv->bhiv', qc * jnp.exp(b), state)
        b_last = b[:, :, -1, :]
        k_dec = kc * jnp.exp(b_last[:, :, None, :] - b)
        state = jnp.exp(b_last)[..., None] * state + jnp.einsum('bhjd,bhjv->bhdv', k_dec, vc)
        return state, o

    s0 = jnp.zeros((nb, nh, GLA_DK, GLA_DV), jnp.float32)
    _, o = lax.scan(step, s0, (q, k, v, log_a))
    return o

def mlstm_chunked(q, k, v, ig, logf):
    mask = jnp.tril(jnp.ones((CHUNK, CHUNK), dtype=bool))
    nb, nh = q.shape[1], q.shape[2]

    def step(carry, inp):
        c_st, n_st, m_st = carry
        qc, kc, vc, ic, fc = inp
        f_cum = jnp.cumsum(fc, axis=-1)
        dmat = jnp.where(mask, f_cum[..., :, None] - f_cum[..., None, :] + ic[..., None, :], -jnp.inf)
        inter = f_cum + m_st[..., None]
        m_row = jnp.maximum(jnp.max(dmat, axis=-1), inter)
        w = jnp.exp(dmat - m_row[..., None])
        s = jnp.einsum('bhid,bhjd->bhij', qc, kc) * w
        w_inter = jnp.exp(inter - m_row)
        num = s @ vc + w_inter[..., None] * jnp.einsum('bhid,bhdv->bhiv', qc, c_st)
        den = jnp.sum(s, axis=-1) + w_inter * jnp.einsum('bhid,bhd->bhi', qc, n_st)
        h = num / jnp.maximum(jnp.abs(den), jnp.exp(-m_row))[..., None]
        f_last = f_cum[..., -1]
        wlog = f_last[..., None] - f_cum + ic
        m_new = jnp.maximum(f_last + m_st, jnp.max(wlog, axis=-1))
        wk = jnp.exp(wlog - m_new[..., None])
        carry_dec = jnp.exp(f_last + m_st - m_new)
        c_st = carry_dec[..., None, None] * c_st + jnp.einsum('bhj,bhjd,bhjv->bhdv', wk, kc, vc)
        n_st = carry_dec[..., None] * n_st + jnp.einsum('bhj,bhjd->bhd', wk, kc)
        return (c_st, n_st, m_new), h

    init = (jnp.zeros((nb, nh, MLSTM_DK, MLSTM_DV), jnp.float32),
            jnp.zeros((nb, nh, MLSTM_DK), jnp.float32),
            jnp.zeros((nb, nh), jnp.float32))
    _, h = lax.scan(step, init, (q, k, v, ig, logf))
    return h

def token_mixers(xn, w_in, gla_gate_up, gla_gate_bias, gla_norm, conv_w, conv_b,
                 igate_bias, fgate_bias, mlstm_norm, w_out):
    gq, gk, gv, gg, glr, mq, mk, mv, mo, mi, mf = split_cols(xn @ w_in)
    log_a = jax.nn.log_sigmoid((glr @ gla_gate_up + gla_gate_bias).astype(jnp.float32)) / GLA_TAU
    o_gla = gla_chunked(to_chunks(gq, GLA_HEADS) * (GLA_DK ** -0.5), to_chunks(gk, GLA_HEADS),
                        to_chunks(gv, GLA_HEADS), to_chunks(log_a, GLA_HEADS))
    y_gla = head_rmsnorm(from_chunks(o_gla), gla_norm, GLA_HEADS) * jax.nn.silu(gg.astype(jnp.float32))
    qk = jax.nn.silu(causal_dwconv(jnp.concatenate([mq, mk], axis=-1), conv_w, conv_b))
    mq_c, mk_c = qk[..., :MLSTM_QK], qk[..., MLSTM_QK:]
    ig = gates_to_chunks(mi + igate_bias)
    logf = jax.nn.log_sigmoid(gates_to_chunks(mf + fgate_bias))
    h = mlstm_chunked(to_chunks(mq_c, MLSTM_HEADS), to_chunks(mk_c, MLSTM_HEADS) * (MLSTM_DK ** -0.5),
                      to_chunks(mv, MLSTM_HEADS), ig, logf)
    y_m = jax.nn.sigmoid(mo.astype(jnp.float32)) * head_rmsnorm(from_chunks(h), mlstm_norm, MLSTM_HEADS)
    y = jnp.concatenate([y_gla, y_m], axis=-1).astype(xn.dtype)
    return y @ w_out

def peer_ffn(xn, w_query, sub_keys, expert_u, expert_v):
    b, s, d = xn.shape
    xt = xn.reshape(-1, PEER_BLOCK, d)

    def block(xb):
        q = (xb @ w_query).reshape(PEER_BLOCK, PEER_HEADS, 2, PEER_QDIM // 2).astype(jnp.float32)
        sc = jnp.einsum('thpd,hpkd->thpk', q, sub_keys.astype(jnp.float32))
        sv, si = lax.top_k(sc, PEER_TOPK)
        cand = (sv[:, :, 0, :, None] + sv[:, :, 1, None, :]).reshape(PEER_BLOCK, PEER_HEADS, PEER_TOPK * PEER_TOPK)
        cidx = (si[:, :, 0, :, None] * N_KEYS + si[:, :, 1, None, :]).reshape(PEER_BLOCK, PEER_HEADS, PEER_TOPK * PEER_TOPK)
        top_s, pos = lax.top_k(cand, PEER_TOPK)
        idx = jnp.take_along_axis(cidx, pos, axis=-1)
        g = jax.nn.softmax(top_s, axis=-1)
        a = jax.nn.gelu(jnp.einsum('thkd,td->thk', expert_u[idx], xb).astype(jnp.float32))
        return jnp.einsum('thk,thkd->td', (g * a).astype(xb.dtype), expert_v[idx])

    return lax.map(block, xt).reshape(b, s, d)

def setup_inputs(seed: int = 0) -> dict:
    key = jax.random.key(seed)
    ks = jax.random.split(key, 24)
    f32 = jnp.float32

    def nrm(k, shape, scale):
        return jax.random.normal(k, shape, f32) * scale

    def gain(k, shape):
        return 1.0 + 0.02 * jax.random.normal(k, shape, f32)

    return {
        "x": nrm(ks[0], (BATCH, SEQ, D_MODEL), 1.0),
        "p": nrm(ks[1], (DEPTH, BATCH, SEQ, PLE_DIM), 1.0),
        "norm_mix": gain(ks[2], (DEPTH, D_MODEL)),
        "w_in": nrm(ks[3], (DEPTH, D_MODEL, IN_COLS), D_MODEL ** -0.5),
        "gla_gate_up": nrm(ks[4], (DEPTH, GLA_GATE_RANK, GLA_QK), GLA_GATE_RANK ** -0.5),
        "gla_gate_bias": nrm(ks[5], (DEPTH, GLA_QK), 0.1),
        "gla_norm": gain(ks[6], (DEPTH, GLA_WIDTH)),
        "mlstm_conv_w": nrm(ks[7], (DEPTH, CONV_WIDTH, 2 * MLSTM_QK), CONV_WIDTH ** -0.5),
        "mlstm_conv_b": nrm(ks[8], (DEPTH, 2 * MLSTM_QK), 0.02),
        "mlstm_igate_bias": nrm(ks[9], (DEPTH, MLSTM_HEADS), 0.1),
        "mlstm_fgate_bias": 3.0 + 3.0 * jax.random.uniform(ks[10], (DEPTH, MLSTM_HEADS), f32),
        "mlstm_norm": gain(ks[11], (DEPTH, MLSTM_WIDTH)),
        "w_out": nrm(ks[12], (DEPTH, GLA_WIDTH + MLSTM_WIDTH, D_MODEL), (GLA_WIDTH + MLSTM_WIDTH) ** -0.5),
        "norm_ffn": gain(ks[13], (DEPTH, D_MODEL)),
        "peer_query": nrm(ks[14], (DEPTH, D_MODEL, PEER_HEADS * PEER_QDIM), D_MODEL ** -0.5),
        "peer_sub_keys": nrm(ks[15], (DEPTH, PEER_HEADS, 2, N_KEYS, PEER_QDIM // 2), (PEER_QDIM // 2) ** -0.5),
        "peer_u": nrm(ks[16], (DEPTH, N_EXPERTS, D_MODEL), D_MODEL ** -0.5),
        "peer_v": nrm(ks[17], (DEPTH, N_EXPERTS, D_MODEL), 0.5),
        "norm_ple": gain(ks[18], (DEPTH, D_MODEL)),
        "w_ple": nrm(ks[19], (DEPTH, PLE_DIM, D_MODEL), PLE_DIM ** -0.5),
        "w_ple_gate": nrm(ks[20], (DEPTH, D_MODEL, D_MODEL), D_MODEL ** -0.5),
        "norm_final": gain(ks[21], (D_MODEL,)),
    }

def reference(x, p, norm_mix, w_in, gla_gate_up, gla_gate_bias, gla_norm, mlstm_conv_w,
              mlstm_conv_b, mlstm_igate_bias, mlstm_fgate_bias, mlstm_norm, w_out, norm_ffn,
              peer_query, peer_sub_keys, peer_u, peer_v, norm_ple, w_ple, w_ple_gate, norm_final):
    h = x
    for i in range(DEPTH):
        h = h + token_mixers(rmsnorm(h, norm_mix[i]), w_in[i], gla_gate_up[i], gla_gate_bias[i],
                             gla_norm[i], mlstm_conv_w[i], mlstm_conv_b[i], mlstm_igate_bias[i],
                             mlstm_fgate_bias[i], mlstm_norm[i], w_out[i])
        h = h + peer_ffn(rmsnorm(h, norm_ffn[i]), peer_query[i], peer_sub_keys[i], peer_u[i], peer_v[i])
        gate = jax.nn.sigmoid(rmsnorm(h, norm_ple[i]) @ w_ple_gate[i])
        h = h + gate * (p[i] @ w_ple[i])
    return rmsnorm(h, norm_final)


_drawn_inputs = setup_inputs


def setup_inputs(seed=0):
    import zlib

    import numpy as np

    out = dict(_drawn_inputs(seed))
    spreads = {}
    factors = {'gla_norm': 24.06,
     'mlstm_conv_b': 3.103,
     'mlstm_igate_bias': 64.0,
     'mlstm_norm': 26.463,
     'norm_ple': 200.0,
     'norm_final': 21.194,
     'norm_ffn': 9.271}
    for name, (base, spread) in spreads.items():
        noise = np.random.default_rng([zlib.crc32(name.encode()), seed]).standard_normal(out[name].shape)
        drawn = base * np.exp(spread * noise) if base else spread * noise
        out[name] = __import__('jax').numpy.asarray(drawn.astype(out[name].dtype))
    for name, factor in factors.items():
        out[name] = (out[name] * factor).astype(out[name].dtype)
    return out
```

```python
from contextlib import ExitStack

import concourse.bass as bass
from concourse import mybir

F32 = mybir.dt.float32
F32R = mybir.dt.float32r
BF16 = mybir.dt.bfloat16
I32 = mybir.dt.int32
U32 = mybir.dt.uint32
U8 = mybir.dt.uint8
ALU = mybir.AluOpType
ACT = mybir.ActivationFunctionType
AXX = mybir.AxisListType.X

P = 128


def build(nc, x, p, norm_mix, w_in, gate_up, gate_bias, gla_norm, conv_w, conv_b, ig_bias, fg_bias,
          mlstm_norm, w_out, norm_ffn, peer_query, sub_keys, peer_u, peer_v, norm_ple, w_ple,
          w_ple_gate, norm_final, out):
    _, S, D = x.shape
    NB = S // P
    KT = D // P
    CW = 512
    NQ = 4
    KQ = KT // NQ
    EPS = 1e-6
    RANK, GQK = gate_up.shape[1:]
    H = 4
    DK = GQK // H
    DV = gla_norm.shape[1] // H
    W2 = H * DV
    TAU = 16.0
    KSC = float(DK) ** -0.5
    CONV = conv_w.shape[1]
    PH, NK = sub_keys.shape[1], sub_keys.shape[3]
    TOPK = 16
    G = NB * PH
    PLE = p.shape[3]
    LEVELS = P.bit_length() - 1
    DEEP = 4
    NEG = -3.0e38
    BIG = 1.0e30

    GLR = 2 * GQK + 2 * W2
    C2 = GLR + RANK
    GATES = C2 + 2 * GQK + 2 * W2
    NSM = RANK + 2 * H
    NA = (GLR + GATES - C2) // CW
    NA1 = GLR // CW
    ND = D // CW
    gA, gB, gQ, gG = 0, NA, NA + ND, NA + 2 * ND

    def slices(w):
        v = w.rearrange("(q k p) n -> q p k n", k=KQ, p=P)
        return [v[q] for q in range(NQ)]

    ctx = ExitStack()
    with ctx:
        KB = 1024

        def at(name, shape, dt, off):
            return nc.alloc_sbuf_tensor_at(name, shape, dt, offset=off)

        base, top = 16512, 229344
        used = [base]

        def next_to(name, shape, dt):
            n = 1
            for s in shape[1:]:
                n *= s
            size = n * (2 if dt == BF16 else 1 if dt == U8 else 4)
            t = at(name, shape, dt, used[0])
            used[0] += (size + 31) // 32 * 32
            return t

        h = next_to("h", [P, NB, D], F32)
        t_hi = next_to("t_hi", [P, KT, S], F32R)
        t_lo = next_to("t_lo", [P, KT, S], F32R)
        v_ring = at("v_ring", [P, DEEP, D], F32, base + 16 * KB)
        raw = next_to("raw", [P, NQ, KQ, CW], F32)
        w_hi = next_to("w_hi", [P, 2, KQ, CW], F32R)
        w_lo = next_to("w_lo", [P, 2, KQ, CW], F32R)
        nrow = next_to("nrow", [P, D], F32)
        ident = next_to("ident", [P, P], F32)
        NPAR = 3 * KT + 4 + CONV * 8 + 8
        par = next_to("par", [P, NPAR], F32)
        mask = next_to("mask", [P, LEVELS + 1, P], U8)
        cbias = next_to("cbias", [P, P], F32)
        zero16 = next_to("zero16", [P, CW], BF16)
        diag = next_to("diag", [P, DEEP, P], F32)
        stat = next_to("stat", [P, 64], F32)
        nwt = next_to("nwt", [P, 8], F32)
        scope = used[0]
        pM, pG, pP, pB, pC, pCB = 0, KT, 2 * KT, 3 * KT, 3 * KT + 4, 3 * KT + 4 + 8 * CONV

        y = next_to("y", [P, NB, D], F32)
        off_q = used[0]
        gq = next_to("gq", [P, H, S], F32)
        gk = next_to("gk", [P, H, S], F32)
        conv = at("conv", [P, 2 * H, S], F32, off_q)
        gv = next_to("gv", [P, NB, W2], F32)
        mv = next_to("mv", [P, NB, W2], F32)
        cin = next_to("cin", [P, 2 * H, CONV - 1 + S], F32)
        tfp = next_to("tfp", [P, 2, KT // 2, P], F32)
        st = next_to("st", [P, NB, H, P], F32)
        stx = next_to("stx", [P, H, P], F32)
        cum = next_to("cum", [P, H, S], F32)
        rowm = next_to("rowm", [P, 5, S], F32)
        glr = next_to("glr", [RANK, S], F32)
        gup = next_to("gup", [RANK, GQK], F32)
        gbias = next_to("gbias", [H, 2], F32)
        sm = next_to("sm", [P, NB, NSM], F32)
        ones = next_to("ones", [P, 1], F32)
        sel = next_to("sel", [H, H, P], F32)
        mixer_end = used[0]
        stack = at("stack", [NPAR, P], F32, off_q)
        wsm = at("wsm", [P, KT, NSM], F32, off_q + 16 * KB)
        wsm_hi = at("wsm_hi", [P, KT, NSM], F32R, off_q + 18 * KB)
        wsm_lo = at("wsm_lo", [P, KT, NSM], F32R, off_q + 20 * KB)
        it_i = at("it_i", [P, P], I32, off_q + 22 * KB)
        it_p = at("it_p", [P, P], I32, off_q + 22 * KB + 512)
        it_x = at("it_x", [P, P], I32, off_q + 23 * KB)
        it_s = at("it_s", [P, P], I32, off_q + 23 * KB + 512)
        it_u = at("it_u", [P, P], F32, off_q + 22 * KB)

        used[0] = scope
        xn2 = next_to("xn2", [P, NB, D], F32)
        off_sc = used[0]
        sc = next_to("sc", [P, G, 2 * NK], F32)
        wple = at("wple", [P, PLE // P, D], F32, off_sc)
        off_u = used[0]
        u_ring = next_to("u_ring", [P, DEEP, D], F32)
        keys = at("keys", [P, 2 * PH, P], F32, off_u)
        gt = at("gt", [P, 2, NB, CW], F32, off_u)
        off_qt = used[0]
        qt = next_to("qt", [P, 4, S], F32)
        pin = at("pin", [P, NB, PLE], F32, off_qt)
        pt = at("pt", [P, PLE // P, S], F32, off_qt + 2 * KB)
        keyst = next_to("keyst", [P, 2 * PH, P], F32)
        s2 = next_to("s2", [P, 2, NK], F32)
        wk = next_to("wk", [P, 2, NK], F32)
        cand = next_to("cand", [P, TOPK, TOPK], F32)
        oh = next_to("oh", [P, TOPK, TOPK], F32)
        i16 = next_to("i16", [P, TOPK], F32)
        tv = next_to("tv", [P, 2, TOPK], F32)
        ti = next_to("ti", [P, 2, TOPK], U32)
        tif = next_to("tif", [P, 2, TOPK], F32)
        cv = next_to("cv", [P, TOPK], F32)
        ci = next_to("ci", [P, TOPK], U32)
        cij = next_to("cij", [P, 2, TOPK], U32)
        cijf = next_to("cijf", [P, 2, TOPK], F32)
        pick = next_to("pick", [P, 2, TOPK], F32)
        idxn = next_to("idxn", [P, TOPK], U32)
        idxu = next_to("idxu", [P, 2, TOPK], U32)
        idxv = next_to("idxv", [P, 2, TOPK], U32)
        topc = next_to("topc", [P, TOPK], F32)
        ex = next_to("ex", [P, TOPK], F32)
        act_a = next_to("act_a", [P, TOPK], F32)
        dots = next_to("dots", [P, TOPK], F32)
        wgt = next_to("wgt", [P, TOPK], F32)
        tick = next_to("tick", [P, 2 * TOPK + 4], F32)
        esm = next_to("esm", [P, 8], F32)
        expert_end = used[0]
        assert max(mixer_end, expert_end) <= top, (mixer_end, expert_end)

        def pair(name):
            return ctx.enter_context(nc.psum_tensor(name, [P, 2 * CW], F32))

        acc = [pair("acc0"), pair("acc1")]
        mix = [pair("mix0"), pair("mix1")]

        def sem(name):
            return ctx.enter_context(nc.semaphore(name))

        x_in = [sem(f"x_in{b}") for b in range(NB)]
        par_in, wsm_in, gup_in, gb_in = sem("par_in"), sem("wsm_in"), sem("gup_in"), sem("gb_in")
        keys_in, nffn_in, nfin_in, p_in, wple_in = (sem(n) for n in ("keys_in", "nffn_in", "nfin_in", "p_in", "wple_in"))
        raw_in = [sem(f"raw_in{q}") for q in range(NQ)]
        hi_done, lo_done, slice_used = sem("hi_done"), sem("lo_done"), sem("slice_used")
        acc_free = [sem(f"acc_free{i}") for i in range(2)]
        mix_ready = sem("mix_ready")
        mix_free = [sem(f"mix_free{i}") for i in range(2)]
        const_ready, mask_ready = sem("const_ready"), sem("mask_ready")
        evac = sem("evac")
        tf_ready, thi_done, tlo_done = sem("tf_ready"), sem("thi_done"), sem("tlo_done")
        ssq_ready, var_ready, sqrt_ready = sem("ssq_ready"), sem("var_ready"), sem("sqrt_ready")
        src_ready = sem("src_ready")
        smw_hi, smw_lo, sm_ready, smt_ready = sem("smw_hi"), sem("smw_lo"), sem("sm_ready"), sem("smt_ready")
        abs_ready, softp = sem("abs_ready"), sem("softp")
        diff_ready, decay_ready, qk_ready = sem("diff_ready"), sem("decay_ready"), sem("qk_ready")
        st_ready, y_ready = sem("st_ready"), sem("y_ready")
        hsq_ready, hvar_ready, hsqrt_ready = sem("hsq_ready"), sem("hvar_ready"), sem("hsqrt_ready")
        conv_ready, silu_ready, rows_ready, cols_ready = sem("conv_ready"), sem("silu_ready"), sem("rows_ready"), sem("cols_ready")
        expo_ready, wexp_ready = sem("expo_ready"), sem("wexp_ready")
        denr_ready = sem("denr_ready")
        keyst_ready = sem("keyst_ready")
        xn2_ready, h_ready = sem("xn2_ready"), sem("h_ready")
        idx_ready, idx_taken = sem("idx_ready"), sem("idx_taken")
        u_in = [sem(f"u_in{i}") for i in range(DEEP)]
        v_in = [sem(f"v_in{i}") for i in range(DEEP)]
        u_free, v_free = sem("u_free"), sem("v_free")
        top_ready, gelu_ready, w_ready, diag_ready = sem("top_ready"), sem("gelu_ready"), sem("w_ready"), sem("diag_ready")
        exp_ready = sem("exp_ready")
        peer_ready, peer_taken = sem("peer_ready"), sem("peer_taken")
        pt_ready, gate_ready, out_ready, out_done = sem("pt_ready"), sem("gate_ready"), sem("out_ready"), sem("out_done")

        names = ["par"] + [f"tA{i}" for i in range(4)] + ["sm", "smt", "z"]
        names += ["lvd"] + [f"lv{n}" for n in range(LEVELS + 1)] + ["go0", "go1"]
        names += ["cols", "mbc", "ps", "psx", "den", "mo0", "mo1"]
        names += [f"tB{i}" for i in range(4)] + ["key0", "key1"]
        names += [f"tQ{i}" for i in range(4)] + [f"sc{c}" for c in range(ND)]
        n_before_peer = len(names)
        names += ["pt"] + [f"tG{i}" for i in range(4)] + [f"pl{c}" for c in range(ND)]
        M = {n: i for i, n in enumerate(names)}

        def mix_of(name):
            return mix[M[name] % 2]

        def wait_mix(eng, name):
            eng.wait_ge(mix_ready, M[name] + 1)

        def free_sem(name):
            return mix_free[M[name] % 2]

        def take_mix(pe, name):
            m = M[name]
            if m >= n_before_peer and m < n_before_peer + 2:
                pe.wait_ge(peer_taken, 1)
            elif m >= 2:
                pe.wait_ge(mix_free[m % 2], m // 2)

        def src_blocks(phase):
            return {"A": y, "B": y, "Q": xn2, "G": xn2}[phase]

        PH_NO = {"A": 0, "B": 1, "Q": 2, "G": 3}
        SLICES_BEFORE = {"A": 0, "B": NQ * gB, "Q": NQ * gQ, "G": NQ * gG}

        with nc.Block() as block:

            @block.sync
            def _(sp):
                for b in range(NB):
                    sp.dma_start(h[:, b, :], x[0, b * P:(b + 1) * P, :]).then_inc(x_in[b], 16)

                def stream(w, g0, n, col0):
                    quarter = slices(w)

                    def chunk(g, col):
                        for q in range(NQ):
                            if not (isinstance(g, int) and g == 0):
                                sp.wait_ge(lo_done, g * NQ + q - NQ + 1)
                            sp.dma_start(raw[:, q, :, :], quarter[q][:, :, col]).then_inc(raw_in[q], 16)

                    first = 1 if g0 == 0 else 0
                    if first:
                        chunk(0, slice(col0, col0 + CW))
                    with sp.Fori(first, n) as c:
                        chunk(c + g0, bass.ds(c * CW + col0, CW))

                stream(w_in[0], gA, NA1, 0)
                stream(w_in[0], gA + NA1, NA - NA1, C2)
                stream(w_out[0], gB, ND, 0)
                stream(peer_query[0], gQ, ND, 0)
                sp.wait_ge(xn2_ready, NB)
                sp.dma_start(nrow[:, :], norm_final.partition_broadcast(P)).then_inc(nfin_in, 16)
                stream(w_ple_gate[0], gG, ND, 0)
                for b in range(NB):
                    sp.wait_ge(out_ready, b + 1)
                    sp.dma_start(out[0, b * P:(b + 1) * P, :], h[:, b, :]).then_inc(out_done, 16)
                sp.wait_ge(out_done, 16 * NB)

            @block.gpsimd
            def _(pool):
                def rows(dst0, vec, n):
                    pool.dma_start(stack[dst0:dst0 + n, :], vec).then_inc(par_in, 16)

                nc.gpsimd.memset(ident[:, :], 0.0)
                rows(pM, norm_mix.rearrange("a (k p) -> (a k) p", p=P), KT)
                rows(pG, gla_norm.rearrange("a (k p) -> (a k) p", p=P), KT // 2)
                rows(pG + KT // 2, mlstm_norm.rearrange("a (k p) -> (a k) p", p=P), KT // 2)
                rows(pP, norm_ple.rearrange("a (k p) -> (a k) p", p=P), KT)
                rows(pB, gate_bias.rearrange("a (k p) -> (a k) p", p=P), 4)
                rows(pC, conv_w.rearrange("a t (k p) -> (a t k) p", p=P), 8 * CONV)
                rows(pCB, conv_b.rearrange("a (k p) -> (a k) p", p=P), 8)
                pool.drain()
                nc.gpsimd.affine_select(out=ident[:, :], in_=ident[:, :], compare_op=ALU.not_equal, fill=1.0,
                                        base=0, pattern=[[-1, P]], channel_multiplier=1)
                nc.gpsimd.iota(it_i[:, :], pattern=[[1, P]], base=0, channel_multiplier=0)
                nc.gpsimd.iota(it_p[:, :], pattern=[[0, P]], base=0, channel_multiplier=1)
                nc.gpsimd.memset(cbias[:, :], 0.0)
                nc.gpsimd.memset(sel[:, :, :], 0.0)
                nc.gpsimd.memset(ones[:, :], 1.0)
                nc.gpsimd.memset(zero16[:, :], 0.0)
                nc.gpsimd.memset(cin[:, :, 0:CONV - 1], 0.0)
                pool.drain()
                nc.gpsimd.affine_select(out=cbias[:, :], in_=cbias[:, :], compare_op=ALU.is_ge, fill=BIG,
                                        base=0, pattern=[[1, P]], channel_multiplier=-1)
                nc.gpsimd.affine_select(out=sel[:, :, :], in_=sel[:, :, :], compare_op=ALU.not_equal, fill=1.0,
                                        base=0, pattern=[[-1, H], [0, P]], channel_multiplier=1)
                pool.drain().then_inc(const_ready, 1)
                wv = w_in[0].rearrange("(k p) n -> p k n", p=P)
                pool.dma_start(wsm[:, :, 0:RANK], wv[:, :, GLR:GLR + RANK]).then_inc(wsm_in, 16)
                pool.dma_start(wsm[:, :, RANK:NSM], wv[:, :, GATES:GATES + 2 * H]).then_inc(wsm_in, 16)
                pool.dma_start(gup[:, :], gate_up[0]).then_inc(gup_in, 16)
                pool.dma_start(gbias[:, 0:1], ig_bias.rearrange("a h -> h a")).then_inc(gb_in, 16)
                pool.dma_start(gbias[:, 1:2], fg_bias.rearrange("a h -> h a")).then_inc(gb_in, 16)
                pool.dma_start(nrow[:, :], norm_ffn[0].partition_broadcast(P)).then_inc(nffn_in, 16)
                pool.wait_ge(tlo_done, 8)
                pool.dma_start(keys[:, :, :], sub_keys[0].rearrange("h t k d -> k (h t) d")).then_inc(keys_in, 16)
                nc.gpsimd.iota(ti[:, 0, :], pattern=[[1, TOPK]], base=0, channel_multiplier=0)
                pool.drain()
                nc.gpsimd.tensor_copy(i16[:, :], ti[:, 0, :]).then_inc(const_ready, 1)

                u_rows, v_rows = peer_u[0], peer_v[0]

                def step(g, e, up, down):
                    if up:
                        pool.wait_ge(idx_ready, g + 1)
                        nc.gpsimd.tensor_tensor(tick[:, 2 * TOPK:2 * TOPK + 1], tick[:, 2 * TOPK + 1:2 * TOPK + 2], tick[:, 2 * TOPK + 2:2 * TOPK + 3], ALU.add)
                    if down:
                        nc.gpsimd.tensor_copy(idxv[:, e, :], idxu[:, 1 - e, :])
                        pool.drain()
                    if up:
                        nc.gpsimd.tensor_copy(idxu[:, e, :], idxn[:, :]).then_inc(idx_taken, 1)
                        pool.drain()
                    for k in range(TOPK):
                        if up:
                            pool.wait_ge(u_free, g * TOPK + k + 1)
                            nc.gpsimd.tensor_tensor(tick[:, 2 * k:2 * k + 1], tick[:, 2 * TOPK + 1:2 * TOPK + 2], tick[:, 2 * TOPK + 2:2 * TOPK + 3], ALU.add)
                            nc.gpsimd.indirect_dma_start(
                                u_ring[:, k % DEEP, :], None, u_rows,
                                bass.IndirectOffsetOnAxis(idxu[:, e, k:k + 1], 0)).then_inc(u_in[k % DEEP], 16)
                        if down:
                            pool.wait_ge(v_free, (g - 1) * TOPK + k + 1)
                            nc.gpsimd.tensor_tensor(tick[:, 2 * k + 1:2 * k + 2], tick[:, 2 * TOPK + 1:2 * TOPK + 2], tick[:, 2 * TOPK + 2:2 * TOPK + 3], ALU.add)
                            nc.gpsimd.indirect_dma_start(
                                v_ring[:, k % DEEP, :], None, v_rows,
                                bass.IndirectOffsetOnAxis(idxv[:, e, k:k + 1], 0)).then_inc(v_in[k % DEEP], 16)

                nc.gpsimd.memset(tick[:, :], 0.0)
                pool.drain()
                step(0, 0, True, False)
                step(1, 1, True, True)
                with pool.Fori(2, G, 2) as g:
                    step(g, 0, True, True)
                    step(g + 1, 1, True, True)
                pool.dma_start(wple[:, :, :], w_ple[0].rearrange("(k p) n -> p k n", p=P)).then_inc(wple_in, 16)
                pool.dma_start(pin[:, :, :], p[0, 0].rearrange("(b q) n -> q b n", q=P)).then_inc(p_in, 16)
                step(G, 0, False, True)

            @block.scalar
            def _(act):
                def rms_square(src, junk, phase_no, b):
                    act.activation(junk, src, ACT.Square, accum_out=stat[:, 2 * phase_no + b:2 * phase_no + b + 1]).then_inc(ssq_ready, 1)

                def rms_sqrt(n, lo, hi):
                    act.wait_ge(var_ready, n)
                    act.activation(stat[:, 16 + lo:16 + hi], stat[:, 8 + lo:8 + hi], ACT.Sqrt).then_inc(sqrt_ready, 1)

                def t_hi_part(phase, items=range(4)):
                    no = PH_NO[phase]
                    for i in items:
                        b, kh = i // 2, i % 2
                        act.wait_ge(tf_ready, 4 * no + i + 1)
                        act.activation(t_hi[:, kh * 8:kh * 8 + 8, b * P:(b + 1) * P], tfp[:, i % 2, :, :],
                                       ACT.Copy).then_inc(thi_done, 1)

                def split_hi(s):
                    g, q = s // NQ, s % NQ
                    act.wait_ge(raw_in[q], 16 * (g + 1))
                    if s >= 2:
                        act.wait_ge(slice_used, s - 1)
                    act.activation(w_hi[:, s % 2, :, :], raw[:, q, :, :], ACT.Copy).then_inc(hi_done, 1)

                def copy_out(g, dst, func, scale=1.0):
                    act.wait_ge(slice_used, NQ * (g + 1))
                    act.activation(dst, acc_view(g), func, scale=scale).then_inc(acc_free[g % 2], 1)

                def acc_view(g):
                    if g < NA and g % 6 < 2 or gQ <= g < gG:
                        return acc[g % 2][:, :].rearrange("p (s t) -> p s t", t=S)
                    return acc[g % 2][:, :].rearrange("p (b n) -> p b n", n=CW)

                for b in range(NB):
                    act.wait_ge(x_in[b], 16)
                    rms_square(h[:, b, :], y[:, b, :], 0, b)
                rms_sqrt(1, 0, 2)
                t_hi_part("A")

                def softplus_piece(n, src, e, lnv):
                    act.wait_ge(abs_ready, n)
                    act.activation(e, src, ACT.Exp, scale=-1.0)
                    act.drain()
                    act.activation(lnv, e, ACT.Ln, bias=1.0).then_inc(softp, 1)

                dests = {0: (gq[:, :, :], ACT.Copy, KSC), 1: (gk[:, :, :], ACT.Copy, 1.0),
                         2: (gv[:, :, 0:CW], ACT.Copy, 1.0), 3: (gv[:, :, CW:2 * CW], ACT.Copy, 1.0),
                         4: (y[:, :, 0:CW], ACT.Silu, 1.0), 5: (y[:, :, CW:2 * CW], ACT.Silu, 1.0),
                         6: (cin[:, 0:H, CONV - 1:], ACT.Copy, 1.0), 7: (cin[:, H:2 * H, CONV - 1:], ACT.Copy, 1.0),
                         8: (mv[:, :, 0:CW], ACT.Copy, 1.0), 9: (mv[:, :, CW:2 * CW], ACT.Copy, 1.0),
                         10: (y[:, :, W2:W2 + CW], ACT.Sigmoid, 1.0), 11: (y[:, :, W2 + CW:2 * W2], ACT.Sigmoid, 1.0)}

                def put_out(g):
                    if g == 8:
                        act.wait_ge(sm_ready, 1)
                        act.wait_ge(mask_ready, 1)
                    dst, func, scale = dests[g]
                    copy_out(g, dst, func, scale)

                act.wait_ge(wsm_in, 32)
                act.activation(wsm_hi[:, :, :], wsm[:, :, :], ACT.Copy).then_inc(smw_hi, 1)
                step_of = {2 * n + 1: n for n in range(LEVELS + 1)}
                for g in range(NA):
                    for q in range(NQ):
                        s = g * NQ + q
                        split_hi(s)
                        if g == 3 and q == 0:
                            softplus_piece(1, tfp[:, 0, :, :], tfp[:, 0, :, :], tfp[:, 1, :, :])
                            softplus_piece(2, rowm[0:H, 2, :], rowm[0:H, 2, :], rowm[0:H, 3, :])
                        r = s - NQ * NA1
                        if r in step_of:
                            act.wait_ge(diff_ready, step_of[r] + 1)
                            e = tfp[:, step_of[r] % 2, :, :]
                            act.activation(e, e, ACT.Exp, scale=1.0 / TAU).then_inc(decay_ready, 1)
                        if q == 1 and g >= 1:
                            put_out(g - 1)
                put_out(NA - 1)

                def head_squares(name, src_scale, junk, col):
                    b = int(name[-1])
                    wait_mix(act, name)
                    for n in range(H):
                        kw = {} if src_scale is None else {"scale": src_scale(b, n)}
                        c = col + b * H + n
                        ins = act.activation(junk[:, 0:DV], mix_of(name)[:, n * DV:(n + 1) * DV], ACT.Square,
                                             accum_out=stat[:, c:c + 1], **kw)
                        if n < H - 1:
                            act.drain()
                    ins.then_inc(hsq_ready, 1)

                junk = cum[:, 0, :]
                head_squares("go0", None, junk, 24)
                act.drain()
                head_squares("go1", None, junk, 24)
                act.wait_ge(hvar_ready, 1)
                act.activation(stat[:, 24:32], stat[:, 24:32], ACT.Sqrt).then_inc(hsqrt_ready, 1)
                act.wait_ge(conv_ready, 1)
                act.activation(conv[:, :, :], conv[:, :, :], ACT.Silu).then_inc(silu_ready, 1)
                act.wait_ge(expo_ready, 1)
                for t, tile in enumerate((st[:, 0], st[:, 1], stx)):
                    for n in range(H):
                        kb = (0, 1, 0)[t]
                        e = tile[:, n, :]
                        ins = act.activation(e, e, ACT.Exp, scale=-1.0, bias=stat[:, 40 + kb * H + n:41 + kb * H + n])
                ins.then_inc(wexp_ready, 1)
                act.wait_ge(denr_ready, 1)
                act.activation(stat[:, 48:56], stat[:, 48:56], ACT.Exp).then_inc(wexp_ready, 1)
                act.wait_ge(denr_ready, 2)
                head_squares("mo0", lambda b, n: stat[:, 56 + b * H + n:57 + b * H + n], junk, 32)
                act.drain()
                head_squares("mo1", lambda b, n: stat[:, 56 + b * H + n:57 + b * H + n], junk, 32)
                act.wait_ge(hvar_ready, 2)
                act.activation(stat[:, 32:40], stat[:, 32:40], ACT.Sqrt).then_inc(hsqrt_ready, 1)
                t_hi_part("B")
                for s in range(NQ * gB, NQ * gQ):
                    split_hi(s)
                for b in range(NB):
                    act.wait_ge(h_ready, b + 1)
                    rms_square(h[:, b, :], xn2[:, b, :], 1, b)
                rms_sqrt(2, 2, 4)
                t_hi_part("Q")
                for g in range(gQ, gG):
                    for q in range(NQ):
                        split_hi(g * NQ + q)
                        if q == 1 and g > gQ:
                            if g > gQ + 1:
                                wait_mix(act, f"sc{g - gQ - 2}")
                            copy_out(g - 1, qt[:, :, :], ACT.Copy)
                wait_mix(act, f"sc{ND - 2}")
                copy_out(gG - 1, qt[:, :, :], ACT.Copy)

                def softmax_top(g):
                    act.wait_ge(top_ready, g + 1)
                    act.activation(ex[:, :], topc[:, :], ACT.Exp, bias=esm[:, 0:1], accum_out=esm[:, 1:2]).then_inc(exp_ready, 1)

                def gelu_of(g):
                    act.wait_ge(u_free, DEEP + TOPK * (g + 1))
                    act.activation(act_a[:, :], dots[:, :], ACT.Gelu_apprx_tanh).then_inc(gelu_ready, 1)

                def diags(g):
                    act.wait_ge(w_ready, g + 1)
                    for k in range(TOPK):
                        act.wait_ge(v_free, g * TOPK + k + 1)
                        act.activation(diag[:, k % DEEP, :], ident[:, :], ACT.Copy, scale=wgt[:, k:k + 1]).then_inc(diag_ready, 1)

                softmax_top(0)
                gelu_of(0)
                with act.Fori(1, G) as g:
                    softmax_top(g)
                    diags(g - 1)
                    gelu_of(g)
                diags(G - 1)
                for b in range(NB):
                    act.wait_ge(h_ready, NB + b + 1)
                    rms_square(h[:, b, :], xn2[:, b, :], 2, b)
                rms_sqrt(3, 4, 6)
                t_hi_part("G")
                for g in range(gG, gG + ND):
                    for q in range(NQ):
                        split_hi(g * NQ + q)
                    c = g - gG
                    if c >= 2:
                        act.wait_ge(h_ready, 2 * NB + c - 1)
                    copy_out(g, gt[:, c % 2, :, :], ACT.Sigmoid)
                    act.drain().then_inc(gate_ready, 1)
                for b in range(NB):
                    act.wait_ge(h_ready, 2 * NB + ND)
                    rms_square(h[:, b, :], xn2[:, b, :], 3, b)
                rms_sqrt(4, 6, 8)

            @block.vector
            def _(dve):
                V = nc.vector

                def rms_scale(n, ssq_count, lo, hi):
                    dve.wait_ge(ssq_ready, ssq_count)
                    v, r, t = stat[:, 8 + lo:8 + hi], stat[:, 16 + lo:16 + hi], nwt[:, 0:hi - lo]
                    V.tensor_scalar(v, stat[:, lo:hi], 1.0 / D, EPS, ALU.mult, ALU.add).then_inc(var_ready, 1)
                    dve.wait_ge(sqrt_ready, n)
                    newton(r, v, t)

                def newton(r, v, t):
                    V.reciprocal(r, r)
                    dve.drain()
                    V.tensor_tensor(t, r, r, ALU.mult)
                    dve.drain()
                    V.tensor_tensor(t, t, v, ALU.mult)
                    dve.drain()
                    V.tensor_scalar(t, t, -0.5, 1.5, ALU.mult, ALU.add)
                    dve.drain()
                    V.tensor_tensor(r, r, t, ALU.mult)
                    dve.drain()

                def t_parts(phase, gain):
                    no = PH_NO[phase]
                    if SLICES_BEFORE[phase]:
                        dve.wait_ge(slice_used, SLICES_BEFORE[phase])

                    def lo(i):
                        b, kh = i // 2, i % 2
                        dve.wait_ge(thi_done, 4 * no + i + 1)
                        hi_v = t_hi[:, kh * 8:kh * 8 + 8, b * P:(b + 1) * P]
                        V.tensor_tensor(t_lo[:, kh * 8:kh * 8 + 8, b * P:(b + 1) * P], tfp[:, i % 2, :, :],
                                        hi_v.bitcast(F32), ALU.subtract).then_inc(tlo_done, 1)

                    for i in range(4):
                        name = f"t{phase}{i}"
                        kh = i % 2
                        if i >= 2:
                            lo(i - 2)
                            dve.drain()
                        wait_mix(dve, name)
                        src = mix_of(name)[:, :].rearrange("p (k t) -> p k t", t=P)
                        if gain is None:
                            V.tensor_copy(tfp[:, i % 2, :, :], src).then_inc(free_sem(name), 1)
                        else:
                            g_ap = par[:, gain + kh * 8:gain + kh * 8 + 8].unsqueeze(2).to_broadcast([P, 8, P])
                            V.tensor_tensor(tfp[:, i % 2, :, :], src, g_ap, ALU.mult).then_inc(free_sem(name), 1)
                        dve.drain().then_inc(tf_ready, 1)
                    lo(2)
                    lo(3)

                def split_lo(s):
                    q = s % NQ
                    dve.wait_ge(hi_done, s + 1)
                    if s >= 2:
                        dve.wait_ge(slice_used, s - 1)
                    V.tensor_tensor(w_lo[:, s % 2, :, :], raw[:, q, :, :], w_hi[:, s % 2, :, :].bitcast(F32),
                                    ALU.subtract).then_inc(lo_done, 1)

                dve.wait_ge(const_ready, 1)
                dve.drain().then_inc(u_free, DEEP)
                dve.drain().then_inc(v_free, DEEP)

                V.tensor_tensor(it_x[:, :], it_i[:, :], it_p[:, :], ALU.bitwise_xor)
                dve.drain()
                V.tensor_tensor(it_u[:, :], it_i[:, :], it_p[:, :], ALU.is_gt)
                V.tensor_scalar(mask[:, LEVELS, :], it_x[:, :], 0.0, None, ALU.is_equal)
                for lv in range(LEVELS):
                    V.tensor_scalar(it_s[:, :], it_x[:, :], lv, None, ALU.logical_shift_right)
                    dve.drain()
                    V.scalar_tensor_tensor(mask[:, lv, :], it_s[:, :], 1.0, it_u[:, :], ALU.is_equal, ALU.mult)
                    dve.drain().then_inc(mask_ready, 1)

                wait_mix(dve, "par")
                V.tensor_copy(par[:, :], mix_of("par")[:, 0:NPAR]).then_inc(free_sem("par"), 1)
                dve.drain()
                rms_scale(1, 2, 0, 2)
                for b in range(NB):
                    V.tensor_scalar(y[:, b, :], h[:, b, :], stat[:, 16 + b:17 + b], None, ALU.mult).then_inc(src_ready, 1)
                t_parts("A", pM)
                dve.wait_ge(smw_hi, 1)
                V.tensor_tensor(wsm_lo[:, :, :], wsm[:, :, :], wsm_hi[:, :, :].bitcast(F32), ALU.subtract).then_inc(smw_lo, 1)

                def small_columns():
                    wait_mix(dve, "sm")
                    V.tensor_copy(sm[:, :, :], mix_of("sm")[:, 0:NB * NSM].rearrange("p (b n) -> p b n", n=NSM)).then_inc(free_sem("sm"), 1)
                    dve.drain().then_inc(sm_ready, 1)
                    wait_mix(dve, "smt")
                    m = mix_of("smt")
                    V.tensor_copy(glr[:, :], m[0:RANK, 0:S])
                    dve.wait_ge(gb_in, 32)
                    V.tensor_scalar(rowm[0:H, 0, :], m[0:H, S:2 * S], gbias[:, 0:1], None, ALU.add)
                    V.tensor_scalar(rowm[0:H, 1, :], m[0:H, 2 * S:3 * S], gbias[:, 1:2], None, ALU.add).then_inc(free_sem("smt"), 1)
                    dve.drain().then_inc(smt_ready, 1)
                    wait_mix(dve, "z")
                    V.tensor_tensor(cum[:, :, :], mix_of("z")[:, :].rearrange("p (h t) -> p h t", t=S),
                                    par[:, pB:pB + H].unsqueeze(2).to_broadcast([P, H, S]), ALU.add).then_inc(free_sem("z"), 1)
                    dve.drain()
                    tf0 = tfp[:, 0, :, :].rearrange("p k t -> p (k t)")
                    zf = cum[:, :, :].rearrange("p h t -> p (h t)")
                    V.scalar_tensor_tensor(tf0, zf, -1.0, zf, ALU.mult, ALU.max).then_inc(abs_ready, 1)
                    V.scalar_tensor_tensor(rowm[0:H, 2, :], rowm[0:H, 1, :], -1.0, rowm[0:H, 1, :], ALU.mult, ALU.max).then_inc(abs_ready, 1)

                def log_decays():
                    dve.wait_ge(softp, 2)
                    cf = cum[:, :, :].rearrange("p h t -> p (h t)")
                    ln = tfp[:, 1, :, :].rearrange("p k t -> p (k t)")
                    e0 = tfp[:, 0, :, :].rearrange("p k t -> p (k t)")
                    V.scalar_tensor_tensor(cf, cf, 0.0, ln, ALU.min, ALU.subtract)
                    V.memset(e0, 1.0)
                    V.scalar_tensor_tensor(rowm[0:H, 1, :], rowm[0:H, 1, :], 0.0, rowm[0:H, 3, :], ALU.min, ALU.subtract)
                    V.memset(rowm[0:H, 2, :], 1.0)
                    dve.drain()
                    for n in range(H):
                        V.tensor_tensor_scan(cum[:, n, :], e0[:, 0:S], cum[:, n, :], 0.0, ALU.mult, ALU.add)
                    V.tensor_tensor_scan(rowm[0:H, 1, :], rowm[0:H, 2, :], rowm[0:H, 1, :], 0.0, ALU.mult, ALU.add)
                    dve.drain()
                    V.tensor_tensor(rowm[0:H, 0, :], rowm[0:H, 0, :], rowm[0:H, 1, :], ALU.subtract)
                    dve.drain()
                    V.tensor_tensor_scan(rowm[0:H, 3, :], rowm[0:H, 0, :], rowm[0:H, 0, :], 0.0, ALU.max, ALU.max)
                    dve.drain()
                    V.scalar_tensor_tensor(rowm[0:H, 4, :], rowm[0:H, 1, :], -1.0, rowm[0:H, 3, :], ALU.mult, ALU.subtract).then_inc(rows_ready, 1)

                def level_view(t, lv):
                    half = 1 << lv
                    f = t.rearrange("p h t -> p (h t)") if len(t.shape) == 3 else t
                    return f.rearrange("p (n two s) -> p n two s", two=2, s=half)

                def e_tile(lv):
                    return tfp[:, lv % 2, :, :].rearrange("p k t -> p (k t)")

                def differences(lv):
                    half = 1 << lv
                    c, e = level_view(cum[:, :, :], lv), level_view(e_tile(lv), lv)
                    n = H * S // (2 * half)
                    anchor = c[:, :, 0, half - 1:half].to_broadcast([P, n, half])
                    V.tensor_tensor(e[:, :, 1, :], c[:, :, 1, :], anchor, ALU.subtract)
                    V.tensor_tensor(e[:, :, 0, :], anchor, c[:, :, 0, :], ALU.subtract).then_inc(diff_ready, 1)

                def decayed(lv):
                    dve.wait_ge(decay_ready, lv + 1)
                    e = level_view(e_tile(lv), lv)
                    V.tensor_tensor(e[:, :, 1, :], e[:, :, 1, :], level_view(gq[:, :, :], lv)[:, :, 1, :], ALU.mult)
                    V.tensor_tensor(e[:, :, 0, :], e[:, :, 0, :], level_view(gk[:, :, :], lv)[:, :, 0, :], ALU.mult)
                    dve.drain().then_inc(qk_ready, 1)

                def take_level(name, lv):
                    wait_mix(dve, name)
                    if name == f"lv{LEVELS}":
                        V.tensor_copy(stx[:, :, :], mix_of(name)[:, 0:H * P].rearrange("p (h t) -> p h t", t=P)).then_inc(free_sem(name), 1)
                        return
                    V.copy_predicated(st[:, :, :, :].rearrange("p b h t -> p (b h) t"),
                                      mask[:, lv, :].unsqueeze(1).to_broadcast([P, NB * H, P]),
                                      mix_of(name)[:, :].rearrange("p (n t) -> p n t", t=P)).then_inc(free_sem(name), 1)
                    dve.drain()

                V.memset(st[:, :, :, :], 0.0)
                for g in range(NA):
                    for q in range(NQ):
                        s = g * NQ + q
                        split_lo(s)
                        if g == 2 and q == 0:
                            small_columns()
                        if g == 4 and q == 0:
                            log_decays()
                            dve.drain()
                        r = s - NQ * NA1
                        if r == 0:
                            take_level("lvd", LEVELS)
                        if r > 0 and r % 2 == 1:
                            n = r // 2
                            if 2 <= n <= LEVELS + 2:
                                take_level(f"lv{n - 2}", n - 2)
                            if n <= LEVELS:
                                differences(n)
                            if 1 <= n <= LEVELS + 1:
                                decayed(n - 1)
                dve.drain().then_inc(st_ready, 1)

                def head_norm(no, col, count_sq):
                    dve.wait_ge(hsq_ready, count_sq)
                    v = esm2[:, 0:8]
                    V.tensor_scalar(v, stat[:, col:col + 8], 1.0 / DV, EPS, ALU.mult, ALU.add)
                    dve.drain()
                    V.tensor_copy(stat[:, col:col + 8], v).then_inc(hvar_ready, 1)
                    dve.wait_ge(hsqrt_ready, no)
                    newton(stat[:, col:col + 8], v, esm2[:, 8:16])

                esm2 = sm[:, 0, 0:16]
                dve.wait_ge(mix_ready, M[f"lv{LEVELS}"] + 1)
                for t in range(CONV):
                    for c in range(2 * H):
                        w_ap = par[:, pC + t * 8 + c:pC + t * 8 + c + 1]
                        src = cin[:, c, t:t + S]
                        if t == 0:
                            ins = V.tensor_scalar(conv[:, c, :], src, w_ap, par[:, pCB + c:pCB + c + 1], ALU.mult, ALU.add)
                        else:
                            ins = V.scalar_tensor_tensor(conv[:, c, :], src, w_ap, conv[:, c, :], ALU.mult, ALU.add)
                    if t < CONV - 1:
                        dve.drain()
                dve.drain().then_inc(conv_ready, 1)
                head_norm(1, 24, 2)
                for b in range(NB):
                    name = f"go{b}"
                    for n in range(H):
                        yv = y[:, b, n * DV:(n + 1) * DV]
                        ins = V.scalar_tensor_tensor(yv, mix_of(name)[:, n * DV:(n + 1) * DV],
                                                     stat[:, 24 + b * H + n:25 + b * H + n], yv, ALU.mult, ALU.mult)
                    ins.then_inc(free_sem(name), 1)
                wait_mix(dve, "cols")
                V.tensor_copy(stat[:, 40:56], mix_of("cols")[:, 0:16]).then_inc(free_sem("cols"), 1)
                wait_mix(dve, "mbc")
                mb = mix_of("mbc")[:, :].rearrange("p (h b t) -> p h b t", h=H, b=NB)
                for b in range(NB):
                    V.tensor_tensor(st[:, b, :, :], mb[:, :, b, :], cbias[:, :].unsqueeze(1).to_broadcast([P, H, P]), ALU.add)
                V.tensor_copy(stx[:, :, :], mb[:, :, 1, :]).then_inc(free_sem("mbc"), 1)
                dve.drain().then_inc(expo_ready, 1)
                dve.drain().then_inc(denr_ready, 1)
                dve.wait_ge(wexp_ready, 1)
                wait_mix(dve, "ps")
                sv = st[:, :, :, :].rearrange("p b h t -> p (b h t)")
                V.scalar_tensor_tensor(sv, mix_of("ps")[:, :], KSC, sv, ALU.mult, ALU.mult).then_inc(free_sem("ps"), 1)
                wait_mix(dve, "psx")
                sv = stx[:, :, :].rearrange("p h t -> p (h t)")
                V.scalar_tensor_tensor(sv, mix_of("psx")[:, 0:H * P], KSC, sv, ALU.mult, ALU.mult).then_inc(free_sem("psx"), 1)
                dve.drain().then_inc(st_ready, 1)
                wait_mix(dve, "den")
                V.tensor_copy(esm2[:, 0:8], mix_of("den")[:, 0:8]).then_inc(free_sem("den"), 1)
                dve.drain()
                V.scalar_tensor_tensor(stat[:, 56:64], esm2[:, 0:8], -1.0, esm2[:, 0:8], ALU.mult, ALU.max)
                dve.drain()
                dve.wait_ge(wexp_ready, 2)
                V.tensor_tensor(stat[:, 56:64], stat[:, 56:64], stat[:, 48:56], ALU.max)
                dve.drain()
                V.reciprocal(stat[:, 56:64], stat[:, 56:64])
                dve.drain().then_inc(denr_ready, 1)
                head_norm(2, 32, 4)
                V.tensor_tensor(stat[:, 32:40], stat[:, 32:40], stat[:, 56:64], ALU.mult)
                dve.drain()
                for b in range(NB):
                    name = f"mo{b}"
                    for n in range(H):
                        yv = y[:, b, W2 + n * DV:W2 + (n + 1) * DV]
                        ins = V.scalar_tensor_tensor(yv, mix_of(name)[:, n * DV:(n + 1) * DV],
                                                     stat[:, 32 + b * H + n:33 + b * H + n], yv, ALU.mult, ALU.mult)
                    ins.then_inc(free_sem(name), 1)
                dve.drain().then_inc(src_ready, NB)
                t_parts("B", pG)
                for g in range(gB, gQ):
                    for q in range(NQ):
                        split_lo(g * NQ + q)
                        if q == 1 and g > gB:
                            add_chunk(dve, V, g - 1, h, acc, slice_used, acc_free, NQ, CW, gB)
                add_chunk(dve, V, gQ - 1, h, acc, slice_used, acc_free, NQ, CW, gB)
                dve.drain().then_inc(h_ready, NB)
                rms_scale(2, 4, 2, 4)
                for b in range(NB):
                    V.tensor_scalar(xn2[:, b, :], h[:, b, :], stat[:, 18 + b:19 + b], None, ALU.mult).then_inc(src_ready, 1)
                for i in range(2):
                    wait_mix(dve, f"key{i}")
                    V.tensor_copy(keyst[:, i * 8:i * 8 + 8, :], mix_of(f"key{i}")[:, :].rearrange("p (k t) -> p k t", t=P)).then_inc(free_sem(f"key{i}"), 1)
                dve.wait_ge(nffn_in, 16)
                dve.drain()
                for b in range(NB):
                    V.tensor_tensor(xn2[:, b, :], xn2[:, b, :], nrow[:, :], ALU.mult).then_inc(xn2_ready, 1)
                t_parts("Q", None)
                dve.drain().then_inc(keyst_ready, 1)

                def take_scores(c):
                    wait_mix(dve, f"sc{c}")
                    m = mix_of(f"sc{c}")[:, :].rearrange("p (b n) -> p b n", b=NB)
                    dst = sc[:, :, :].rearrange("p (b h) n -> p b (h n)", b=NB)[:, :, c * CW:(c + 1) * CW]
                    V.tensor_copy(dst, m).then_inc(free_sem(f"sc{c}"), 1)

                for g in range(gQ, gG):
                    for q in range(NQ):
                        split_lo(g * NQ + q)
                        if q == 3 and g > gQ:
                            take_scores(g - gQ - 1)
                take_scores(ND - 1)
                dve.drain()

                dve.wait_ge(const_ready, 2)

                def top_k(g):
                    V.tensor_copy(s2[:, :, :].rearrange("p a n -> p (a n)").unsqueeze(1), sc[:, bass.ds(g, 1), :])
                    dve.drain()
                    for a in range(2):
                        V.max(tv[:, a, 0:8], s2[:, a, :])
                    dve.drain()
                    for a in range(2):
                        V.max_index(ti[:, a, 0:8], tv[:, a, 0:8], s2[:, a, :])
                        V.match_replace(wk[:, a, :], tv[:, a, 0:8], s2[:, a, :], NEG)
                    dve.drain()
                    for a in range(2):
                        V.max(tv[:, a, 8:16], wk[:, a, :])
                    dve.drain()
                    for a in range(2):
                        V.max_index(ti[:, a, 8:16], tv[:, a, 8:16], wk[:, a, :])
                    V.tensor_tensor(cand[:, :, :], tv[:, 0, :].unsqueeze(2).to_broadcast([P, TOPK, TOPK]),
                                    tv[:, 1, :].unsqueeze(1).to_broadcast([P, TOPK, TOPK]), ALU.add)
                    dve.drain()
                    V.tensor_copy(tif[:, :, :], ti[:, :, :])
                    cf, wf = cand[:, :, :].rearrange("p a n -> p (a n)"), wk[:, :, :].rearrange("p a n -> p (a n)")
                    V.max(cv[:, 0:8], cf)
                    dve.drain()
                    V.max_index(ci[:, 0:8], cv[:, 0:8], cf)
                    V.match_replace(wf, cv[:, 0:8], cf, NEG)
                    dve.drain()
                    V.max(cv[:, 8:16], wf)
                    dve.drain()
                    V.max_index(ci[:, 8:16], cv[:, 8:16], wf)
                    dve.drain()
                    V.tensor_scalar(cij[:, 0, :], ci[:, :], 4, None, ALU.logical_shift_right)
                    V.tensor_scalar(cij[:, 1, :], ci[:, :], TOPK - 1, None, ALU.bitwise_and)
                    dve.drain()
                    V.tensor_copy(cijf[:, :, :], cij[:, :, :])
                    dve.drain()
                    for a in range(2):
                        V.tensor_tensor(oh[:, :, :], cijf[:, a, :].unsqueeze(2).to_broadcast([P, TOPK, TOPK]),
                                        i16[:, :].unsqueeze(1).to_broadcast([P, TOPK, TOPK]), ALU.is_equal)
                        dve.drain()
                        V.tensor_tensor(oh[:, :, :], oh[:, :, :], tif[:, a, :].unsqueeze(1).to_broadcast([P, TOPK, TOPK]), ALU.mult)
                        dve.drain()
                        V.tensor_reduce(pick[:, a, :], oh[:, :, :], AXX, ALU.add)
                        dve.drain()
                    V.scalar_tensor_tensor(pick[:, 0, :], pick[:, 0, :], float(NK), pick[:, 1, :], ALU.mult, ALU.add)
                    dve.drain()
                    if not (isinstance(g, int) and g == 0):
                        dve.wait_ge(idx_taken, g)
                    V.tensor_copy(idxn[:, :], pick[:, 0, :]).then_inc(idx_ready, 1)

                def current_top(g):
                    V.tensor_copy(topc[:, :], cv[:, :])
                    V.tensor_scalar(esm[:, 0:1], cv[:, 0:1], -1.0, None, ALU.mult)
                    dve.drain().then_inc(top_ready, 1)

                def products(g, b):
                    for k in range(TOPK):
                        dve.wait_ge(u_in[k % DEEP], 16 * (TOPK // DEEP) * g + 16 * (k // DEEP + 1))
                        V.tensor_tensor_reduce(out=u_ring[:, k % DEEP, :], in0=u_ring[:, k % DEEP, :], in1=xn2[:, b, :],
                                               scale=1.0, scalar=0.0, op0=ALU.mult, op1=ALU.add,
                                               accum_out=dots[:, k:k + 1]).then_inc(u_free, 1)
                    dve.wait_ge(exp_ready, g + 1)
                    V.reciprocal(esm[:, 2:3], esm[:, 1:2])
                    dve.drain()
                    dve.wait_ge(gelu_ready, g + 1)
                    V.scalar_tensor_tensor(wgt[:, :], ex[:, :], esm[:, 2:3], act_a[:, :], ALU.mult, ALU.mult).then_inc(w_ready, 1)

                top_k(0)
                for b in range(NB):
                    with dve.Fori(b * PH, (b + 1) * PH - (b == NB - 1)) as g:
                        dve.drain()
                        current_top(g)
                        top_k(g + 1)
                        products(g, b)
                dve.drain()
                current_top(G - 1)
                products(G - 1, NB - 1)
                for b, pairs in enumerate((mix, acc)):
                    dve.wait_ge(peer_ready, b + 1)
                    for i in range(2):
                        hv = h[:, b, i * 2 * CW:(i + 1) * 2 * CW]
                        V.tensor_tensor(hv, hv, pairs[i][:, :], ALU.add)
                    dve.drain().then_inc(h_ready, 1)
                    dve.drain().then_inc(peer_taken, 1)
                dve.drain()
                rms_scale(3, 6, 4, 6)
                for b in range(NB):
                    V.tensor_scalar(xn2[:, b, :], h[:, b, :], stat[:, 20 + b:21 + b], None, ALU.mult).then_inc(src_ready, 1)
                wait_mix(dve, "pt")
                V.tensor_copy(pt[:, :, :], mix_of("pt")[:, 0:2 * S].rearrange("p (k t) -> p k t", t=S)).then_inc(free_sem("pt"), 1)
                dve.drain().then_inc(pt_ready, 1)
                t_parts("G", pP)
                for g in range(gG, gG + ND):
                    c = g - gG
                    for q in range(NQ):
                        split_lo(g * NQ + q)
                    dve.wait_ge(gate_ready, c + 1)
                    wait_mix(dve, f"pl{c}")
                    gv_ = gt[:, c % 2, :, :]
                    V.tensor_tensor(gv_, gv_, mix_of(f"pl{c}")[:, :].rearrange("p (b n) -> p b n", b=NB), ALU.mult).then_inc(free_sem(f"pl{c}"), 1)
                    dve.drain()
                    hv = h[:, :, c * CW:(c + 1) * CW]
                    V.tensor_tensor(hv, hv, gv_, ALU.add).then_inc(h_ready, 1)
                dve.drain()
                rms_scale(4, 8, 6, 8)
                dve.wait_ge(nfin_in, 16)
                for b in range(NB):
                    V.scalar_tensor_tensor(h[:, b, :], h[:, b, :], stat[:, 22 + b:23 + b], nrow[:, :], ALU.mult, ALU.mult).then_inc(out_ready, 1)

            @block.tensor
            def _(pe):
                T = nc.tensor

                def transposes(phase):
                    src = src_blocks(phase)
                    no = PH_NO[phase]
                    for i in range(4):
                        name = f"t{phase}{i}"
                        b, kh = i // 2, i % 2
                        pe.wait_ge(src_ready, NB * no + (b + 1 if phase in "AG" else NB))
                        if phase == "Q":
                            pe.wait_ge(xn2_ready, b + 1)
                        take_mix(pe, name)
                        for k in range(8):
                            kt = kh * 8 + k
                            ins = T.transpose(mix_of(name)[:, k * P:(k + 1) * P], src[:, b, kt * P:(kt + 1) * P], ident[:, :])
                        ins.then_inc(mix_ready, 1)

                def begin_chunk(set_no, uses):
                    if uses is not None:
                        pe.wait_ge(acc_free[set_no], uses)

                def token_slice(set_no, s_slot, q, lo_count):
                    pe.wait_ge(lo_done, lo_count)
                    for k in range(KQ):
                        kt = q * KQ + k
                        for b in range(NB):
                            tok = slice(b * P, (b + 1) * P)
                            for n, (a, w) in enumerate(((t_hi, w_hi), (t_hi, w_lo), (t_lo, w_hi))):
                                ins = T.matmul(acc[set_no][:, b * CW:(b + 1) * CW], a[:, kt, tok], w[:, s_slot, k, :],
                                               start=(kt == 0 and n == 0), stop=(kt == KT - 1 and n == 2))
                    ins.then_inc(slice_used, 1)

                def column_slice(set_no, s_slot, q, lo_count):
                    pe.wait_ge(lo_done, lo_count)
                    for k in range(KQ):
                        kt = q * KQ + k
                        for c in range(CW // P):
                            for n, (w, a) in enumerate(((w_hi, t_hi), (w_hi, t_lo), (w_lo, t_hi))):
                                ins = T.matmul(acc[set_no][:, c * S:(c + 1) * S], w[:, s_slot, k, c * P:(c + 1) * P], a[:, kt, :],
                                               start=(kt == 0 and n == 0 and c % 2 == 0), stop=(kt == KT - 1 and n == 2),
                                               skip_group_check=True)
                    ins.then_inc(slice_used, 1)

                def chunk(g, kind, after=None):
                    begin_chunk(g % 2, g // 2 if g >= 2 else None)
                    for q in range(NQ):
                        kind(g % 2, (g * NQ + q) % 2, q, g * NQ + q + 1)
                        if after is not None:
                            after(g * NQ + q)

                pe.wait_ge(const_ready, 1)
                pe.wait_ge(par_in, 16 * 7)
                T.transpose(mix_of("par")[:, 0:NPAR], stack[:, :], ident[0:NPAR, 0:NPAR]).then_inc(mix_ready, 1)
                transposes("A")
                pe.wait_ge(tlo_done, 4)
                for g in (0, 1):
                    chunk(g, column_slice)
                take_mix(pe, "sm")
                pe.wait_ge(smw_lo, 1)
                for kt in range(KT):
                    for b in range(NB):
                        tok = slice(b * P, (b + 1) * P)
                        for n, (a, w) in enumerate(((t_hi, wsm_hi), (t_hi, wsm_lo), (t_lo, wsm_hi))):
                            ins = T.matmul(mix_of("sm")[:, b * NSM:(b + 1) * NSM], a[:, kt, tok], w[:, kt, :],
                                           start=(kt == 0 and n == 0 and b == 0), stop=(kt == KT - 1 and n == 2),
                                           skip_group_check=True)
                ins.then_inc(mix_ready, 1)
                take_mix(pe, "smt")
                pe.wait_ge(sm_ready, 1)
                for b in range(NB):
                    m = mix_of("smt")
                    T.transpose(m[0:RANK, b * P:(b + 1) * P], sm[:, b, 0:RANK], ident[:, :])
                    T.transpose(m[0:H, S + b * P:S + (b + 1) * P], sm[:, b, RANK:RANK + H], ident[:, :])
                    ins = T.transpose(m[0:H, 2 * S + b * P:2 * S + (b + 1) * P], sm[:, b, RANK + H:NSM], ident[:, :])
                ins.then_inc(mix_ready, 1)
                take_mix(pe, "z")
                pe.wait_ge(smt_ready, 1)
                pe.wait_ge(gup_in, 16)
                for n in range(H):
                    ins = T.matmul(mix_of("z")[:, n * S:(n + 1) * S], gup[:, n * DK:(n + 1) * DK], glr[:, :], start=True, stop=True)
                ins.then_inc(mix_ready, 1)

                with pe.Fori(0, (NA1 - 2) // 2) as t:
                    for e in range(2):
                        begin_chunk(e, t + 1)
                        for q in range(NQ):
                            token_slice(e, q % 2, q, t * 2 * NQ + (2 + e) * NQ + q + 1)

                def level_item(name, lv):
                    take_mix(pe, name)
                    m = mix_of(name)
                    if name == "lvd":
                        pe.wait_ge(acc_free[1], 1)
                        kk, qq = gk[:, :, :], gq[:, :, :]
                    else:
                        pe.wait_ge(qk_ready, lv + 1)
                        kk = qq = tfp[:, lv % 2, :, :].rearrange("p k t -> p (k t)").rearrange("p (h t) -> p h t", t=S)
                    if lv == LEVELS and name != "lvd":
                        for n in range(H):
                            ins = T.matmul(m[:, n * P:(n + 1) * P], kk[:, n, 0:P], qq[:, n, P:2 * P], start=True, stop=True)
                    else:
                        for b in range(NB):
                            for n in range(H):
                                ins = T.matmul(m[:, (b * H + n) * P:(b * H + n + 1) * P], kk[:, n, b * P:(b + 1) * P],
                                               qq[:, n, b * P:(b + 1) * P], start=True, stop=True)
                    ins.then_inc(mix_ready, 1)

                def between(s):
                    r = s - NQ * NA1
                    if r >= 4 and r % 2 == 0 and (r - 4) // 2 <= LEVELS:
                        lv = (r - 4) // 2
                        level_item(f"lv{lv}", lv)

                level_item("lvd", LEVELS)
                for g in range(NA1, NA):
                    chunk(g, column_slice if g < NA1 + 2 else token_slice, between)

                def attend(prefix, values, ready, with_den):
                    pe.wait_ge(st_ready, ready)
                    if with_den:
                        take_mix(pe, "den")
                        for b in range(NB):
                            for n in range(H):
                                o = mix_of("den")[:, b * H + n:b * H + n + 1]
                                ins = T.matmul(o, st[:, b, n, :], ones[:, :], start=True, stop=(b == 0))
                                if b == 1:
                                    ins = T.matmul(o, stx[:, n, :], ones[:, :], start=False, stop=True)
                        ins.then_inc(mix_ready, 1)
                    for b in range(NB):
                        name = f"{prefix}{b}"
                        take_mix(pe, name)
                        for n in range(H):
                            o = mix_of(name)[:, n * DV:(n + 1) * DV]
                            ins = T.matmul(o, st[:, b, n, :], values[:, b, n * DV:(n + 1) * DV], start=True, stop=(b == 0))
                            if b == 1:
                                ins = T.matmul(o, stx[:, n, :], values[:, 0, n * DV:(n + 1) * DV], start=False, stop=True)
                        ins.then_inc(mix_ready, 1)

                pe.wait_ge(acc_free[1], 2)
                attend("go", gv, 1, False)
                take_mix(pe, "cols")
                pe.wait_ge(rows_ready, 1)
                for i, row in enumerate((0, 4)):
                    for b in range(NB):
                        c = i * 8 + b * H
                        ins = T.transpose(mix_of("cols")[:, c:c + H], rowm[0:H, row, b * P:(b + 1) * P], ident[0:H, 0:H])
                ins.then_inc(mix_ready, 1)
                take_mix(pe, "mbc")
                for n in range(H):
                    ins = T.matmul(mix_of("mbc")[:, n * S:(n + 1) * S], sel[:, n, :], rowm[0:H, 3, :], start=True, stop=True)
                ins.then_inc(mix_ready, 1)
                take_mix(pe, "ps")
                pe.wait_ge(silu_ready, 1)
                for b in range(NB):
                    for n in range(H):
                        ins = T.matmul(mix_of("ps")[:, (b * H + n) * P:(b * H + n + 1) * P], conv[:, H + n, b * P:(b + 1) * P],
                                       conv[:, n, b * P:(b + 1) * P], start=True, stop=True)
                ins.then_inc(mix_ready, 1)
                take_mix(pe, "psx")
                for n in range(H):
                    ins = T.matmul(mix_of("psx")[:, n * P:(n + 1) * P], conv[:, H + n, 0:P], conv[:, n, P:2 * P], start=True, stop=True)
                ins.then_inc(mix_ready, 1)
                pe.wait_ge(acc_free[1], 5)
                attend("mo", mv, 2, True)
                transposes("B")
                pe.wait_ge(tlo_done, 8)
                with pe.Fori(0, ND // 2) as t:
                    for e in range(2):
                        begin_chunk(e, t + gB // 2)
                        for q in range(NQ):
                            token_slice(e, q % 2, q, t * 2 * NQ + (gB + e) * NQ + q + 1)
                for i in range(2):
                    take_mix(pe, f"key{i}")
                    pe.wait_ge(keys_in, 16)
                    for k in range(8):
                        ins = T.transpose(mix_of(f"key{i}")[:, k * P:(k + 1) * P], keys[:, i * 8 + k, :], ident[:, :])
                    ins.then_inc(mix_ready, 1)
                transposes("Q")
                pe.wait_ge(tlo_done, 12)
                pe.wait_ge(keyst_ready, 1)

                def scores(c):
                    name = f"sc{c}"
                    g = gQ + c
                    take_mix(pe, name)
                    pe.wait_ge(acc_free[g % 2], g // 2 + 1)
                    for b in range(NB):
                        for a in range(4):
                            ins = T.matmul(mix_of(name)[:, (b * 4 + a) * P:(b * 4 + a + 1) * P], qt[:, a, b * P:(b + 1) * P],
                                           keyst[:, c * 4 + a, :], start=True, stop=True)
                    ins.then_inc(mix_ready, 1)

                for c in range(ND):
                    g = gQ + c
                    begin_chunk(g % 2, g // 2)
                    for q in range(NQ):
                        column_slice(g % 2, q % 2, q, g * NQ + q + 1)
                        if q == 2 and c >= 1:
                            scores(c - 1)
                scores(ND - 1)

                for b, pairs in enumerate((mix, acc)):
                    if b == 0:
                        for i in range(2):
                            last = max(m for m in range(n_before_peer) if m % 2 == i)
                            pe.wait_ge(mix_free[i], last // 2 + 1)
                    for i in range(2):
                        for j in range(2):
                            T.matmul(pairs[i][:, j * CW:(j + 1) * CW], zero16[:, 0:P], zero16[:, :], start=True, stop=False, skip_group_check=True)
                    with pe.Fori(b * PH, (b + 1) * PH) as g:
                        for k in range(TOPK):
                            pe.wait_ge(diag_ready, g * TOPK + k + 1)
                            pe.wait_ge(v_in[k % DEEP], 16 * (TOPK // DEEP) * g + 16 * (k // DEEP + 1))
                            for j in range(4):
                                ins = T.matmul(pairs[j // 2][:, (j % 2) * CW:(j % 2 + 1) * CW], diag[:, k % DEEP, :],
                                               v_ring[:, k % DEEP, j * CW:(j + 1) * CW], start=False, stop=False, skip_group_check=True)
                            ins.then_inc(v_free, 1)
                    for i in range(2):
                        for j in range(2):
                            ins = T.matmul(pairs[i][:, j * CW:(j + 1) * CW], zero16[:, 0:P], zero16[:, :], start=False, stop=True, skip_group_check=True)
                    ins.then_inc(peer_ready, 1)

                take_mix(pe, "pt")
                pe.wait_ge(p_in, 16)
                for b in range(NB):
                    for k in range(PLE // P):
                        ins = T.transpose(mix_of("pt")[:, k * S + b * P:k * S + (b + 1) * P], pin[:, b, k * P:(k + 1) * P], ident[:, :])
                ins.then_inc(mix_ready, 1)
                transposes("G")
                pe.wait_ge(tlo_done, 16)
                pe.wait_ge(pt_ready, 1)
                pe.wait_ge(wple_in, 16)
                pe.wait_ge(peer_taken, 2)
                for c in range(ND):
                    g = gG + c
                    if c >= 2:
                        begin_chunk(g % 2, g // 2)
                    for q in range(NQ):
                        token_slice(g % 2, q % 2, q, g * NQ + q + 1)
                    name = f"pl{c}"
                    take_mix(pe, name)
                    for b in range(NB):
                        for k in range(PLE // P):
                            ins = T.matmul(mix_of(name)[:, b * CW:(b + 1) * CW], pt[:, k, b * P:(b + 1) * P], wple[:, k, c * CW:(c + 1) * CW],
                                           start=(k == 0), stop=(k == PLE // P - 1))
                    ins.then_inc(mix_ready, 1)


def add_chunk(dve, V, g, h, acc, slice_used, acc_free, NQ, CW, gB):
    dve.wait_ge(slice_used, NQ * (g + 1))
    c = g - gB
    hv = h[:, :, c * CW:(c + 1) * CW]
    V.tensor_tensor(hv, hv, acc[g % 2][:, :].rearrange("p (b n) -> p b n", n=CW), ALU.add).then_inc(acc_free[g % 2], 1)


_INS = ['x', 'p', 'norm_mix', 'w_in', 'gla_gate_up', 'gla_gate_bias', 'gla_norm', 'mlstm_conv_w', 'mlstm_conv_b',
        'mlstm_igate_bias', 'mlstm_fgate_bias', 'mlstm_norm', 'w_out', 'norm_ffn', 'peer_query', 'peer_sub_keys',
        'peer_u', 'peer_v', 'norm_ple', 'w_ple', 'w_ple_gate', 'norm_final']


def kernel(**inputs):
    import numpy as _np
    import concourse.bacc as _bacc
    from concourse import mybir as _mybir
    from concourse.bass_utils import run_bass_kernel_spmd as _run

    nc = _bacc.Bacc("TRN2", target_bir_lowering=False, num_devices=1)
    arrays, args = {}, []
    for name in _INS:
        a = _np.ascontiguousarray(inputs[name])
        arrays[f"in_{name}_dram"] = a
        args.append(nc.dram_tensor(f"in_{name}_dram", a.shape, _mybir.dt.from_np(a.dtype), kind="ExternalInput").ap())
    shape = tuple(inputs['x'].shape)
    args.append(nc.dram_tensor("out_0_dram", shape, _mybir.dt.float32, kind="ExternalOutput").ap())
    build(nc, *args)
    r = _run(nc, [arrays], core_ids=[0])
    return r.results[0]["out_0_dram"]
```

```python
from contextlib import ExitStack

import concourse.bass as bass
from concourse import mybir

F32 = mybir.dt.float32
F32R = mybir.dt.float32r
BF16 = mybir.dt.bfloat16
I32 = mybir.dt.int32
U32 = mybir.dt.uint32
U8 = mybir.dt.uint8
ALU = mybir.AluOpType
ACT = mybir.ActivationFunctionType
AXX = mybir.AxisListType.X

P = 128


def build(nc, x, p, norm_mix, w_in, gate_up, gate_bias, gla_norm, conv_w, conv_b, ig_bias, fg_bias,
          mlstm_norm, w_out, norm_ffn, peer_query, sub_keys, peer_u, peer_v, norm_ple, w_ple,
          w_ple_gate, norm_final, out):
    _, S, D = x.shape
    NB = S // P
    KT = D // P
    CW = 512
    NQ = 4
    KQ = KT // NQ
    EPS = 1e-6
    RANK, GQK = gate_up.shape[1:]
    H = 4
    DK = GQK // H
    DV = gla_norm.shape[1] // H
    W2 = H * DV
    TAU = 16.0
    KSC = float(DK) ** -0.5
    CONV = conv_w.shape[1]
    PH, NK = sub_keys.shape[1], sub_keys.shape[3]
    TOPK = 16
    G = NB * PH
    PLE = p.shape[3]
    LEVELS = P.bit_length() - 1
    DEEP = 4
    NEG = -3.0e38
    BIG = 1.0e30

    GLR = 2 * GQK + 2 * W2
    C2 = GLR + RANK
    GATES = C2 + 2 * GQK + 2 * W2
    NSM = RANK + 2 * H
    NA = (GLR + GATES - C2) // CW
    ND = D // CW
    gA, gB, gQ, gG = 0, NA, NA + ND, NA + 2 * ND

    def slices(w):
        v = w.rearrange("(q k p) n -> q p k n", k=KQ, p=P)
        return [v[q] for q in range(NQ)]

    ctx = ExitStack()
    with ctx:
        KB = 1024

        def at(name, shape, dt, off):
            return nc.alloc_sbuf_tensor_at(name, shape, dt, offset=off)

        base, top = 16512, 229344
        used = [base]

        def next_to(name, shape, dt):
            n = 1
            for s in shape[1:]:
                n *= s
            size = n * (2 if dt == BF16 else 1 if dt == U8 else 4)
            t = at(name, shape, dt, used[0])
            used[0] += (size + 31) // 32 * 32
            return t

        h = next_to("h", [P, NB, D], F32)
        t_hi = next_to("t_hi", [P, KT, S], F32R)
        t_lo = next_to("t_lo", [P, KT, S], F32R)
        v_ring = at("v_ring", [P, DEEP, D], F32, base + 16 * KB)
        raw = next_to("raw", [P, NQ, KQ, CW], F32)
        w_hi = next_to("w_hi", [P, 2, KQ, CW], F32R)
        w_lo = next_to("w_lo", [P, 2, KQ, CW], F32R)
        nrow = next_to("nrow", [P, D], F32)
        ident = next_to("ident", [P, P], F32)
        NPAR = 3 * KT + 4 + CONV * 8 + 8
        par = next_to("par", [P, NPAR], F32)
        mask = next_to("mask", [P, LEVELS + 1, P], U8)
        cbias = next_to("cbias", [P, P], F32)
        zero16 = next_to("zero16", [P, CW], BF16)
        diag = next_to("diag", [P, DEEP, P], F32)
        stat = next_to("stat", [P, 64], F32)
        nwt = next_to("nwt", [P, 8], F32)
        scope = used[0]
        pM, pG, pP, pB, pC, pCB = 0, KT, 2 * KT, 3 * KT, 3 * KT + 4, 3 * KT + 4 + 8 * CONV

        y = next_to("y", [P, NB, D], F32)
        off_q = used[0]
        gq = next_to("gq", [P, H, S], F32)
        gk = next_to("gk", [P, H, S], F32)
        conv = at("conv", [P, 2 * H, S], F32, off_q)
        gv = next_to("gv", [P, NB, W2], F32)
        mv = next_to("mv", [P, NB, W2], F32)
        cin = next_to("cin", [P, 2 * H, CONV - 1 + S], F32)
        tfp = next_to("tfp", [P, 2, KT // 2, P], F32)
        st = next_to("st", [P, NB, H, P], F32)
        stx = next_to("stx", [P, H, P], F32)
        cum = next_to("cum", [P, H, S], F32)
        rowm = next_to("rowm", [P, 5, S], F32)
        glr = next_to("glr", [RANK, S], F32)
        stx2 = at("stx2", [P, H, P], F32, used[0])
        gup = next_to("gup", [RANK, GQK], F32)
        st2 = next_to("st2", [P, NB, H, P], F32)
        gbias = next_to("gbias", [H, 2], F32)
        sm = next_to("sm", [P, NB, NSM], F32)
        ones = next_to("ones", [P, 1], F32)
        sel = next_to("sel", [H, H, P], F32)
        mixer_end = used[0]
        stack = at("stack", [NPAR, P], F32, off_q)
        wsm = at("wsm", [P, KT, NSM], F32, off_q + 16 * KB)
        wsm_hi = at("wsm_hi", [P, KT, NSM], F32R, off_q + 18 * KB)
        wsm_lo = at("wsm_lo", [P, KT, NSM], F32R, off_q + 20 * KB)
        it_i = at("it_i", [P, P], I32, off_q + 22 * KB)
        it_p = at("it_p", [P, P], I32, off_q + 22 * KB + 512)
        it_x = at("it_x", [P, P], I32, off_q + 23 * KB)
        it_s = at("it_s", [P, P], I32, off_q + 23 * KB + 512)
        it_u = at("it_u", [P, P], F32, off_q + 22 * KB)

        used[0] = scope
        xn2 = next_to("xn2", [P, NB, D], F32)
        off_sc = used[0]
        sc = next_to("sc", [P, G, 2 * NK], F32)
        wple = at("wple", [P, PLE // P, D], F32, off_sc)
        off_u = used[0]
        u_ring = next_to("u_ring", [P, DEEP, D], F32)
        keys = at("keys", [P, 2 * PH, P], F32, off_u)
        gt = at("gt", [P, 2, NB, CW], F32, off_u)
        ple01 = at("ple01", [P, 2, NB, CW], F32, off_u + 8 * KB)
        off_qt = used[0]
        qt = next_to("qt", [P, 4, S], F32)
        pin = at("pin", [P, NB, PLE], F32, off_qt)
        pt = at("pt", [P, PLE // P, S], F32, off_qt + 2 * KB)
        ple23 = at("ple23", [P, 2, NB, CW], F32, used[0])
        keyst = next_to("keyst", [P, 2 * PH, P], F32)
        s2 = next_to("s2", [P, 2, NK], F32)
        wk = next_to("wk", [P, 2, NK], F32)
        cand = next_to("cand", [P, TOPK, TOPK], F32)
        oh = next_to("oh", [P, TOPK, TOPK], F32)
        i16 = next_to("i16", [P, TOPK], F32)
        tv = next_to("tv", [P, 2, TOPK], F32)
        ti = next_to("ti", [P, 2, TOPK], U32)
        tif = next_to("tif", [P, 2, TOPK], F32)
        cv = next_to("cv", [P, TOPK], F32)
        ci = next_to("ci", [P, TOPK], U32)
        cij = next_to("cij", [P, 2, TOPK], U32)
        cijf = next_to("cijf", [P, 2, TOPK], F32)
        pick = next_to("pick", [P, 2, TOPK], F32)
        idxn = next_to("idxn", [P, TOPK], U32)
        idxu = next_to("idxu", [P, 2, TOPK], U32)
        idxv = next_to("idxv", [P, 2, TOPK], U32)
        topc = next_to("topc", [P, TOPK], F32)
        ex = next_to("ex", [P, TOPK], F32)
        act_a = next_to("act_a", [P, TOPK], F32)
        dots = next_to("dots", [P, TOPK], F32)
        wgt = next_to("wgt", [P, TOPK], F32)
        tick = next_to("tick", [P, 2 * TOPK + 8], F32)
        esm = next_to("esm", [P, 8], F32)
        expert_end = used[0]
        assert max(mixer_end, expert_end) <= top, (mixer_end, expert_end)

        def pair(name):
            return ctx.enter_context(nc.psum_tensor(name, [P, 2 * CW], F32))

        acc = [pair("acc0"), pair("acc1")]
        mix = [pair("mix0"), pair("mix1")]

        def sem(name):
            return ctx.enter_context(nc.semaphore(name))

        x_in = [sem(f"x_in{b}") for b in range(NB)]
        par_in, wsm_in, gup_in, gb_in = sem("par_in"), sem("wsm_in"), sem("gup_in"), sem("gb_in")
        keys_in, nffn_in, nfin_in, p_in, wple_in = (sem(n) for n in ("keys_in", "nffn_in", "nfin_in", "p_in", "wple_in"))
        raw_in = [sem(f"raw_in{q}") for q in range(NQ)]
        hi_done, lo_done, slice_used = sem("hi_done"), sem("lo_done"), sem("slice_used")
        acc_free = [sem(f"acc_free{i}") for i in range(2)]
        mix_ready = sem("mix_ready")
        mix_free = [sem(f"mix_free{i}") for i in range(2)]
        const_ready, mask_ready = sem("const_ready"), sem("mask_ready")
        evac = sem("evac")
        tf_ready, thi_done, tlo_done = sem("tf_ready"), sem("thi_done"), sem("tlo_done")
        ssq_ready, var_ready, sqrt_ready = sem("ssq_ready"), sem("var_ready"), sem("sqrt_ready")
        src_ready = sem("src_ready")
        smw_hi, smw_lo, sm_ready, smt_ready = sem("smw_hi"), sem("smw_lo"), sem("sm_ready"), sem("smt_ready")
        abs_ready, softp = sem("abs_ready"), sem("softp")
        diff_ready, decay_ready, qk_ready = sem("diff_ready"), sem("decay_ready"), sem("qk_ready")
        st_ready, y_ready = sem("st_ready"), sem("y_ready")
        hsq_ready, hvar_ready, hsqrt_ready = sem("hsq_ready"), sem("hvar_ready"), sem("hsqrt_ready")
        conv_ready, silu_ready, rows_ready, cols_ready = sem("conv_ready"), sem("silu_ready"), sem("rows_ready"), sem("cols_ready")
        expo_ready, wexp_ready = sem("expo_ready"), sem("wexp_ready")
        denr_ready = sem("denr_ready")
        keyst_ready = sem("keyst_ready")
        xn2_ready, h_ready = sem("xn2_ready"), sem("h_ready")
        idx_ready, idx_taken, idx_moved = sem("idx_ready"), sem("idx_taken"), sem("idx_moved")
        u_in = [sem(f"u_in{i}") for i in range(DEEP)]
        v_in = [sem(f"v_in{i}") for i in range(DEEP)]
        u_free, v_free = sem("u_free"), sem("v_free")
        top_ready, gelu_ready, w_ready, diag_ready = sem("top_ready"), sem("gelu_ready"), sem("w_ready"), sem("diag_ready")
        exp_ready = sem("exp_ready")
        peer_ready, peer_taken = sem("peer_ready"), sem("peer_taken")
        pt_ready, ple_ready, gate_ready, out_ready, out_done = sem("pt_ready"), sem("ple_ready"), sem("gate_ready"), sem("out_ready"), sem("out_done")

        names = ["par"] + [f"tA{i}" for i in range(4)] + ["sm", "smt", "z"]
        names += ["lvd"] + [f"lv{n}" for n in range(LEVELS + 1)] + ["cols", "mbc", "go0", "go1"]
        names += ["ps", "psx", "den", "mo0", "mo1"]
        names += [f"tB{i}" for i in range(4)] + ["key0", "key1"]
        names += [f"tQ{i}" for i in range(4)] + [f"sc{c}" for c in range(ND)]
        n_before_peer = len(names)
        names += ["pt", "tG0", "tG1"] + [f"pl{c}" for c in range(ND)] + ["tG2", "tG3"]
        M = {n: i for i, n in enumerate(names)}

        def ple_tile(c):
            return (ple01 if c < 2 else ple23)[:, c % 2, :, :]

        def mix_of(name):
            return mix[M[name] % 2]

        def wait_mix(eng, name):
            eng.wait_ge(mix_ready, M[name] + 1)

        def free_sem(name):
            return mix_free[M[name] % 2]

        def take_mix(pe, name):
            m = M[name]
            if m >= n_before_peer and m < n_before_peer + 2:
                pe.wait_ge(peer_taken, 1)
            elif m >= 2:
                pe.wait_ge(mix_free[m % 2], m // 2)

        def src_blocks(phase):
            return {"A": y, "B": y, "Q": xn2, "G": xn2}[phase]

        L0 = 10
        PH_NO = {"A": 0, "B": 1, "Q": 2, "G": 3}
        SLICES_BEFORE = {"A": 0, "B": NQ * gB, "Q": NQ * gQ, "G": NQ * gG}

        with nc.Block() as block:

            @block.sync
            def _(sp):
                for b in range(NB):
                    sp.dma_start(h[:, b, :], x[0, b * P:(b + 1) * P, :]).then_inc(x_in[b], 16)

                def stream(w, g0, n, col0):
                    quarter = slices(w)

                    def chunk(g, col):
                        for q in range(NQ):
                            if not (isinstance(g, int) and g == 0):
                                sp.wait_ge(lo_done, g * NQ + q - NQ + 1)
                            sp.dma_start(raw[:, q, :, :], quarter[q][:, :, col]).then_inc(raw_in[q], 16)

                    first = 1 if g0 == 0 else 0
                    if first:
                        chunk(0, slice(col0, col0 + CW))
                    with sp.Fori(first, n) as c:
                        chunk(c + g0, bass.ds(c * CW + col0, CW))

                stream(w_in[0], 0, 4, 0)
                stream(w_in[0], 4, 4, C2)
                stream(w_in[0], 8, 2, 2 * GQK + W2)
                stream(w_in[0], 10, 2, C2 + 2 * GQK + W2)
                stream(w_out[0], gB, ND, 0)
                stream(peer_query[0], gQ, ND, 0)
                sp.wait_ge(xn2_ready, NB)
                sp.dma_start(nrow[:, :], norm_final.partition_broadcast(P)).then_inc(nfin_in, 16)
                stream(w_ple_gate[0], gG, ND, 0)
                for b in range(NB):
                    sp.wait_ge(out_ready, b + 1)
                    sp.dma_start(out[0, b * P:(b + 1) * P, :], h[:, b, :]).then_inc(out_done, 16)
                sp.wait_ge(out_done, 16 * NB)

            @block.gpsimd
            def _(pool):
                nc.gpsimd.memset(ident[:, :], 0.0)
                pool.drain()
                nc.gpsimd.affine_select(out=ident[:, :], in_=ident[:, :], compare_op=ALU.not_equal, fill=1.0,
                                        base=0, pattern=[[-1, P]], channel_multiplier=1)
                nc.gpsimd.iota(it_i[:, :], pattern=[[1, P]], base=0, channel_multiplier=0)
                nc.gpsimd.iota(it_p[:, :], pattern=[[0, P]], base=0, channel_multiplier=1)
                nc.gpsimd.memset(cbias[:, :], 0.0)
                nc.gpsimd.memset(sel[:, :, :], 0.0)
                nc.gpsimd.memset(ones[:, :], 1.0)
                nc.gpsimd.memset(zero16[:, :], 0.0)
                nc.gpsimd.memset(cin[:, :, 0:CONV - 1], 0.0)
                pool.drain()
                nc.gpsimd.affine_select(out=cbias[:, :], in_=cbias[:, :], compare_op=ALU.is_ge, fill=BIG,
                                        base=0, pattern=[[1, P]], channel_multiplier=-1)
                nc.gpsimd.affine_select(out=sel[:, :, :], in_=sel[:, :, :], compare_op=ALU.not_equal, fill=1.0,
                                        base=0, pattern=[[-1, H], [0, P]], channel_multiplier=1)
                pool.drain().then_inc(const_ready, 1)
                pool.dma_start(nrow[:, :], norm_ffn[0].partition_broadcast(P)).then_inc(nffn_in, 16)
                pool.wait_ge(tlo_done, 8)
                pool.dma_start(keys[:, :, :], sub_keys[0].rearrange("h t k d -> k (h t) d")).then_inc(keys_in, 16)
                nc.gpsimd.iota(ti[:, 0, :], pattern=[[1, TOPK]], base=0, channel_multiplier=0)
                pool.drain()
                nc.gpsimd.tensor_copy(i16[:, :], ti[:, 0, :]).then_inc(const_ready, 1)

                u_rows, v_rows = peer_u[0], peer_v[0]

                def tock(i):
                    c = 2 * TOPK + i
                    nc.gpsimd.tensor_tensor(tick[:, c:c + 1], tick[:, c + 4:c + 5], tick[:, c + 4:c + 5], ALU.add)

                def step(g, e, up, down):
                    if down:
                        pool.wait_ge(idx_taken, g)
                        tock(0)
                        nc.gpsimd.tensor_copy(idxv[:, e, :], idxu[:, 1 - e, :]).then_inc(idx_moved, 1)
                    if up:
                        pool.wait_ge(idx_ready, g + 1)
                        tock(1)
                        nc.gpsimd.tensor_copy(idxu[:, e, :], idxn[:, :]).then_inc(idx_taken, 1)
                        pool.wait_ge(idx_taken, g + 1)
                        tock(2)
                    if down:
                        pool.wait_ge(idx_moved, g)
                        tock(3)
                    for k in range(TOPK):
                        if up:
                            pool.wait_ge(u_free, g * TOPK + k + 1)
                            nc.gpsimd.tensor_tensor(tick[:, 2 * k:2 * k + 1], tick[:, 2 * TOPK + 4:2 * TOPK + 5], tick[:, 2 * TOPK + 5:2 * TOPK + 6], ALU.add)
                            nc.gpsimd.indirect_dma_start(
                                u_ring[:, k % DEEP, :], None, u_rows,
                                bass.IndirectOffsetOnAxis(idxu[:, e, k:k + 1], 0)).then_inc(u_in[k % DEEP], 16)
                        if down:
                            pool.wait_ge(v_free, (g - 1) * TOPK + k + 1)
                            nc.gpsimd.tensor_tensor(tick[:, 2 * k + 1:2 * k + 2], tick[:, 2 * TOPK + 4:2 * TOPK + 5], tick[:, 2 * TOPK + 5:2 * TOPK + 6], ALU.add)
                            nc.gpsimd.indirect_dma_start(
                                v_ring[:, k % DEEP, :], None, v_rows,
                                bass.IndirectOffsetOnAxis(idxv[:, e, k:k + 1], 0)).then_inc(v_in[k % DEEP], 16)

                nc.gpsimd.memset(tick[:, :], 0.0)
                pool.drain()
                step(0, 0, True, False)
                pool.wait_ge(slice_used, NQ * gG)
                step(1, 1, True, True)
                with pool.Fori(2, G, 2) as g:
                    step(g, 0, True, True)
                    step(g + 1, 1, True, True)
                pool.dma_start(wple[:, :, :], w_ple[0].rearrange("(k p) n -> p k n", p=P)).then_inc(wple_in, 16)
                pool.dma_start(pin[:, :, :], p[0, 0].rearrange("(b q) n -> q b n", q=P)).then_inc(p_in, 16)
                step(G, 0, False, True)

            @block.scalar
            def _(act):
                def rms_square(src, junk, phase_no, b):
                    act.activation(junk, src, ACT.Square, accum_out=stat[:, 2 * phase_no + b:2 * phase_no + b + 1]).then_inc(ssq_ready, 1)

                def rms_sqrt(n, lo, hi):
                    act.wait_ge(var_ready, n)
                    act.activation(stat[:, 16 + lo:16 + hi], stat[:, 8 + lo:8 + hi], ACT.Sqrt).then_inc(sqrt_ready, 1)

                def t_hi_part(phase, items=range(4)):
                    no = PH_NO[phase]
                    for i in items:
                        b, kh = i // 2, i % 2
                        act.wait_ge(tf_ready, 4 * no + i + 1)
                        act.activation(t_hi[:, kh * 8:kh * 8 + 8, b * P:(b + 1) * P], tfp[:, i % 2, :, :],
                                       ACT.Copy).then_inc(thi_done, 1)

                def split_hi(s):
                    g, q = s // NQ, s % NQ
                    act.wait_ge(raw_in[q], 16 * (g + 1))
                    if s >= 2:
                        act.wait_ge(slice_used, s - 1)
                    act.activation(w_hi[:, s % 2, :, :], raw[:, q, :, :], ACT.Copy).then_inc(hi_done, 1)

                def copy_out(g, dst, func, scale=1.0):
                    act.wait_ge(slice_used, NQ * (g + 1))
                    act.activation(dst, acc_view(g), func, scale=scale).then_inc(acc_free[g % 2], 1)

                def acc_view(g):
                    if g in (0, 1, 4, 5) or gQ <= g < gG:
                        return acc[g % 2][:, :].rearrange("p (s t) -> p s t", t=S)
                    return acc[g % 2][:, :].rearrange("p (b n) -> p b n", n=CW)

                def rows(dst0, vec, n):
                    act.dma_start(stack[dst0:dst0 + n, :], vec).then_inc(par_in, 16)

                rows(pM, norm_mix.rearrange("a (k p) -> (a k) p", p=P), KT)
                rows(pG, gla_norm.rearrange("a (k p) -> (a k) p", p=P), KT // 2)
                rows(pG + KT // 2, mlstm_norm.rearrange("a (k p) -> (a k) p", p=P), KT // 2)
                rows(pP, norm_ple.rearrange("a (k p) -> (a k) p", p=P), KT)
                rows(pB, gate_bias.rearrange("a (k p) -> (a k) p", p=P), 4)
                rows(pC, conv_w.rearrange("a t (k p) -> (a t k) p", p=P), 8 * CONV)
                rows(pCB, conv_b.rearrange("a (k p) -> (a k) p", p=P), 8)
                wv = w_in[0].rearrange("(k p) n -> p k n", p=P)
                act.dma_start(wsm[:, :, 0:RANK], wv[:, :, GLR:GLR + RANK]).then_inc(wsm_in, 16)
                act.dma_start(wsm[:, :, RANK:NSM], wv[:, :, GATES:GATES + 2 * H]).then_inc(wsm_in, 16)
                act.dma_start(gup[:, :], gate_up[0]).then_inc(gup_in, 16)
                act.dma_start(gbias[:, 0:1], ig_bias.rearrange("a h -> h a")).then_inc(gb_in, 16)
                act.dma_start(gbias[:, 1:2], fg_bias.rearrange("a h -> h a")).then_inc(gb_in, 16)
                for b in range(NB):
                    act.wait_ge(x_in[b], 16)
                    rms_square(h[:, b, :], y[:, b, :], 0, b)
                    rms_sqrt(b + 1, b, b + 1)
                t_hi_part("A")

                def softplus_piece(n, e, lnv):
                    act.wait_ge(abs_ready, n)
                    act.activation(e, e, ACT.Exp, scale=-1.0)
                    act.drain()
                    act.activation(lnv, e, ACT.Ln, bias=1.0).then_inc(softp, 1)

                dests = [(gq[:, :, :], ACT.Copy, KSC), (gk[:, :, :], ACT.Copy, 1.0),
                         (gv[:, :, 0:CW], ACT.Copy, 1.0), (gv[:, :, CW:2 * CW], ACT.Copy, 1.0),
                         (cin[:, 0:H, CONV - 1:], ACT.Copy, 1.0), (cin[:, H:2 * H, CONV - 1:], ACT.Copy, 1.0),
                         (mv[:, :, 0:CW], ACT.Copy, 1.0), (mv[:, :, CW:2 * CW], ACT.Copy, 1.0),
                         (y[:, :, 0:CW], ACT.Silu, 1.0), (y[:, :, CW:2 * CW], ACT.Silu, 1.0),
                         (y[:, :, W2:W2 + CW], ACT.Sigmoid, 1.0), (y[:, :, W2 + CW:2 * W2], ACT.Sigmoid, 1.0)]

                def put_out(g):
                    if g == 6:
                        act.wait_ge(sm_ready, 1)
                        act.wait_ge(mask_ready, 1)
                    copy_out(g, *dests[g])

                def decay(lv):
                    act.wait_ge(diff_ready, lv + 1)
                    e = tfp[:, lv % 2, :, :]
                    act.activation(e, e, ACT.Exp, scale=1.0 / TAU).then_inc(decay_ready, 1)

                junk = cum[:, 0, :]

                def head_squares(name, scale_col, col):
                    b = int(name[-1])
                    wait_mix(act, name)
                    for n in range(H):
                        i = b * H + n
                        if n or b:
                            act.drain()
                        kw = {} if scale_col is None else {"scale": stat[:, scale_col + i:scale_col + i + 1]}
                        ins = act.activation(junk[:, 0:DV], mix_of(name)[:, n * DV:(n + 1) * DV], ACT.Square,
                                             accum_out=stat[:, col + i:col + i + 1], **kw)
                    ins.then_inc(hsq_ready, 1)

                def head_sqrt(no, col):
                    act.wait_ge(hvar_ready, no)
                    act.activation(stat[:, col:col + 8], stat[:, col:col + 8], ACT.Sqrt).then_inc(hsqrt_ready, 1)

                def weights_exp(t):
                    act.wait_ge(expo_ready, 1)
                    tile, kb = ((st2[:, 0], 0), (st2[:, 1], 1), (stx2, 0))[t]
                    for n in range(H):
                        e = tile[:, n, :]
                        ins = act.activation(e, e, ACT.Exp, scale=-1.0, bias=stat[:, 40 + kb * H + n:41 + kb * H + n])
                    ins.then_inc(wexp_ready, 1)

                def act_slot(s):
                    if s == 4:
                        softplus_piece(1, tfp[:, 0, :, :], tfp[:, 1, :, :])
                        softplus_piece(2, rowm[0:H, 2, :], rowm[0:H, 3, :])
                    r = s - L0 - 1
                    if r >= 0 and r % 2 == 0 and r // 2 <= LEVELS:
                        decay(r // 2)
                    if s == 33:
                        head_squares("go0", None, 24)
                    if s == 34:
                        head_squares("go1", None, 24)
                    if s == 35:
                        act.wait_ge(conv_ready, 1)
                        act.activation(conv[:, :, :], conv[:, :, :], ACT.Silu).then_inc(silu_ready, 1)
                    if s == 36:
                        head_sqrt(1, 24)
                    if s in (38, 39, 40):
                        weights_exp(s - 38)
                    if s == 40:
                        act.activation(stat[:, 48:56], stat[:, 48:56], ACT.Exp).then_inc(wexp_ready, 1)

                act.wait_ge(wsm_in, 32)
                act.activation(wsm_hi[:, :, :], wsm[:, :, :], ACT.Copy).then_inc(smw_hi, 1)
                for g in range(NA):
                    for q in range(NQ):
                        split_hi(g * NQ + q)
                        if q == 1 and g >= 1:
                            put_out(g - 1)
                        act_slot(g * NQ + q)
                put_out(NA - 1)
                act.wait_ge(denr_ready, 1)
                head_squares("mo0", 56, 32)
                head_squares("mo1", 56, 32)
                head_sqrt(2, 32)
                t_hi_part("B")
                for s in range(NQ * gB, NQ * gQ):
                    split_hi(s)
                for b in range(NB):
                    act.wait_ge(h_ready, b + 1)
                    rms_square(h[:, b, :], xn2[:, b, :], 1, b)
                rms_sqrt(3, 2, 4)
                t_hi_part("Q")
                for g in range(gQ, gG):
                    for q in range(NQ):
                        split_hi(g * NQ + q)
                        if q == 1 and g > gQ:
                            if g > gQ + 1:
                                wait_mix(act, f"sc{g - gQ - 2}")
                            copy_out(g - 1, qt[:, :, :], ACT.Copy)
                wait_mix(act, f"sc{ND - 2}")
                copy_out(gG - 1, qt[:, :, :], ACT.Copy)

                def softmax_top(g):
                    act.wait_ge(top_ready, g + 1)
                    act.activation(ex[:, :], topc[:, :], ACT.Exp, bias=esm[:, 0:1], accum_out=esm[:, 1:2]).then_inc(exp_ready, 1)

                def gelu_of(g):
                    act.wait_ge(u_free, DEEP + TOPK * (g + 1))
                    act.activation(act_a[:, :], dots[:, :], ACT.Gelu_apprx_tanh).then_inc(gelu_ready, 1)

                def diags(g):
                    act.wait_ge(w_ready, g + 1)
                    for k in range(TOPK):
                        act.wait_ge(v_free, g * TOPK + k + 1)
                        act.activation(diag[:, k % DEEP, :], ident[:, :], ACT.Copy, scale=wgt[:, k:k + 1]).then_inc(diag_ready, 1)

                softmax_top(0)
                gelu_of(0)
                with act.Fori(1, G) as g:
                    softmax_top(g)
                    diags(g - 1)
                    gelu_of(g)
                act.wait_ge(h_ready, NB + 1)
                rms_square(h[:, 0, :], xn2[:, 0, :], 2, 0)
                rms_sqrt(4, 4, 5)
                diags(G - 1)
                split_hi(NQ * gG)
                split_hi(NQ * gG + 1)
                act.wait_ge(peer_ready, NB)
                t_hi_part("G", (0, 1))
                act.wait_ge(h_ready, NB + 2)
                rms_square(h[:, 1, :], xn2[:, 1, :], 2, 1)
                rms_sqrt(5, 5, 6)
                for c in range(ND):
                    name = f"pl{c}"
                    wait_mix(act, name)
                    act.activation(ple_tile(c), mix_of(name)[:, :].rearrange("p (b n) -> p b n", b=NB), ACT.Copy).then_inc(free_sem(name), 1)
                act.drain().then_inc(ple_ready, ND)
                t_hi_part("G", (2, 3))

                def gate(c):
                    if c >= 2:
                        act.wait_ge(h_ready, 2 * NB + c - 1)
                    copy_out(gG + c, gt[:, c % 2, :, :], ACT.Sigmoid)
                    act.drain().then_inc(gate_ready, 1)

                for g in range(gG, gG + ND):
                    for q in range(NQ):
                        if g * NQ + q >= NQ * gG + 2:
                            split_hi(g * NQ + q)
                        if q == 1 and g > gG:
                            gate(g - gG - 1)
                gate(ND - 1)
                for b in range(NB):
                    act.wait_ge(h_ready, 2 * NB + ND)
                    rms_square(h[:, b, :], xn2[:, b, :], 3, b)
                rms_sqrt(6, 6, 8)

            @block.vector
            def _(dve):
                V = nc.vector

                def rms_scale(n, ssq_count, lo, hi):
                    dve.wait_ge(ssq_ready, ssq_count)
                    v, r, t = stat[:, 8 + lo:8 + hi], stat[:, 16 + lo:16 + hi], nwt[:, 0:hi - lo]
                    V.tensor_scalar(v, stat[:, lo:hi], 1.0 / D, EPS, ALU.mult, ALU.add).then_inc(var_ready, 1)
                    dve.wait_ge(sqrt_ready, n)
                    newton(r, v, t)

                def newton(r, v, t):
                    V.reciprocal(r, r)
                    dve.drain()
                    V.tensor_tensor(t, r, r, ALU.mult)
                    dve.drain()
                    V.tensor_tensor(t, t, v, ALU.mult)
                    dve.drain()
                    V.tensor_scalar(t, t, -0.5, 1.5, ALU.mult, ALU.add)
                    dve.drain()
                    V.tensor_tensor(r, r, t, ALU.mult)
                    dve.drain()

                def t_scale(phase, gain, i):
                    name = f"t{phase}{i}"
                    kh = i % 2
                    dve.drain()
                    wait_mix(dve, name)
                    src = mix_of(name)[:, :].rearrange("p (k t) -> p k t", t=P)
                    if gain is None:
                        V.tensor_copy(tfp[:, i % 2, :, :], src).then_inc(free_sem(name), 1)
                    else:
                        g_ap = par[:, gain + kh * 8:gain + kh * 8 + 8].unsqueeze(2).to_broadcast([P, 8, P])
                        V.tensor_tensor(tfp[:, i % 2, :, :], src, g_ap, ALU.mult).then_inc(free_sem(name), 1)
                    dve.drain().then_inc(tf_ready, 1)

                def t_lo_part(phase, i):
                    b, kh = i // 2, i % 2
                    dve.wait_ge(thi_done, 4 * PH_NO[phase] + i + 1)
                    hi_v = t_hi[:, kh * 8:kh * 8 + 8, b * P:(b + 1) * P]
                    V.tensor_tensor(t_lo[:, kh * 8:kh * 8 + 8, b * P:(b + 1) * P], tfp[:, i % 2, :, :],
                                    hi_v.bitcast(F32), ALU.subtract).then_inc(tlo_done, 1)

                def t_parts(phase, gain):
                    if SLICES_BEFORE[phase]:
                        dve.wait_ge(slice_used, SLICES_BEFORE[phase])
                    for i in range(4):
                        if i >= 2:
                            t_lo_part(phase, i - 2)
                        t_scale(phase, gain, i)
                    t_lo_part(phase, 2)
                    t_lo_part(phase, 3)

                def split_lo(s):
                    q = s % NQ
                    dve.wait_ge(hi_done, s + 1)
                    if s >= 2:
                        dve.wait_ge(slice_used, s - 1)
                    V.tensor_tensor(w_lo[:, s % 2, :, :], raw[:, q, :, :], w_hi[:, s % 2, :, :].bitcast(F32),
                                    ALU.subtract).then_inc(lo_done, 1)

                dve.wait_ge(const_ready, 1)
                dve.drain().then_inc(u_free, DEEP)
                dve.drain().then_inc(v_free, DEEP)

                wait_mix(dve, "par")
                V.tensor_copy(par[:, :], mix_of("par")[:, 0:NPAR]).then_inc(free_sem("par"), 1)
                dve.drain()
                for b in range(NB):
                    rms_scale(b + 1, b + 1, b, b + 1)
                    V.tensor_scalar(y[:, b, :], h[:, b, :], stat[:, 16 + b:17 + b], None, ALU.mult).then_inc(src_ready, 1)
                t_parts("A", pM)
                dve.wait_ge(smw_hi, 1)
                V.tensor_tensor(wsm_lo[:, :, :], wsm[:, :, :], wsm_hi[:, :, :].bitcast(F32), ALU.subtract).then_inc(smw_lo, 1)

                def small_steps(i):
                    m = mix_of(("sm", "smt", "z")[i])
                    wait_mix(dve, ("sm", "smt", "z")[i])
                    if i == 0:
                        V.tensor_copy(sm[:, :, :], m[:, 0:NB * NSM].rearrange("p (b n) -> p b n", n=NSM)).then_inc(free_sem("sm"), 1)
                        dve.drain().then_inc(sm_ready, 1)
                    if i == 1:
                        V.tensor_copy(glr[:, :], m[0:RANK, 0:S])
                        dve.wait_ge(gb_in, 32)
                        V.tensor_scalar(rowm[0:H, 0, :], m[0:H, S:2 * S], gbias[:, 0:1], None, ALU.add)
                        V.tensor_scalar(rowm[0:H, 1, :], m[0:H, 2 * S:3 * S], gbias[:, 1:2], None, ALU.add).then_inc(free_sem("smt"), 1)
                        dve.drain().then_inc(smt_ready, 1)
                    if i == 2:
                        V.tensor_tensor(cum[:, :, :], m[:, :].rearrange("p (h t) -> p h t", t=S),
                                        par[:, pB:pB + H].unsqueeze(2).to_broadcast([P, H, S]), ALU.add).then_inc(free_sem("z"), 1)
                        dve.drain()
                        tf0 = tfp[:, 0, :, :].rearrange("p k t -> p (k t)")
                        zf = cum[:, :, :].rearrange("p h t -> p (h t)")
                        V.scalar_tensor_tensor(tf0, zf, -1.0, zf, ALU.mult, ALU.max).then_inc(abs_ready, 1)
                        V.scalar_tensor_tensor(rowm[0:H, 2, :], rowm[0:H, 1, :], -1.0, rowm[0:H, 1, :], ALU.mult, ALU.max).then_inc(abs_ready, 1)

                def log_decays(i):
                    one = ones[:, 0:1].to_broadcast([P, S])
                    if i == 0:
                        dve.wait_ge(softp, 2)
                        cf = cum[:, :, :].rearrange("p h t -> p (h t)")
                        ln = tfp[:, 1, :, :].rearrange("p k t -> p (k t)")
                        V.scalar_tensor_tensor(cf, cf, 0.0, ln, ALU.min, ALU.subtract)
                        V.scalar_tensor_tensor(rowm[0:H, 1, :], rowm[0:H, 1, :], 0.0, rowm[0:H, 3, :], ALU.min, ALU.subtract)
                    if i == 1:
                        for n in range(H):
                            V.tensor_tensor_scan(cum[:, n, :], one, cum[:, n, :], 0.0, ALU.mult, ALU.add)
                    if i == 2:
                        V.tensor_tensor_scan(rowm[0:H, 1, :], one[0:H], rowm[0:H, 1, :], 0.0, ALU.mult, ALU.add)
                        dve.drain()
                        V.tensor_tensor(rowm[0:H, 0, :], rowm[0:H, 0, :], rowm[0:H, 1, :], ALU.subtract)
                        dve.drain()
                        V.tensor_tensor_scan(rowm[0:H, 3, :], rowm[0:H, 0, :], rowm[0:H, 0, :], 0.0, ALU.max, ALU.max)
                        dve.drain()
                        V.scalar_tensor_tensor(rowm[0:H, 4, :], rowm[0:H, 1, :], -1.0, rowm[0:H, 3, :], ALU.mult, ALU.subtract).then_inc(rows_ready, 1)
                    dve.drain()

                def level_view(t, lv):
                    half = 1 << lv
                    f = t.rearrange("p h t -> p (h t)") if len(t.shape) == 3 else t
                    return f.rearrange("p (n two s) -> p n two s", two=2, s=half)

                def e_tile(lv):
                    return tfp[:, lv % 2, :, :].rearrange("p k t -> p (k t)")

                def differences(lv):
                    if lv >= 2:
                        dve.wait_ge(mix_ready, M[f"lv{lv - 2}"] + 1)
                    half = 1 << lv
                    c, e = level_view(cum[:, :, :], lv), level_view(e_tile(lv), lv)
                    n = H * S // (2 * half)
                    anchor = c[:, :, 0, half - 1:half].to_broadcast([P, n, half])
                    V.tensor_tensor(e[:, :, 1, :], c[:, :, 1, :], anchor, ALU.subtract)
                    V.tensor_tensor(e[:, :, 0, :], anchor, c[:, :, 0, :], ALU.subtract).then_inc(diff_ready, 1)

                def decayed(lv):
                    dve.wait_ge(decay_ready, lv + 1)
                    e = level_view(e_tile(lv), lv)
                    V.tensor_tensor(e[:, :, 1, :], e[:, :, 1, :], level_view(gq[:, :, :], lv)[:, :, 1, :], ALU.mult)
                    V.tensor_tensor(e[:, :, 0, :], e[:, :, 0, :], level_view(gk[:, :, :], lv)[:, :, 0, :], ALU.mult)
                    dve.drain().then_inc(qk_ready, 1)

                def take_level(name, lv):
                    wait_mix(dve, name)
                    if name == f"lv{LEVELS}":
                        V.tensor_copy(stx[:, :, :], mix_of(name)[:, 0:H * P].rearrange("p (h t) -> p h t", t=P)).then_inc(free_sem(name), 1)
                        return
                    V.copy_predicated(st[:, :, :, :].rearrange("p b h t -> p (b h) t"),
                                      mask[:, lv, :].unsqueeze(1).to_broadcast([P, NB * H, P]),
                                      mix_of(name)[:, :].rearrange("p (n t) -> p n t", t=P)).then_inc(free_sem(name), 1)
                    dve.drain()

                V.memset(st[:, :, :, :], 0.0)
                V.tensor_tensor(it_x[:, :], it_i[:, :], it_p[:, :], ALU.bitwise_xor)
                dve.drain()
                V.tensor_tensor(it_u[:, :], it_i[:, :], it_p[:, :], ALU.is_gt)
                V.tensor_scalar(mask[:, LEVELS, :], it_x[:, :], 0.0, None, ALU.is_equal)
                for lv in range(LEVELS):
                    V.tensor_scalar(it_s[:, :], it_x[:, :], lv, None, ALU.logical_shift_right)
                    dve.drain()
                    V.scalar_tensor_tensor(mask[:, lv, :], it_s[:, :], 1.0, it_u[:, :], ALU.is_equal, ALU.mult)
                    dve.drain().then_inc(mask_ready, 1)


                esm2 = sm[:, 0, 0:16]

                def head_var(no, col):
                    dve.wait_ge(hsq_ready, 2 * no)
                    V.tensor_scalar(esm2[:, 0:8], stat[:, col:col + 8], 1.0 / DV, EPS, ALU.mult, ALU.add)
                    dve.drain()
                    V.tensor_copy(stat[:, col:col + 8], esm2[:, 0:8]).then_inc(hvar_ready, 1)

                def head_scale(no, col):
                    dve.wait_ge(hsqrt_ready, no)
                    newton(stat[:, col:col + 8], esm2[:, 0:8], esm2[:, 8:16])

                def conv_tap(t):
                    if t == 0:
                        dve.wait_ge(mix_ready, M[f"lv{LEVELS}"] + 1)
                        dve.wait_ge(acc_free[1], 3)
                    else:
                        dve.drain()
                    for c in range(2 * H):
                        w_ap = par[:, pC + t * 8 + c:pC + t * 8 + c + 1]
                        src = cin[:, c, t:t + S]
                        if t == 0:
                            V.tensor_scalar(conv[:, c, :], src, w_ap, par[:, pCB + c:pCB + c + 1], ALU.mult, ALU.add)
                        else:
                            V.scalar_tensor_tensor(conv[:, c, :], src, w_ap, conv[:, c, :], ALU.mult, ALU.add)
                    if t == CONV - 1:
                        dve.drain().then_inc(conv_ready, 1)

                def normed(prefix, col, dst):
                    for b in range(NB):
                        name = f"{prefix}{b}"
                        for n in range(H):
                            i = b * H + n
                            cols = slice(n * DV, (n + 1) * DV)
                            ins = V.tensor_scalar(dst[:, b, cols], mix_of(name)[:, cols], stat[:, col + i:col + i + 1], None, ALU.mult)
                        ins.then_inc(free_sem(name), 1)

                def dve_slot(s):
                    if s in (0, 1, 3):
                        small_steps((0, 1, 3).index(s))
                    if s in (6, 7, 8):
                        log_decays(s - 6)
                    if s == 12:
                        take_level("lvd", LEVELS)
                    r = s - L0
                    if r >= 0 and r % 2 == 0:
                        n = r // 2
                        if n <= LEVELS:
                            differences(n)
                        if 1 <= n <= LEVELS + 1:
                            decayed(n - 1)
                    if r >= 0 and r % 2 == 1 and 2 <= r // 2 <= LEVELS + 2:
                        take_level(f"lv{r // 2 - 2}", r // 2 - 2)
                        if r // 2 == LEVELS + 2:
                            dve.drain().then_inc(st_ready, 1)
                    if s in (27, 28, 30, 32):
                        conv_tap((27, 28, 30, 32).index(s))
                    if s == 31:
                        wait_mix(dve, "cols")
                        V.tensor_copy(stat[:, 40:56], mix_of("cols")[:, 0:16]).then_inc(free_sem("cols"), 1)
                        wait_mix(dve, "mbc")
                        mb = mix_of("mbc")[:, :].rearrange("p (h b t) -> p h b t", h=H, b=NB)
                        for b in range(NB):
                            V.tensor_tensor(st2[:, b, :, :], mb[:, :, b, :], cbias[:, :].unsqueeze(1).to_broadcast([P, H, P]), ALU.add)
                        V.tensor_copy(stx2[:, :, :], mb[:, :, 1, :]).then_inc(free_sem("mbc"), 1)
                        dve.drain().then_inc(expo_ready, 1)
                    if s == 35:
                        head_var(1, 24)
                    if s == 37:
                        head_scale(1, 24)
                        normed("go", 24, gv)
                    if s == 42:
                        dve.wait_ge(wexp_ready, 3)
                        wait_mix(dve, "ps")
                        sv = st2[:, :, :, :].rearrange("p b h t -> p (b h t)")
                        V.scalar_tensor_tensor(sv, mix_of("ps")[:, :], KSC, sv, ALU.mult, ALU.mult).then_inc(free_sem("ps"), 1)
                        wait_mix(dve, "psx")
                        sv = stx2[:, :, :].rearrange("p h t -> p (h t)")
                        V.scalar_tensor_tensor(sv, mix_of("psx")[:, 0:H * P], KSC, sv, ALU.mult, ALU.mult).then_inc(free_sem("psx"), 1)
                        dve.drain().then_inc(st_ready, 1)
                    if s == 45:
                        dve.wait_ge(acc_free[1], 5)
                        V.tensor_tensor(y[:, :, 0:W2], y[:, :, 0:W2], gv[:, :, :], ALU.mult)
                    if s == 46:
                        wait_mix(dve, "den")
                        V.tensor_copy(esm2[:, 0:8], mix_of("den")[:, 0:8]).then_inc(free_sem("den"), 1)
                        dve.drain()
                        V.scalar_tensor_tensor(stat[:, 56:64], esm2[:, 0:8], -1.0, esm2[:, 0:8], ALU.mult, ALU.max)
                        dve.drain()
                        dve.wait_ge(wexp_ready, 4)
                        V.tensor_tensor(stat[:, 56:64], stat[:, 56:64], stat[:, 48:56], ALU.max)
                        dve.drain()
                        V.reciprocal(stat[:, 56:64], stat[:, 56:64])
                        dve.drain().then_inc(denr_ready, 1)

                for g in range(NA):
                    for q in range(NQ):
                        split_lo(g * NQ + q)
                        dve_slot(g * NQ + q)
                dve.drain().then_inc(src_ready, 1)
                head_var(2, 32)
                head_scale(2, 32)
                V.tensor_tensor(stat[:, 32:40], stat[:, 32:40], stat[:, 56:64], ALU.mult)
                dve.drain()
                normed("mo", 32, mv)
                dve.drain()
                dve.wait_ge(acc_free[1], 6)
                V.tensor_tensor(y[:, :, W2:], y[:, :, W2:], mv[:, :, :], ALU.mult)
                dve.drain().then_inc(src_ready, 1)
                t_parts("B", pG)
                for g in range(gB, gQ):
                    for q in range(NQ):
                        split_lo(g * NQ + q)
                        if q == 1 and g > gB:
                            add_chunk(dve, V, g - 1, h, acc, slice_used, acc_free, NQ, CW, gB)
                add_chunk(dve, V, gQ - 1, h, acc, slice_used, acc_free, NQ, CW, gB)
                dve.drain().then_inc(h_ready, NB)
                rms_scale(3, 4, 2, 4)
                for b in range(NB):
                    V.tensor_scalar(xn2[:, b, :], h[:, b, :], stat[:, 18 + b:19 + b], None, ALU.mult).then_inc(src_ready, 1)
                for i in range(2):
                    wait_mix(dve, f"key{i}")
                    V.tensor_copy(keyst[:, i * 8:i * 8 + 8, :], mix_of(f"key{i}")[:, :].rearrange("p (k t) -> p k t", t=P)).then_inc(free_sem(f"key{i}"), 1)
                dve.wait_ge(nffn_in, 16)
                dve.drain()
                for b in range(NB):
                    V.tensor_tensor(xn2[:, b, :], xn2[:, b, :], nrow[:, :], ALU.mult).then_inc(xn2_ready, 1)
                t_parts("Q", None)
                dve.drain().then_inc(keyst_ready, 1)

                def take_scores(c):
                    wait_mix(dve, f"sc{c}")
                    m = mix_of(f"sc{c}")[:, :].rearrange("p (b n) -> p b n", b=NB)
                    dst = sc[:, :, :].rearrange("p (b h) n -> p b (h n)", b=NB)[:, :, c * CW:(c + 1) * CW]
                    V.tensor_copy(dst, m).then_inc(free_sem(f"sc{c}"), 1)


                def top_k(g):
                    V.tensor_copy(s2[:, :, :].rearrange("p a n -> p (a n)").unsqueeze(1), sc[:, bass.ds(g, 1), :])
                    dve.drain()
                    for a in range(2):
                        V.max(tv[:, a, 0:8], s2[:, a, :])
                    dve.drain()
                    for a in range(2):
                        V.max_index(ti[:, a, 0:8], tv[:, a, 0:8], s2[:, a, :])
                        V.match_replace(wk[:, a, :], tv[:, a, 0:8], s2[:, a, :], NEG)
                    dve.drain()
                    for a in range(2):
                        V.max(tv[:, a, 8:16], wk[:, a, :])
                    dve.drain()
                    for a in range(2):
                        V.max_index(ti[:, a, 8:16], tv[:, a, 8:16], wk[:, a, :])
                    V.tensor_tensor(cand[:, :, :], tv[:, 0, :].unsqueeze(2).to_broadcast([P, TOPK, TOPK]),
                                    tv[:, 1, :].unsqueeze(1).to_broadcast([P, TOPK, TOPK]), ALU.add)
                    dve.drain()
                    V.tensor_copy(tif[:, :, :], ti[:, :, :])
                    cf, wf = cand[:, :, :].rearrange("p a n -> p (a n)"), wk[:, :, :].rearrange("p a n -> p (a n)")
                    V.max(cv[:, 0:8], cf)
                    dve.drain()
                    V.max_index(ci[:, 0:8], cv[:, 0:8], cf)
                    V.match_replace(wf, cv[:, 0:8], cf, NEG)
                    dve.drain()
                    V.max(cv[:, 8:16], wf)
                    dve.drain()
                    V.max_index(ci[:, 8:16], cv[:, 8:16], wf)
                    dve.drain()
                    V.tensor_scalar(cij[:, 0, :], ci[:, :], 4, None, ALU.logical_shift_right)
                    V.tensor_scalar(cij[:, 1, :], ci[:, :], TOPK - 1, None, ALU.bitwise_and)
                    dve.drain()
                    V.tensor_copy(cijf[:, :, :], cij[:, :, :])
                    dve.drain()
                    for a in range(2):
                        V.tensor_tensor(oh[:, :, :], cijf[:, a, :].unsqueeze(2).to_broadcast([P, TOPK, TOPK]),
                                        i16[:, :].unsqueeze(1).to_broadcast([P, TOPK, TOPK]), ALU.is_equal)
                        dve.drain()
                        V.tensor_tensor(oh[:, :, :], oh[:, :, :], tif[:, a, :].unsqueeze(1).to_broadcast([P, TOPK, TOPK]), ALU.mult)
                        dve.drain()
                        V.tensor_reduce(pick[:, a, :], oh[:, :, :], AXX, ALU.add)
                        dve.drain()
                    V.scalar_tensor_tensor(pick[:, 0, :], pick[:, 0, :], float(NK), pick[:, 1, :], ALU.mult, ALU.add)
                    dve.drain()
                    if not (isinstance(g, int) and g == 0):
                        dve.wait_ge(idx_taken, g)
                    V.tensor_copy(idxn[:, :], pick[:, 0, :]).then_inc(idx_ready, 1)

                def current_top(g):
                    V.tensor_copy(topc[:, :], cv[:, :])
                    V.tensor_scalar(esm[:, 0:1], cv[:, 0:1], -1.0, None, ALU.mult)
                    dve.drain().then_inc(top_ready, 1)

                def products(g, b, picks=range(TOPK)):
                    for k in picks:
                        dve.wait_ge(u_in[k % DEEP], 16 * (TOPK // DEEP) * g + 16 * (k // DEEP + 1))
                        V.tensor_tensor_reduce(out=u_ring[:, k % DEEP, :], in0=u_ring[:, k % DEEP, :], in1=xn2[:, b, :],
                                               scale=1.0, scalar=0.0, op0=ALU.mult, op1=ALU.add,
                                               accum_out=dots[:, k:k + 1]).then_inc(u_free, 1)

                def weights(g):
                    dve.wait_ge(exp_ready, g + 1)
                    V.reciprocal(esm[:, 2:3], esm[:, 1:2])
                    dve.drain()
                    dve.wait_ge(gelu_ready, g + 1)
                    V.scalar_tensor_tensor(wgt[:, :], ex[:, :], esm[:, 2:3], act_a[:, :], ALU.mult, ALU.mult).then_inc(w_ready, 1)

                dve.wait_ge(const_ready, 2)
                per_slice = {(2, 2): range(0, 2), (2, 3): range(2, 4), (3, 0): range(4, 6), (3, 1): range(6, 9),
                             (3, 2): range(9, 12), (3, 3): range(12, 16)}
                for c in range(ND):
                    for q in range(NQ):
                        split_lo((gQ + c) * NQ + q)
                        if q == 3 and c > 0:
                            take_scores(c - 1)
                        if (c, q) == (2, 0):
                            dve.drain()
                            top_k(0)
                            dve.drain()
                            current_top(0)
                        if (c, q) == (3, 0):
                            top_k(1)
                        if (c, q) in per_slice:
                            products(0, 0, per_slice[c, q])
                take_scores(ND - 1)
                weights(0)
                for b in range(NB):
                    with dve.Fori(max(b * PH, 1), (b + 1) * PH - (b == NB - 1)) as g:
                        dve.drain()
                        current_top(g)
                        top_k(g + 1)
                        products(g, b)
                        weights(g)
                dve.drain()
                current_top(G - 1)
                products(G - 1, NB - 1)
                weights(G - 1)

                def add_experts(b, pairs):
                    dve.wait_ge(peer_ready, b + 1)
                    for i in range(2):
                        hv = h[:, b, i * 2 * CW:(i + 1) * 2 * CW]
                        V.tensor_tensor(hv, hv, pairs[i][:, :], ALU.add)
                    dve.drain().then_inc(h_ready, 1)
                    dve.drain().then_inc(peer_taken, 1)
                    rms_scale(4 + b, 5 + b, 4 + b, 5 + b)
                    V.tensor_scalar(xn2[:, b, :], h[:, b, :], stat[:, 20 + b:21 + b], None, ALU.mult).then_inc(src_ready, 1)

                add_experts(0, mix)
                wait_mix(dve, "pt")
                V.tensor_copy(pt[:, :, :], mix_of("pt")[:, 0:2 * S].rearrange("p (k t) -> p k t", t=S)).then_inc(free_sem("pt"), 1)
                dve.drain().then_inc(pt_ready, 1)
                t_scale("G", pP, 0)
                t_scale("G", pP, 1)
                split_lo(NQ * gG)
                split_lo(NQ * gG + 1)
                add_experts(1, acc)
                t_lo_part("G", 0)
                t_lo_part("G", 1)
                t_scale("G", pP, 2)
                t_scale("G", pP, 3)
                t_lo_part("G", 2)
                t_lo_part("G", 3)

                def add_ple(c):
                    dve.wait_ge(gate_ready, c + 1)
                    dve.wait_ge(ple_ready, c + 1)
                    gv_ = gt[:, c % 2, :, :]
                    V.tensor_tensor(gv_, gv_, ple_tile(c), ALU.mult)
                    dve.drain()
                    hv = h[:, :, c * CW:(c + 1) * CW]
                    V.tensor_tensor(hv, hv, gv_, ALU.add).then_inc(h_ready, 1)

                for g in range(gG, gG + ND):
                    for q in range(NQ):
                        if g * NQ + q >= NQ * gG + 2:
                            split_lo(g * NQ + q)
                        if q == 2 and g > gG:
                            add_ple(g - gG - 1)
                add_ple(ND - 1)
                dve.drain()
                rms_scale(6, 8, 6, 8)
                dve.wait_ge(nfin_in, 16)
                for b in range(NB):
                    V.scalar_tensor_tensor(h[:, b, :], h[:, b, :], stat[:, 22 + b:23 + b], nrow[:, :], ALU.mult, ALU.mult).then_inc(out_ready, 1)

            @block.tensor
            def _(pe):
                T = nc.tensor

                def transposes(phase, items=range(4)):
                    src = src_blocks(phase)
                    no = PH_NO[phase]
                    for i in items:
                        name = f"t{phase}{i}"
                        b, kh = i // 2, i % 2
                        pe.wait_ge(src_ready, NB * no + (kh + 1 if phase == "B" else b + 1 if phase in "AG" else NB))
                        if phase == "Q":
                            pe.wait_ge(xn2_ready, b + 1)
                        take_mix(pe, name)
                        for k in range(8):
                            kt = kh * 8 + k
                            ins = T.transpose(mix_of(name)[:, k * P:(k + 1) * P], src[:, b, kt * P:(kt + 1) * P], ident[:, :])
                        ins.then_inc(mix_ready, 1)

                def begin_chunk(set_no, uses):
                    if uses is not None:
                        pe.wait_ge(acc_free[set_no], uses)

                def token_slice(set_no, s_slot, q, lo_count):
                    pe.wait_ge(lo_done, lo_count)
                    for k in range(KQ):
                        kt = q * KQ + k
                        for b in range(NB):
                            tok = slice(b * P, (b + 1) * P)
                            for n, (a, w) in enumerate(((t_hi, w_hi), (t_hi, w_lo), (t_lo, w_hi))):
                                ins = T.matmul(acc[set_no][:, b * CW:(b + 1) * CW], a[:, kt, tok], w[:, s_slot, k, :],
                                               start=(kt == 0 and n == 0), stop=(kt == KT - 1 and n == 2))
                    ins.then_inc(slice_used, 1)

                def column_slice(set_no, s_slot, q, lo_count):
                    pe.wait_ge(lo_done, lo_count)
                    for k in range(KQ):
                        kt = q * KQ + k
                        for c in range(CW // P):
                            for n, (w, a) in enumerate(((w_hi, t_hi), (w_hi, t_lo), (w_lo, t_hi))):
                                ins = T.matmul(acc[set_no][:, c * S:(c + 1) * S], w[:, s_slot, k, c * P:(c + 1) * P], a[:, kt, :],
                                               start=(kt == 0 and n == 0 and c % 2 == 0), stop=(kt == KT - 1 and n == 2),
                                               skip_group_check=True)
                    ins.then_inc(slice_used, 1)

                def chunk(g, kind, after=None):
                    begin_chunk(g % 2, g // 2 if g >= 2 else None)
                    for q in range(NQ):
                        kind(g % 2, (g * NQ + q) % 2, q, g * NQ + q + 1)
                        if after is not None:
                            after(g * NQ + q)

                pe.wait_ge(const_ready, 1)
                pe.wait_ge(par_in, 16 * 7)
                T.transpose(mix_of("par")[:, 0:NPAR], stack[:, :], ident[0:NPAR, 0:NPAR]).then_inc(mix_ready, 1)
                transposes("A")
                pe.wait_ge(tlo_done, 4)
                take_mix(pe, "sm")
                pe.wait_ge(smw_lo, 1)
                for kt in range(KT):
                    for b in range(NB):
                        tok = slice(b * P, (b + 1) * P)
                        for n, (a, w) in enumerate(((t_hi, wsm_hi), (t_hi, wsm_lo), (t_lo, wsm_hi))):
                            ins = T.matmul(mix_of("sm")[:, b * NSM:(b + 1) * NSM], a[:, kt, tok], w[:, kt, :],
                                           start=(kt == 0 and n == 0 and b == 0), stop=(kt == KT - 1 and n == 2),
                                           skip_group_check=True)
                ins.then_inc(mix_ready, 1)

                def level_item(name, lv):
                    take_mix(pe, name)
                    m = mix_of(name)
                    if name == "lvd":
                        pe.wait_ge(acc_free[1], 1)
                        kk, qq = gk[:, :, :], gq[:, :, :]
                    else:
                        pe.wait_ge(qk_ready, lv + 1)
                        kk = qq = tfp[:, lv % 2, :, :].rearrange("p k t -> p (k t)").rearrange("p (h t) -> p h t", t=S)
                    if lv == LEVELS and name != "lvd":
                        for n in range(H):
                            ins = T.matmul(m[:, n * P:(n + 1) * P], kk[:, n, 0:P], qq[:, n, P:2 * P], start=True, stop=True)
                    else:
                        for b in range(NB):
                            for n in range(H):
                                ins = T.matmul(m[:, (b * H + n) * P:(b * H + n + 1) * P], kk[:, n, b * P:(b + 1) * P],
                                               qq[:, n, b * P:(b + 1) * P], start=True, stop=True)
                    ins.then_inc(mix_ready, 1)

                def attend(name, within, across, values):
                    b = int(name[-1])
                    take_mix(pe, name)
                    for n in range(H):
                        o, cols = mix_of(name)[:, n * DV:(n + 1) * DV], slice(n * DV, (n + 1) * DV)
                        ins = T.matmul(o, within[:, b, n, :], values[:, b, cols], start=True, stop=(b == 0))
                        if b == 1:
                            ins = T.matmul(o, across[:, n, :], values[:, 0, cols], start=False, stop=True)
                    ins.then_inc(mix_ready, 1)

                def pe_slot(s):
                    if s == 0:
                        take_mix(pe, "smt")
                        pe.wait_ge(sm_ready, 1)
                        for b in range(NB):
                            m = mix_of("smt")
                            T.transpose(m[0:RANK, b * P:(b + 1) * P], sm[:, b, 0:RANK], ident[:, :])
                            T.transpose(m[0:H, S + b * P:S + (b + 1) * P], sm[:, b, RANK:RANK + H], ident[:, :])
                            ins = T.transpose(m[0:H, 2 * S + b * P:2 * S + (b + 1) * P], sm[:, b, RANK + H:NSM], ident[:, :])
                        ins.then_inc(mix_ready, 1)
                    if s == 2:
                        take_mix(pe, "z")
                        pe.wait_ge(smt_ready, 1)
                        pe.wait_ge(gup_in, 16)
                        for n in range(H):
                            ins = T.matmul(mix_of("z")[:, n * S:(n + 1) * S], gup[:, n * DK:(n + 1) * DK], glr[:, :], start=True, stop=True)
                        ins.then_inc(mix_ready, 1)
                    if s == L0:
                        level_item("lvd", LEVELS)
                    r = s - L0
                    if r >= 2 and r % 2 == 0 and r // 2 <= LEVELS + 1:
                        level_item(f"lv{r // 2 - 1}", r // 2 - 1)
                    if s == 28:
                        take_mix(pe, "cols")
                        pe.wait_ge(rows_ready, 1)
                        for i, row in enumerate((0, 4)):
                            for b in range(NB):
                                c = i * 8 + b * H
                                ins = T.transpose(mix_of("cols")[:, c:c + H], rowm[0:H, row, b * P:(b + 1) * P], ident[0:H, 0:H])
                        ins.then_inc(mix_ready, 1)
                        take_mix(pe, "mbc")
                        for n in range(H):
                            ins = T.matmul(mix_of("mbc")[:, n * S:(n + 1) * S], sel[:, n, :], rowm[0:H, 3, :], start=True, stop=True)
                        ins.then_inc(mix_ready, 1)
                    if s == 31:
                        pe.wait_ge(st_ready, 1)
                        pe.wait_ge(acc_free[1], 2)
                        attend("go0", st, stx, gv)
                        attend("go1", st, stx, gv)
                    if s == 39:
                        take_mix(pe, "ps")
                        pe.wait_ge(silu_ready, 1)
                        for b in range(NB):
                            for n in range(H):
                                ins = T.matmul(mix_of("ps")[:, (b * H + n) * P:(b * H + n + 1) * P], conv[:, H + n, b * P:(b + 1) * P],
                                               conv[:, n, b * P:(b + 1) * P], start=True, stop=True)
                        ins.then_inc(mix_ready, 1)
                        take_mix(pe, "psx")
                        for n in range(H):
                            ins = T.matmul(mix_of("psx")[:, n * P:(n + 1) * P], conv[:, H + n, 0:P], conv[:, n, P:2 * P], start=True, stop=True)
                        ins.then_inc(mix_ready, 1)
                    if s == 43:
                        pe.wait_ge(st_ready, 2)
                        take_mix(pe, "den")
                        for b in range(NB):
                            for n in range(H):
                                o = mix_of("den")[:, b * H + n:b * H + n + 1]
                                ins = T.matmul(o, st2[:, b, n, :], ones[:, :], start=True, stop=(b == 0))
                                if b == 1:
                                    ins = T.matmul(o, stx2[:, n, :], ones[:, :], start=False, stop=True)
                        ins.then_inc(mix_ready, 1)
                        pe.wait_ge(acc_free[1], 4)
                        attend("mo0", st2, stx2, mv)
                    if s == 46:
                        attend("mo1", st2, stx2, mv)

                for g in range(NA):
                    chunk(g, column_slice if g in (0, 1, 4, 5) else token_slice, pe_slot)
                transposes("B")
                pe.wait_ge(tlo_done, 8)
                with pe.Fori(0, ND // 2) as t:
                    for e in range(2):
                        begin_chunk(e, t + gB // 2)
                        for q in range(NQ):
                            token_slice(e, q % 2, q, t * 2 * NQ + (gB + e) * NQ + q + 1)
                for i in range(2):
                    take_mix(pe, f"key{i}")
                    pe.wait_ge(keys_in, 16)
                    for k in range(8):
                        ins = T.transpose(mix_of(f"key{i}")[:, k * P:(k + 1) * P], keys[:, i * 8 + k, :], ident[:, :])
                    ins.then_inc(mix_ready, 1)
                transposes("Q")
                pe.wait_ge(tlo_done, 12)
                pe.wait_ge(keyst_ready, 1)

                def scores(c):
                    name = f"sc{c}"
                    g = gQ + c
                    take_mix(pe, name)
                    pe.wait_ge(acc_free[g % 2], g // 2 + 1)
                    for b in range(NB):
                        for a in range(4):
                            ins = T.matmul(mix_of(name)[:, (b * 4 + a) * P:(b * 4 + a + 1) * P], qt[:, a, b * P:(b + 1) * P],
                                           keyst[:, c * 4 + a, :], start=True, stop=True)
                    ins.then_inc(mix_ready, 1)

                for c in range(ND):
                    g = gQ + c
                    begin_chunk(g % 2, g // 2)
                    for q in range(NQ):
                        column_slice(g % 2, q % 2, q, g * NQ + q + 1)
                        if q == 2 and c >= 1:
                            scores(c - 1)
                scores(ND - 1)

                for b, pairs in enumerate((mix, acc)):
                    if b == 0:
                        for i in range(2):
                            last = max(m for m in range(n_before_peer) if m % 2 == i)
                            pe.wait_ge(mix_free[i], last // 2 + 1)
                    for i in range(2):
                        for j in range(2):
                            T.matmul(pairs[i][:, j * CW:(j + 1) * CW], zero16[:, 0:P], zero16[:, :], start=True, stop=False, skip_group_check=True)

                    def down(g, picks):
                        for k in picks:
                            pe.wait_ge(diag_ready, g * TOPK + k + 1)
                            pe.wait_ge(v_in[k % DEEP], 16 * (TOPK // DEEP) * g + 16 * (k // DEEP + 1))
                            for j in range(4):
                                ins = T.matmul(pairs[j // 2][:, (j % 2) * CW:(j % 2 + 1) * CW], diag[:, k % DEEP, :],
                                               v_ring[:, k % DEEP, j * CW:(j + 1) * CW], start=False, stop=False, skip_group_check=True)
                            ins.then_inc(v_free, 1)

                    with pe.Fori(b * PH, (b + 1) * PH - (b == NB - 1)) as g:
                        down(g, range(TOPK))
                    if b == NB - 1:
                        down(G - 1, range(TOPK // 2))
                        take_mix(pe, "pt")
                        pe.wait_ge(p_in, 16)
                        for bb in range(NB):
                            for k in range(PLE // P):
                                ins = T.transpose(mix_of("pt")[:, k * S + bb * P:k * S + (bb + 1) * P], pin[:, bb, k * P:(k + 1) * P], ident[:, :])
                        ins.then_inc(mix_ready, 1)
                        transposes("G", (0, 1))
                        down(G - 1, range(TOPK // 2, TOPK))
                    for i in range(2):
                        for j in range(2):
                            ins = T.matmul(pairs[i][:, j * CW:(j + 1) * CW], zero16[:, 0:P], zero16[:, :], start=False, stop=True, skip_group_check=True)
                    ins.then_inc(peer_ready, 1)

                pe.wait_ge(pt_ready, 1)
                pe.wait_ge(wple_in, 16)
                for c in range(ND):
                    name = f"pl{c}"
                    take_mix(pe, name)
                    for b in range(NB):
                        for k in range(PLE // P):
                            ins = T.matmul(mix_of(name)[:, b * CW:(b + 1) * CW], pt[:, k, b * P:(b + 1) * P], wple[:, k, c * CW:(c + 1) * CW],
                                           start=(k == 0), stop=(k == PLE // P - 1))
                    ins.then_inc(mix_ready, 1)
                transposes("G", (2, 3))
                pe.wait_ge(tlo_done, 16)
                pe.wait_ge(peer_taken, 2)
                for c in range(ND):
                    g = gG + c
                    if c >= 2:
                        begin_chunk(g % 2, g // 2)
                    for q in range(NQ):
                        token_slice(g % 2, q % 2, q, g * NQ + q + 1)


def add_chunk(dve, V, g, h, acc, slice_used, acc_free, NQ, CW, gB):
    dve.wait_ge(slice_used, NQ * (g + 1))
    c = g - gB
    hv = h[:, :, c * CW:(c + 1) * CW]
    V.tensor_tensor(hv, hv, acc[g % 2][:, :].rearrange("p (b n) -> p b n", n=CW), ALU.add).then_inc(acc_free[g % 2], 1)


_INS = ['x', 'p', 'norm_mix', 'w_in', 'gla_gate_up', 'gla_gate_bias', 'gla_norm', 'mlstm_conv_w', 'mlstm_conv_b',
        'mlstm_igate_bias', 'mlstm_fgate_bias', 'mlstm_norm', 'w_out', 'norm_ffn', 'peer_query', 'peer_sub_keys',
        'peer_u', 'peer_v', 'norm_ple', 'w_ple', 'w_ple_gate', 'norm_final']


def kernel(**inputs):
    import numpy as _np
    import concourse.bacc as _bacc
    from concourse import mybir as _mybir
    from concourse.bass_utils import run_bass_kernel_spmd as _run

    nc = _bacc.Bacc("TRN2", target_bir_lowering=False, num_devices=1)
    arrays, args = {}, []
    for name in _INS:
        a = _np.ascontiguousarray(inputs[name])
        arrays[f"in_{name}_dram"] = a
        args.append(nc.dram_tensor(f"in_{name}_dram", a.shape, _mybir.dt.from_np(a.dtype), kind="ExternalInput").ap())
    shape = tuple(inputs['x'].shape)
    args.append(nc.dram_tensor("out_0_dram", shape, _mybir.dt.float32, kind="ExternalOutput").ap())
    build(nc, *args)
    r = _run(nc, [arrays], core_ids=[0])
    return r.results[0]["out_0_dram"]
```

```python
from contextlib import ExitStack

import concourse.bass as bass
from concourse import mybir

F32 = mybir.dt.float32
F32R = mybir.dt.float32r
BF16 = mybir.dt.bfloat16
I32 = mybir.dt.int32
U32 = mybir.dt.uint32
U8 = mybir.dt.uint8
ALU = mybir.AluOpType
ACT = mybir.ActivationFunctionType
AXX = mybir.AxisListType.X

P = 128


def build(nc, x, p, norm_mix, w_in, gate_up, gate_bias, gla_norm, conv_w, conv_b, ig_bias, fg_bias,
          mlstm_norm, w_out, norm_ffn, peer_query, sub_keys, peer_u, peer_v, norm_ple, w_ple,
          w_ple_gate, norm_final, out):
    _, S, D = x.shape
    NB = S // P
    KT = D // P
    CW = 512
    NQ = 4
    KQ = KT // NQ
    EPS = 1e-6
    RANK, GQK = gate_up.shape[1:]
    H = 4
    DK = GQK // H
    DV = gla_norm.shape[1] // H
    W2 = H * DV
    TAU = 16.0
    KSC = float(DK) ** -0.5
    CONV = conv_w.shape[1]
    PH, NK = sub_keys.shape[1], sub_keys.shape[3]
    TOPK = 16
    G = NB * PH
    PLE = p.shape[3]
    LEVELS = P.bit_length() - 1
    DEEP = 4
    NEG = -3.0e38
    BIG = 1.0e30

    GLR = 2 * GQK + 2 * W2
    C2 = GLR + RANK
    GATES = C2 + 2 * GQK + 2 * W2
    NSM = RANK + 2 * H
    NA = (GLR + GATES - C2) // CW
    ND = D // CW
    gB, gQ, gG = NA, NA + ND, NA + 2 * ND

    def slices(w):
        v = w.rearrange("(q k p) n -> q p k n", k=KQ, p=P)
        return [v[q] for q in range(NQ)]

    ctx = ExitStack()
    with ctx:
        KB = 1024

        def at(name, shape, dt, off):
            return nc.alloc_sbuf_tensor_at(name, shape, dt, offset=off)

        base, top = 16512, 229344
        used = [base]

        def next_to(name, shape, dt):
            n = 1
            for s in shape[1:]:
                n *= s
            size = n * (2 if dt == BF16 else 1 if dt == U8 else 4)
            t = at(name, shape, dt, used[0])
            used[0] += (size + 31) // 32 * 32
            return t

        h = next_to("h", [P, NB, D], F32)
        t_hi = next_to("t_hi", [P, KT, S], F32R)
        t_lo = next_to("t_lo", [P, KT, S], F32R)
        v_ring = at("v_ring", [P, DEEP, D], F32, base + 16 * KB)
        raw = next_to("raw", [P, NQ, KQ, CW], F32)
        w_hi = next_to("w_hi", [P, 2, KQ, CW], F32R)
        w_lo = next_to("w_lo", [P, 2, KQ, CW], F32R)
        conv = at("conv", [P, 2 * H, S], F32, used[0])
        nrow = next_to("nrow", [P, D], F32)
        ident = next_to("ident", [P, P], F32)
        NPAR = 4 * KT + 4 + CONV * 8 + 8
        par = next_to("par", [P, NPAR], F32)
        mask = next_to("mask", [P, LEVELS + 1, P], U8)
        cbias = next_to("cbias", [P, P], F32)
        zero16 = next_to("zero16", [P, CW], BF16)
        diag = next_to("diag", [P, DEEP, P], F32)
        stat = next_to("stat", [P, 64], F32)
        nwt = next_to("nwt", [P, 8], F32)
        scope = used[0]
        pM, pG, pP, pF, pB, pC, pCB = 0, KT, 2 * KT, 3 * KT, 4 * KT, 4 * KT + 4, 4 * KT + 4 + 8 * CONV

        y = next_to("y", [P, NB, D], F32)
        off_q = used[0]
        gq = next_to("gq", [P, H, S], F32)
        gk = next_to("gk", [P, H, S], F32)
        mo = at("mo", [P, NB, W2], F32, off_q)
        gv = next_to("gv", [P, NB, W2], F32)
        mv = next_to("mv", [P, NB, W2], F32)
        cin = next_to("cin", [P, 2 * H, CONV - 1 + S], F32)
        tfp = next_to("tfp", [P, 2, KT // 2, P], F32)
        st = next_to("st", [P, NB, H, P], F32)
        stx = next_to("stx", [P, H, P], F32)
        cum = next_to("cum", [P, H, S], F32)
        rowm = next_to("rowm", [P, 5, S], F32)
        glr = next_to("glr", [RANK, S], F32)
        stx2 = at("stx2", [P, H, P], F32, used[0])
        gup = next_to("gup", [RANK, GQK], F32)
        st2 = next_to("st2", [P, NB, H, P], F32)
        gbias = next_to("gbias", [H, 2], F32)
        sm_sum = next_to("sm_sum", [2 * NSM, NSM], F32)
        small = next_to("small", [P, 24], F32)
        ones = next_to("ones", [P, 1], F32)
        sel = next_to("sel", [H, H, P], F32)
        mixer_end = used[0]
        stack = at("stack", [NPAR, P], F32, off_q)
        wsm = at("wsm", [P, KT, NSM], F32, off_q + 16 * KB)
        wsm_hl = at("wsm_hl", [P, KT, 2 * NSM], F32R, off_q + 18 * KB)
        it_i = at("it_i", [P, P], I32, off_q + 22 * KB)
        it_p = at("it_p", [P, P], I32, off_q + 22 * KB + 512)
        it_x = at("it_x", [P, P], I32, off_q + 23 * KB)
        it_s = at("it_s", [P, P], I32, off_q + 23 * KB + 512)
        it_u = at("it_u", [P, P], F32, off_q + 22 * KB)

        used[0] = scope
        xn2 = next_to("xn2", [P, NB, D], F32)
        off_sc = used[0]
        sc = next_to("sc", [P, G, 2 * NK], F32)
        wple = at("wple", [P, PLE // P, D], F32, off_sc)
        off_u = used[0]
        u_ring = next_to("u_ring", [P, DEEP, D], F32)
        keys = at("keys", [P, 2 * PH, P], F32, off_u)
        gt = at("gt", [P, 2, NB, CW], F32, off_u)
        ple01 = at("ple01", [P, 2, NB, CW], F32, scope)
        junk_g = [xn2[:, 1, :], u_ring[:, 1, :]]
        hn = u_ring[:, 2:4, :]
        off_qt = used[0]
        qt = next_to("qt", [P, 4, S], F32)
        pin = at("pin", [P, NB, PLE], F32, off_qt)
        pt = at("pt", [P, PLE // P, S], F32, off_qt + 2 * KB)
        ple23 = at("ple23", [P, 2, NB, CW], F32, used[0])
        keyst = next_to("keyst", [P, 2 * PH, P], F32)
        s2 = next_to("s2", [P, 2, NK], F32)
        wk = next_to("wk", [P, 2, NK], F32)
        cand = next_to("cand", [P, TOPK, TOPK], F32)
        oh = next_to("oh", [P, TOPK, TOPK], F32)
        i16 = next_to("i16", [P, TOPK], F32)
        tv = next_to("tv", [P, 2, TOPK], F32)
        ti = next_to("ti", [P, 2, TOPK], U32)
        tif = next_to("tif", [P, 2, TOPK], F32)
        cv = next_to("cv", [P, TOPK], F32)
        ci = next_to("ci", [P, TOPK], U32)
        cij = next_to("cij", [P, 2, TOPK], U32)
        cijf = next_to("cijf", [P, 2, TOPK], F32)
        pick = next_to("pick", [P, 2, TOPK], F32)
        idxn = next_to("idxn", [P, TOPK], U32)
        idxu = next_to("idxu", [P, 2, TOPK], U32)
        idxv = next_to("idxv", [P, 2, TOPK], U32)
        topc = next_to("topc", [P, TOPK], F32)
        ex = next_to("ex", [P, TOPK], F32)
        act_a = next_to("act_a", [P, TOPK], F32)
        dots = next_to("dots", [P, TOPK], F32)
        wgt = next_to("wgt", [P, TOPK], F32)
        tick = next_to("tick", [P, 2 * TOPK + 8], F32)
        esm = next_to("esm", [P, 8], F32)
        expert_end = used[0]
        assert max(mixer_end, expert_end) <= top, (mixer_end, expert_end)

        def pair(name):
            return ctx.enter_context(nc.psum_tensor(name, [P, 2 * CW], F32))

        acc = [pair("acc0"), pair("acc1")]
        mix = [pair("mix0"), pair("mix1")]

        def sem(name):
            return ctx.enter_context(nc.semaphore(name))

        x_in = [sem(f"x_in{b}") for b in range(NB)]
        par_in, wsm_in, gup_in, gb_in = sem("par_in"), sem("wsm_in"), sem("gup_in"), sem("gb_in")
        keys_in, nffn_in, nfin_in, p_in, wple_in = (sem(n) for n in ("keys_in", "nffn_in", "nfin_in", "p_in", "wple_in"))
        raw_in = [sem(f"raw_in{q}") for q in range(NQ)]
        hi_done, lo_done, slice_used = sem("hi_done"), sem("lo_done"), sem("slice_used")
        acc_free = [sem(f"acc_free{i}") for i in range(2)]
        mix_ready = sem("mix_ready")
        mix_free = [sem(f"mix_free{i}") for i in range(2)]
        const_ready, mask_ready = sem("const_ready"), sem("mask_ready")
        tf_ready, thi_done, tlo_done = sem("tf_ready"), sem("thi_done"), sem("tlo_done")
        ssq_ready, var_ready, sqrt_ready = sem("ssq_ready"), sem("var_ready"), sem("sqrt_ready")
        src_ready = sem("src_ready")
        smw_hi, smw_lo, sm_ready, smt_ready = sem("smw_hi"), sem("smw_lo"), sem("sm_ready"), sem("smt_ready")
        abs_ready, softp = sem("abs_ready"), sem("softp")
        diff_ready, decay_ready, qk_ready = sem("diff_ready"), sem("decay_ready"), sem("qk_ready")
        st_ready = sem("st_ready")
        hsq_ready, hvar_ready, hsqrt_ready = sem("hsq_ready"), sem("hvar_ready"), sem("hsqrt_ready")
        tap0_ready, conv_ready, silu_ready, rows_ready = (
            sem(n) for n in ("tap0_ready", "conv_ready", "silu_ready", "rows_ready"))
        out_copied = sem("out_copied")
        expo_ready, wexp_ready = sem("expo_ready"), sem("wexp_ready")
        denr_ready = sem("denr_ready")
        keyst_ready = sem("keyst_ready")
        rs_ready = sem("rs_ready")
        xn2_ready, h_ready, h_chunk = sem("xn2_ready"), sem("h_ready"), sem("h_chunk")
        idx_ready, idx_taken, idx_moved = sem("idx_ready"), sem("idx_taken"), sem("idx_moved")
        u_in = [sem(f"u_in{i}") for i in range(DEEP)]
        v_in = [sem(f"v_in{i}") for i in range(DEEP)]
        v_free_dve = sem("v_free_dve")
        u_free, v_free = sem("u_free"), sem("v_free")
        top_ready, gelu_ready, w_ready, diag_ready = sem("top_ready"), sem("gelu_ready"), sem("w_ready"), sem("diag_ready")
        exp_ready = sem("exp_ready")
        peer_ready, peer_taken = sem("peer_ready"), sem("peer_taken")
        pt_ready, ple_ready, gate_ready, gate_last = sem("pt_ready"), sem("ple_ready"), sem("gate_ready"), sem("gate_last")
        out_ready = [sem(f"out_ready{b}") for b in range(NB)]
        out_done = sem("out_done")

        names = ["par"] + [f"tA{i}" for i in range(4)] + ["sm", "smt", "z"]
        names += ["lvd", "cols", "mbc"] + [f"lv{n}" for n in range(LEVELS + 1)] + ["go0", "go1"]
        names += ["ps", "psx", "den", "mo0", "mo1"]
        names += [f"tB{i}" for i in range(4)] + ["tQ0", "key0", "key1", "tQ1", "tQ2", "tQ3"]
        names += [f"sc{c}" for c in range(ND)]
        n_before_peer = len(names)
        names += ["pt"] + [f"pl{c}" for c in range(ND)] + [f"tG{i}" for i in range(4)]
        M = {n: i for i, n in enumerate(names)}

        def ple_tile(c):
            return (ple01 if c < 2 else ple23)[:, c % 2, :, :]

        def mix_of(name):
            return mix[M[name] % 2]

        def wait_mix(eng, name):
            eng.wait_ge(mix_ready, M[name] + 1)

        def free_sem(name):
            return mix_free[M[name] % 2]

        def take_mix(pe, name):
            m = M[name]
            if m >= n_before_peer and m < n_before_peer + 2:
                pe.wait_ge(peer_taken, 1)
            elif m >= 2:
                pe.wait_ge(mix_free[m % 2], m // 2)

        def item(phase, i):
            return (i % 2, i // 2) if phase in "AB" else (i // 2, i % 2)

        small_t = y[0:2 * NSM, 0, 0:S]

        def src_blocks(phase):
            return {"A": h, "B": y, "G": h}[phase]

        def part(t, phase, i):
            if phase == "Q":
                return t[:, 4 * i:4 * i + 4, :]
            b, kh = item(phase, i)
            return t[:, kh * 8:kh * 8 + 8, b * P:(b + 1) * P]

        def staged(phase, i):
            t = tfp[:, i % 2, :, :]
            return t.rearrange("p k t -> p (k t)").rearrange("p (k t) -> p k t", t=S) if phase == "Q" else t

        dve_picks = range(DEEP - 1, TOPK, DEEP)
        pe_picks = [k for k in range(TOPK) if k not in dve_picks]

        def free_before(k):
            return DEEP + (G - 1) * TOPK + pe_picks.index(k - DEEP) + 1

        L0 = 11
        PH_NO = {"A": 0, "B": 1, "Q": 2, "G": 3}

        with nc.Block() as block:

            @block.sync
            def _(sp):
                for b in range(NB):
                    sp.dma_start(h[:, b, :], x[0, b * P:(b + 1) * P, :]).then_inc(x_in[b], 16)

                sp.wait_ge(par_in, 16 * 8)
                sp.wait_ge(wsm_in, 32)

                def stream(w, g0, n, col0):
                    quarter = slices(w)

                    def chunk(g, col):
                        for q in range(NQ):
                            if not (isinstance(g, int) and g == 0):
                                sp.wait_ge(lo_done, g * NQ + q - NQ + 1)
                            sp.dma_start(raw[:, q, :, :], quarter[q][:, :, col]).then_inc(raw_in[q], 16)

                    first = 1 if g0 == 0 else 0
                    if first:
                        chunk(0, slice(col0, col0 + CW))
                    with sp.Fori(first, n) as c:
                        chunk(c + g0, bass.ds(c * CW + col0, CW))

                stream(w_in[0], 0, 2, 0)
                stream(w_in[0], 2, 2, C2)
                stream(w_in[0], 4, 2, 2 * GQK)
                stream(w_in[0], 6, 2, C2 + 2 * GQK)
                stream(w_in[0], 8, 2, 2 * GQK + W2)
                stream(w_in[0], 10, 2, C2 + 2 * GQK + W2)
                stream(w_out[0], gB, ND, 0)
                stream(peer_query[0], gQ, ND, 0)
                quarter = slices(w_ple_gate[0])
                for q in range(NQ):
                    if q == NQ // 2:
                        sp.wait_ge(v_in[DEEP - 1], 16 * (TOPK // DEEP) * G)
                    sp.wait_ge(lo_done, (gG - 1) * NQ + q + 1)
                    sp.dma_start(raw[:, q, :, :], quarter[q][:, :, 0:CW]).then_inc(raw_in[q], 16)
                sp.wait_ge(xn2_ready, NB)
                sp.dma_start(nrow[:, :], norm_final.partition_broadcast(P)).then_inc(nfin_in, 16)
                stream(w_ple_gate[0], gG + 1, ND - 1, CW)
                for b in range(NB):
                    sp.wait_ge(out_ready[b], 1)
                    sp.dma_start(out[0, b * P:(b + 1) * P, :], hn[:, b, :]).then_inc(out_done, 16)
                sp.wait_ge(out_done, 16 * NB)

            @block.gpsimd
            def _(pool):
                nc.gpsimd.memset(ident[:, :], 0.0)
                pool.drain()
                nc.gpsimd.affine_select(out=ident[:, :], in_=ident[:, :], compare_op=ALU.not_equal, fill=1.0,
                                        base=0, pattern=[[-1, P]], channel_multiplier=1)
                nc.gpsimd.iota(it_i[:, :], pattern=[[1, P]], base=0, channel_multiplier=0)
                nc.gpsimd.iota(it_p[:, :], pattern=[[0, P]], base=0, channel_multiplier=1)
                nc.gpsimd.memset(cbias[:, :], 0.0)
                nc.gpsimd.memset(sel[:, :, :], 0.0)
                nc.gpsimd.memset(ones[:, :], 1.0)
                nc.gpsimd.memset(zero16[:, :], 0.0)
                nc.gpsimd.memset(cin[:, :, 0:CONV - 1], 0.0)
                pool.drain()
                nc.gpsimd.affine_select(out=cbias[:, :], in_=cbias[:, :], compare_op=ALU.is_ge, fill=BIG,
                                        base=0, pattern=[[1, P]], channel_multiplier=-1)
                nc.gpsimd.affine_select(out=sel[:, :, :], in_=sel[:, :, :], compare_op=ALU.not_equal, fill=1.0,
                                        base=0, pattern=[[-1, H], [0, P]], channel_multiplier=1)
                pool.drain().then_inc(const_ready, 1)
                pool.wait_ge(tlo_done, 8)
                pool.dma_start(keys[:, :, :], sub_keys[0].rearrange("h t k d -> k (h t) d")).then_inc(keys_in, 16)
                pool.dma_start(nrow[:, :], norm_ffn[0].partition_broadcast(P)).then_inc(nffn_in, 16)
                nc.gpsimd.iota(ti[:, 0, :], pattern=[[1, TOPK]], base=0, channel_multiplier=0)
                pool.drain()
                nc.gpsimd.tensor_copy(i16[:, :], ti[:, 0, :]).then_inc(const_ready, 1)

                u_rows, v_rows = peer_u[0], peer_v[0]

                def tock(i):
                    c = 2 * TOPK + i
                    nc.gpsimd.tensor_tensor(tick[:, c:c + 1], tick[:, c + 4:c + 5], tick[:, c + 4:c + 5], ALU.add)

                def step(g, e, up, down, lead=0, last=False):
                    if down:
                        pool.wait_ge(idx_taken, g)
                        tock(0)
                        nc.gpsimd.tensor_copy(idxv[:, e, :], idxu[:, 1 - e, :]).then_inc(idx_moved, 1)
                    if up:
                        pool.wait_ge(idx_ready, g + 1)
                        tock(1)
                        nc.gpsimd.tensor_copy(idxu[:, e, :], idxn[:, :]).then_inc(idx_taken, 1)
                        pool.wait_ge(idx_taken, g + 1)
                        tock(2)
                    if down:
                        pool.wait_ge(idx_moved, g)
                        tock(3)
                    if lead:
                        pool.dma_start(wple[:, :, :], w_ple[0].rearrange("(k p) n -> p k n", p=P)).then_inc(wple_in, 16)
                    for i in range(TOPK + lead):
                        if up and i < TOPK:
                            k = i
                            pool.wait_ge(u_free, g * TOPK + k + 1)
                            nc.gpsimd.tensor_tensor(tick[:, 2 * k:2 * k + 1], tick[:, 2 * TOPK + 4:2 * TOPK + 5], tick[:, 2 * TOPK + 5:2 * TOPK + 6], ALU.add)
                            nc.gpsimd.indirect_dma_start(
                                u_ring[:, k % DEEP, :], None, u_rows,
                                bass.IndirectOffsetOnAxis(idxu[:, e, k:k + 1], 0)).then_inc(u_in[k % DEEP], 16)
                        if down and i >= lead:
                            k = i - lead
                            if not last or k < DEEP:
                                pool.wait_ge(v_free, (g - 1) * TOPK + k + 1)
                            elif k in dve_picks:
                                pool.wait_ge(v_free_dve, k // DEEP)
                            else:
                                pool.wait_ge(v_free, free_before(k))
                            nc.gpsimd.tensor_tensor(tick[:, 2 * k + 1:2 * k + 2], tick[:, 2 * TOPK + 4:2 * TOPK + 5], tick[:, 2 * TOPK + 5:2 * TOPK + 6], ALU.add)
                            nc.gpsimd.indirect_dma_start(
                                v_ring[:, k % DEEP, :], None, v_rows,
                                bass.IndirectOffsetOnAxis(idxv[:, e, k:k + 1], 0)).then_inc(v_in[k % DEEP], 16)

                nc.gpsimd.memset(tick[:, :], 0.0)
                pool.drain()
                step(0, 0, True, False)
                pool.wait_ge(slice_used, NQ * gG)
                step(1, 1, True, True)
                with pool.Fori(2, G - 2, 2) as g:
                    step(g, 0, True, True)
                    step(g + 1, 1, True, True)
                pool.dma_start(pin[:, :, :], p[0, 0].rearrange("(b q) n -> q b n", q=P)).then_inc(p_in, 16)
                step(G - 2, 0, True, True)
                step(G - 1, 1, True, True, lead=2)
                step(G, 0, False, True, last=True)

            @block.scalar
            def _(act):
                def rms_square(src, junk, phase_no, b):
                    act.activation(junk, src, ACT.Square, accum_out=stat[:, 2 * phase_no + b:2 * phase_no + b + 1]).then_inc(ssq_ready, 1)

                def rms_sqrt(n, lo, hi):
                    act.wait_ge(var_ready, n)
                    act.activation(stat[:, 16 + lo:16 + hi], stat[:, 8 + lo:8 + hi], ACT.Sqrt).then_inc(sqrt_ready, 1)

                def t_hi_part(phase, items=range(4)):
                    no = PH_NO[phase]
                    for i in items:
                        act.wait_ge(tf_ready, 4 * no + i + 1)
                        act.activation(part(t_hi, phase, i), staged(phase, i), ACT.Copy).then_inc(thi_done, 1)

                def split_hi(s):
                    g, q = s // NQ, s % NQ
                    act.wait_ge(raw_in[q], 16 * (g + 1))
                    if s >= 2:
                        act.wait_ge(slice_used, s - 1)
                    act.activation(w_hi[:, s % 2, :, :], raw[:, q, :, :], ACT.Copy).then_inc(hi_done, 1)

                def copy_out(g, dst, func, scale=1.0):
                    act.wait_ge(slice_used, NQ * (g + 1))
                    act.activation(dst, acc_view(g), func, scale=scale).then_inc(acc_free[g % 2], 1)

                def acc_view(g):
                    if g < 4 or gQ <= g < gG:
                        return acc[g % 2][:, :].rearrange("p (s t) -> p s t", t=S)
                    return acc[g % 2][:, :].rearrange("p (b n) -> p b n", n=CW)

                def rows(dst0, vec, n):
                    act.dma_start(stack[dst0:dst0 + n, :], vec).then_inc(par_in, 16)

                rows(pM, norm_mix.rearrange("a (k p) -> (a k) p", p=P), KT)
                rows(pG, gla_norm.rearrange("a (k p) -> (a k) p", p=P), KT // 2)
                rows(pG + KT // 2, mlstm_norm.rearrange("a (k p) -> (a k) p", p=P), KT // 2)
                rows(pP, norm_ple.rearrange("a (k p) -> (a k) p", p=P), KT)
                rows(pF, norm_ffn.rearrange("a (k p) -> (a k) p", p=P), KT)
                rows(pB, gate_bias.rearrange("a (k p) -> (a k) p", p=P), 4)
                rows(pC, conv_w.rearrange("a t (k p) -> (a t k) p", p=P), 8 * CONV)
                rows(pCB, conv_b.rearrange("a (k p) -> (a k) p", p=P), 8)
                wv = w_in[0].rearrange("(k p) n -> p k n", p=P)
                act.dma_start(wsm[:, :, 0:RANK], wv[:, :, GLR:GLR + RANK]).then_inc(wsm_in, 16)
                act.dma_start(wsm[:, :, RANK:NSM], wv[:, :, GATES:GATES + 2 * H]).then_inc(wsm_in, 16)
                act.dma_start(gup[:, :], gate_up[0]).then_inc(gup_in, 16)
                act.dma_start(gbias[:, 0:1], ig_bias.rearrange("a h -> h a")).then_inc(gb_in, 16)
                act.dma_start(gbias[:, 1:2], fg_bias.rearrange("a h -> h a")).then_inc(gb_in, 16)
                for b in range(NB):
                    act.wait_ge(x_in[b], 16)
                    rms_square(h[:, b, :], y[:, b, :], 0, b)
                    rms_sqrt(b + 1, b, b + 1)
                t_hi_part("A", (0, 1))
                split_hi(0)
                t_hi_part("A", (2,))
                split_hi(1)
                t_hi_part("A", (3,))

                def softplus_parts():
                    pieces = ((tfp[:, 0, :, :], tfp[:, 1, :, :]), (rowm[0:H, 2, :], rowm[0:H, 3, :]))
                    for n, (e, _) in enumerate(pieces):
                        act.wait_ge(abs_ready, n + 1)
                        act.activation(e, e, ACT.Exp, scale=-1.0)
                    act.drain()
                    for e, lnv in pieces:
                        act.activation(lnv, e, ACT.Ln, bias=1.0).then_inc(softp, 1)

                dests = [(gq[:, :, :], ACT.Copy, KSC), (gk[:, :, :], ACT.Copy, 1.0),
                         (cin[:, 0:H, CONV - 1:], ACT.Copy, 1.0), (cin[:, H:2 * H, CONV - 1:], ACT.Copy, 1.0),
                         (gv[:, :, 0:CW], ACT.Copy, 1.0), (gv[:, :, CW:2 * CW], ACT.Copy, 1.0),
                         (mv[:, :, 0:CW], ACT.Copy, 1.0), (mv[:, :, CW:2 * CW], ACT.Copy, 1.0),
                         (y[:, :, 0:CW], ACT.Silu, 1.0), (y[:, :, CW:2 * CW], ACT.Silu, 1.0),
                         (y[:, :, W2:W2 + CW], ACT.Sigmoid, 1.0), (y[:, :, W2 + CW:2 * W2], ACT.Sigmoid, 1.0)]

                def put_out(g):
                    if g == 6:
                        act.wait_ge(sm_ready, 1)
                        act.wait_ge(mask_ready, LEVELS)
                    copy_out(g, *dests[g])

                def decay(lv):
                    act.wait_ge(diff_ready, lv + 1)
                    e = tfp[:, lv % 2, :, :]
                    act.activation(e, e, ACT.Exp, scale=1.0 / TAU).then_inc(decay_ready, 1)

                junk = cum[:, 0, :]

                def head_squares(no, b, src, scale_col, col):
                    act.wait_ge(out_copied, NB * no + b + 1)
                    for n in range(H):
                        i = b * H + n
                        if n or b:
                            act.drain()
                        kw = {} if scale_col is None else {"scale": stat[:, scale_col + i:scale_col + i + 1]}
                        ins = act.activation(junk[:, 0:DV], src[:, b, n * DV:(n + 1) * DV], ACT.Square,
                                             accum_out=stat[:, col + i:col + i + 1], **kw)
                    ins.then_inc(hsq_ready, 1)

                def head_sqrt(no, col):
                    act.wait_ge(hvar_ready, no)
                    act.activation(stat[:, col:col + 8], stat[:, col:col + 8], ACT.Sqrt).then_inc(hsqrt_ready, 1)

                def weights_exp(t):
                    act.wait_ge(expo_ready, 1)
                    tile, kb = ((st2[:, 0], 0), (st2[:, 1], 1), (stx2, 0))[t]
                    for n in range(H):
                        e = tile[:, n, :]
                        ins = act.activation(e, e, ACT.Exp, scale=-1.0, bias=stat[:, 40 + kb * H + n:41 + kb * H + n])
                    ins.then_inc(wexp_ready, 1)

                def act_slot(s):
                    if s == 8:
                        softplus_parts()
                    r = s - L0 - 1
                    if r >= 0 and r % 2 == 0 and r // 2 <= LEVELS:
                        decay(r // 2)
                    if s in (18, 19):
                        act.drain()
                        act.wait_ge(const_ready, 1)
                        for c in range((s - 18) * H, (s - 17) * H):
                            ins = act.activation(conv[:, c, :], cin[:, c, 0:S], ACT.Identity, bias=par[:, pCB + c:pCB + c + 1],
                                                 scale=par[:, pC + c:pC + c + 1])
                        ins.then_inc(tap0_ready, 1)
                    if s in (21, 23, 25):
                        weights_exp((s - 21) // 2)
                    if s == 25:
                        act.activation(stat[:, 48:56], stat[:, 48:56], ACT.Exp).then_inc(wexp_ready, 1)
                    if s == 31:
                        act.wait_ge(conv_ready, 1)
                        act.activation(conv[:, :, :], conv[:, :, :], ACT.Silu).then_inc(silu_ready, 1)
                    if s in (34, 35):
                        head_squares(0, s - 34, gv, None, 24)
                    if s == 37:
                        head_sqrt(1, 24)
                    if s in (39, 40):
                        act.wait_ge(denr_ready, 1)
                        head_squares(1, s - 39, mo, 56, 32)
                    if s == 42:
                        head_sqrt(2, 32)
                    if s == 47:
                        t_hi_part("B", (0, 1))

                act.wait_ge(wsm_in, 32)
                act.activation(wsm_hl[:, :, 0:NSM], wsm[:, :, :], ACT.Copy).then_inc(smw_hi, 1)
                for g in range(NA):
                    for q in range(NQ):
                        if g * NQ + q >= 2:
                            split_hi(g * NQ + q)
                        if q == 1 and g >= 1:
                            put_out(g - 1)
                        act_slot(g * NQ + q)
                split_hi(NQ * gB)
                put_out(NA - 1)
                split_hi(NQ * gB + 1)
                t_hi_part("B", (2, 3))
                for s in range(NQ * gB + 2, NQ * gQ):
                    split_hi(s)
                    if s in (NQ * gQ - 2, NQ * gQ - 1):
                        t_hi_part("Q", (s - NQ * gQ + 2,))
                split_hi(NQ * gQ)
                t_hi_part("Q", (2,))
                split_hi(NQ * gQ + 1)
                t_hi_part("Q", (3,))
                for g in range(gQ, gG):
                    for q in range(NQ):
                        if g * NQ + q >= NQ * gQ + 2:
                            split_hi(g * NQ + q)
                        if (g, q) == (gQ, 2):
                            act.wait_ge(h_ready, NB)
                            for b in range(NB):
                                rms_square(h[:, b, :], xn2[:, b, :], 1, b)
                        if (g, q) == (gQ, 3):
                            rms_sqrt(3, 2, 4)
                        if q == 1 and g > gQ:
                            if g > gQ + 1:
                                wait_mix(act, f"sc{g - gQ - 2}")
                            copy_out(g - 1, qt[:, :, :], ACT.Copy)
                wait_mix(act, f"sc{ND - 2}")
                copy_out(gG - 1, qt[:, :, :], ACT.Copy)

                def softmax_top(g):
                    act.wait_ge(top_ready, g + 1)
                    act.activation(ex[:, :], topc[:, :], ACT.Exp, bias=esm[:, 0:1], accum_out=esm[:, 1:2]).then_inc(exp_ready, 1)

                def gelu_of(g):
                    act.wait_ge(u_free, DEEP + TOPK * (g + 1))
                    act.activation(act_a[:, :], dots[:, :], ACT.Gelu_apprx_tanh).then_inc(gelu_ready, 1)

                def diags(g, picks=range(TOPK)):
                    if picks[0] == 0:
                        act.wait_ge(w_ready, g + 1)
                    for k in picks:
                        act.wait_ge(v_free, g * TOPK + k + 1)
                        act.activation(diag[:, k % DEEP, :], ident[:, :], ACT.Copy, scale=wgt[:, k:k + 1]).then_inc(diag_ready, 1)

                def take_ple(c):
                    wait_mix(act, f"pl{c}")
                    act.activation(ple_tile(c), mix_of(f"pl{c}")[:, :].rearrange("p (b n) -> p b n", b=NB), ACT.Copy).then_inc(free_sem(f"pl{c}"), 1)

                softmax_top(0)
                gelu_of(0)
                with act.Fori(1, G - 1) as g:
                    softmax_top(g)
                    diags(g - 1)
                    gelu_of(g)
                softmax_top(G - 1)
                diags(G - 2, range(0, 4))
                for c in range(ND - 1):
                    diags(G - 2, range(4 * c + 4, 4 * c + 8))
                    if c < ND - 2:
                        take_ple(c)
                gelu_of(G - 1)
                take_ple(ND - 2)
                take_ple(ND - 1)
                act.drain().then_inc(ple_ready, ND)
                act.wait_ge(w_ready, G)
                for k in pe_picks:
                    act.wait_ge(v_free, (G - 1) * TOPK + k + 1 if k < DEEP else free_before(k))
                    act.activation(diag[:, k % DEEP, :], ident[:, :], ACT.Copy, scale=wgt[:, k:k + 1]).then_inc(diag_ready, 1)
                split_hi(NQ * gG)
                split_hi(NQ * gG + 1)
                act.wait_ge(peer_ready, NB)
                act.wait_ge(v_free_dve, len(dve_picks))
                t_hi_part("G", (0, 1))
                t_hi_part("G", (2, 3))

                def gate(c):
                    if c >= 2:
                        act.wait_ge(h_ready, 2 * NB + c - 1)
                    act.wait_ge(slice_used, NQ * (gG + c + 1))
                    for b in range(NB):
                        ins = act.activation(gt[:, c % 2, b, :], acc_view(gG + c)[:, b, :], ACT.Sigmoid, scale=stat[:, 20 + b:21 + b])
                    ins.then_inc(acc_free[(gG + c) % 2], 1)
                    act.drain().then_inc(gate_ready, 1)

                for g in range(gG, gG + ND):
                    for q in range(NQ):
                        if g * NQ + q >= NQ * gG + 2:
                            split_hi(g * NQ + q)
                        if (g, q) == (gG, 2):
                            act.wait_ge(h_ready, 2 * NB)
                            for b in range(NB):
                                rms_square(h[:, b, :], junk_g[b], 2, b)
                        if (g, q) == (gG, 3):
                            rms_sqrt(4, 4, 6)
                        if q == 1 and g == gG + 1:
                            act.wait_ge(rs_ready, 1)
                        if q == 1 and g > gG:
                            gate(g - gG - 1)
                act.wait_ge(h_ready, 2 * NB + ND - 1)
                for b in range(NB):
                    act.activation(junk_g[b][:, 0:3 * CW], h[:, b, 0:3 * CW], ACT.Square, accum_out=stat[:, 24 + b:25 + b]).then_inc(ssq_ready, 1)
                act.wait_ge(slice_used, NQ * (gG + ND))
                for b in range(NB):
                    act.activation(gt[:, (ND - 1) % 2, b, :], acc_view(gG + ND - 1)[:, b, :], ACT.Sigmoid,
                                   scale=stat[:, 20 + b:21 + b]).then_inc(gate_last, 1)
                for b in range(NB):
                    act.wait_ge(h_ready, 2 * NB + ND + b)
                    act.activation(junk_g[b][:, 3 * CW:], h[:, b, 3 * CW:], ACT.Square, accum_out=stat[:, 6 + b:7 + b]).then_inc(ssq_ready, 1)
                rms_sqrt(5, 6, 8)
                act.wait_ge(rs_ready, 2)
                act.activation(hn[:, 1, :], hn[:, 1, :], ACT.Copy, scale=stat[:, 23:24]).then_inc(out_ready[1], 1)

            @block.vector
            def _(dve):
                V = nc.vector

                def rms_scale(n, ssq_count, lo, hi):
                    dve.wait_ge(ssq_ready, ssq_count)
                    v, r, t = stat[:, 8 + lo:8 + hi], stat[:, 16 + lo:16 + hi], nwt[:, 0:hi - lo]
                    V.tensor_scalar(v, stat[:, lo:hi], 1.0 / D, EPS, ALU.mult, ALU.add).then_inc(var_ready, 1)
                    dve.wait_ge(sqrt_ready, n)
                    newton(r, v, t)

                def newton(r, v, t):
                    V.reciprocal(r, r)
                    dve.drain()
                    V.tensor_tensor(t, r, r, ALU.mult)
                    dve.drain()
                    V.tensor_tensor(t, t, v, ALU.mult)
                    dve.drain()
                    V.tensor_scalar(t, t, -0.5, 1.5, ALU.mult, ALU.add)
                    dve.drain()
                    V.tensor_tensor(r, r, t, ALU.mult)
                    dve.drain()

                def t_scale(phase, gain, i):
                    name = f"t{phase}{i}"
                    dve.drain()
                    wait_mix(dve, name)
                    dst = staged(phase, i)
                    n, w = dst.shape[1], dst.shape[2]
                    first = gain + (4 * i if phase == "Q" else 8 * item(phase, i)[1])
                    V.tensor_tensor(dst, mix_of(name)[:, :].rearrange("p (k t) -> p k t", t=w),
                                    par[:, first:first + n].unsqueeze(2).to_broadcast([P, n, w]), ALU.mult).then_inc(free_sem(name), 1)
                    dve.drain().then_inc(tf_ready, 1)

                def t_lo_part(phase, i):
                    dve.wait_ge(thi_done, 4 * PH_NO[phase] + i + 1)
                    V.tensor_tensor(part(t_lo, phase, i), staged(phase, i), part(t_hi, phase, i).bitcast(F32),
                                    ALU.subtract).then_inc(tlo_done, 1)

                def split_lo(s):
                    q = s % NQ
                    dve.wait_ge(hi_done, s + 1)
                    if s >= 2:
                        dve.wait_ge(slice_used, s - 1)
                    V.tensor_tensor(w_lo[:, s % 2, :, :], raw[:, q, :, :], w_hi[:, s % 2, :, :].bitcast(F32),
                                    ALU.subtract).then_inc(lo_done, 1)

                dve.wait_ge(const_ready, 1)
                dve.drain().then_inc(u_free, DEEP)
                dve.drain().then_inc(v_free, DEEP)

                wait_mix(dve, "par")
                V.tensor_copy(par[:, :], mix_of("par")[:, 0:NPAR]).then_inc(free_sem("par"), 1)
                dve.drain()
                for b in range(NB):
                    rms_scale(b + 1, b + 1, b, b + 1)
                    V.tensor_scalar(diag[:, b, :], ident[:, :], stat[:, 16 + b:17 + b], None, ALU.mult).then_inc(src_ready, 1)
                t_scale("A", pM, 0)
                t_scale("A", pM, 1)
                t_lo_part("A", 0)
                t_lo_part("A", 1)
                split_lo(0)
                t_scale("A", pM, 2)
                split_lo(1)
                t_scale("A", pM, 3)
                t_lo_part("A", 2)
                t_lo_part("A", 3)
                dve.wait_ge(smw_hi, 1)
                V.tensor_tensor(wsm_hl[:, :, NSM:2 * NSM], wsm[:, :, :], wsm_hl[:, :, 0:NSM].bitcast(F32), ALU.subtract).then_inc(smw_lo, 1)
                V.tensor_tensor(sm_sum[:, :], ident[0:2 * NSM, 0:NSM], ident[0:2 * NSM, NSM:2 * NSM], ALU.add)

                def small_steps(i):
                    m = mix_of(("sm", "smt", "z")[i])
                    wait_mix(dve, ("sm", "smt", "z")[i])
                    if i == 0:
                        V.tensor_copy(small_t, m[0:2 * NSM, 0:S]).then_inc(free_sem("sm"), 1)
                        dve.drain().then_inc(sm_ready, 1)
                    if i == 1:
                        V.tensor_copy(glr[:, :], m[0:RANK, 0:S])
                        dve.wait_ge(gb_in, 32)
                        V.tensor_scalar(rowm[0:H, 0, :], m[0:H, S:2 * S], gbias[:, 0:1], None, ALU.add)
                        V.tensor_scalar(rowm[0:H, 1, :], m[0:H, 2 * S:3 * S], gbias[:, 1:2], None, ALU.add).then_inc(free_sem("smt"), 1)
                        dve.drain().then_inc(smt_ready, 1)
                    if i == 2:
                        V.tensor_tensor(cum[:, :, :], m[:, :].rearrange("p (h t) -> p h t", t=S),
                                        par[:, pB:pB + H].unsqueeze(2).to_broadcast([P, H, S]), ALU.add).then_inc(free_sem("z"), 1)
                        dve.drain()
                        tf0 = tfp[:, 0, :, :].rearrange("p k t -> p (k t)")
                        zf = cum[:, :, :].rearrange("p h t -> p (h t)")
                        V.scalar_tensor_tensor(tf0, zf, -1.0, zf, ALU.mult, ALU.max).then_inc(abs_ready, 1)
                        V.scalar_tensor_tensor(rowm[0:H, 2, :], rowm[0:H, 1, :], -1.0, rowm[0:H, 1, :], ALU.mult, ALU.max).then_inc(abs_ready, 1)

                def log_decays(i):
                    one = ones[:, 0:1].to_broadcast([P, S])
                    if i == 0:
                        dve.wait_ge(softp, 2)
                        cf = cum[:, :, :].rearrange("p h t -> p (h t)")
                        ln = tfp[:, 1, :, :].rearrange("p k t -> p (k t)")
                        V.scalar_tensor_tensor(cf, cf, 0.0, ln, ALU.min, ALU.subtract)
                        V.scalar_tensor_tensor(rowm[0:H, 1, :], rowm[0:H, 1, :], 0.0, rowm[0:H, 3, :], ALU.min, ALU.subtract)
                    if i == 1:
                        for n in range(H):
                            V.tensor_tensor_scan(cum[:, n, :], one, cum[:, n, :], 0.0, ALU.mult, ALU.add)
                    if i == 2:
                        V.tensor_tensor_scan(rowm[0:H, 1, :], one[0:H], rowm[0:H, 1, :], 0.0, ALU.mult, ALU.add)
                        dve.drain()
                        V.tensor_tensor(rowm[0:H, 0, :], rowm[0:H, 0, :], rowm[0:H, 1, :], ALU.subtract)
                        dve.drain()
                        V.tensor_tensor_scan(rowm[0:H, 3, :], rowm[0:H, 0, :], rowm[0:H, 0, :], 0.0, ALU.max, ALU.max)
                        dve.drain()
                        V.scalar_tensor_tensor(rowm[0:H, 4, :], rowm[0:H, 1, :], -1.0, rowm[0:H, 3, :], ALU.mult, ALU.subtract).then_inc(rows_ready, 1)
                    dve.drain()

                def level_view(t, lv):
                    half = 1 << lv
                    f = t.rearrange("p h t -> p (h t)") if len(t.shape) == 3 else t
                    return f.rearrange("p (n two s) -> p n two s", two=2, s=half)

                def e_tile(lv):
                    return tfp[:, lv % 2, :, :].rearrange("p k t -> p (k t)")

                def differences(lv):
                    if lv >= 2:
                        dve.wait_ge(mix_ready, M[f"lv{lv - 2}"] + 1)
                    half = 1 << lv
                    c, e = level_view(cum[:, :, :], lv), level_view(e_tile(lv), lv)
                    n = H * S // (2 * half)
                    anchor = c[:, :, 0, half - 1:half].to_broadcast([P, n, half])
                    V.tensor_tensor(e[:, :, 1, :], c[:, :, 1, :], anchor, ALU.subtract)
                    V.tensor_tensor(e[:, :, 0, :], anchor, c[:, :, 0, :], ALU.subtract).then_inc(diff_ready, 1)

                def decayed(lv):
                    dve.wait_ge(decay_ready, lv + 1)
                    e = level_view(e_tile(lv), lv)
                    V.tensor_tensor(e[:, :, 1, :], e[:, :, 1, :], level_view(gq[:, :, :], lv)[:, :, 1, :], ALU.mult)
                    V.tensor_tensor(e[:, :, 0, :], e[:, :, 0, :], level_view(gk[:, :, :], lv)[:, :, 0, :], ALU.mult)
                    dve.drain().then_inc(qk_ready, 1)

                def take_level(name, lv):
                    wait_mix(dve, name)
                    if name == f"lv{LEVELS}":
                        V.tensor_copy(stx[:, :, :], mix_of(name)[:, 0:H * P].rearrange("p (h t) -> p h t", t=P)).then_inc(free_sem(name), 1)
                        return
                    V.copy_predicated(st[:, :, :, :].rearrange("p b h t -> p (b h) t"),
                                      mask[:, lv, :].unsqueeze(1).to_broadcast([P, NB * H, P]),
                                      mix_of(name)[:, :].rearrange("p (n t) -> p n t", t=P)).then_inc(free_sem(name), 1)
                    dve.drain()

                def clear_scores_and_make_masks():
                    V.memset(st[:, :, :, :], 0.0)
                    V.tensor_tensor(it_x[:, :], it_i[:, :], it_p[:, :], ALU.bitwise_xor)
                    dve.drain()
                    V.tensor_tensor(it_u[:, :], it_i[:, :], it_p[:, :], ALU.is_gt)
                    V.tensor_scalar(mask[:, LEVELS, :], it_x[:, :], 0.0, None, ALU.is_equal)
                    for lv in range(LEVELS):
                        V.tensor_scalar(it_s[:, :], it_x[:, :], lv, None, ALU.logical_shift_right)
                        dve.drain()
                        V.scalar_tensor_tensor(mask[:, lv, :], it_s[:, :], 1.0, it_u[:, :], ALU.is_equal, ALU.mult)
                        dve.drain().then_inc(mask_ready, 1)

                esm2 = small[:, 0:16]

                def head_var(no, col):
                    dve.wait_ge(hsq_ready, 2 * no)
                    V.tensor_scalar(esm2[:, 0:8], stat[:, col:col + 8], 1.0 / DV, EPS, ALU.mult, ALU.add)
                    dve.drain()
                    V.tensor_copy(stat[:, col:col + 8], esm2[:, 0:8]).then_inc(hvar_ready, 1)

                def head_scale(no, col):
                    dve.wait_ge(hsqrt_ready, no)
                    newton(stat[:, col:col + 8], esm2[:, 0:8], esm2[:, 8:16])

                def conv_tap(t, half):
                    dve.drain()
                    dve.wait_ge(tap0_ready, half + 1)
                    for c in range(half * H, (half + 1) * H):
                        w_ap = par[:, pC + t * 8 + c:pC + t * 8 + c + 1]
                        V.scalar_tensor_tensor(conv[:, c, :], cin[:, c, t:t + S], w_ap, conv[:, c, :], ALU.mult, ALU.add)

                def copy_heads(name, dst):
                    b = int(name[-1])
                    wait_mix(dve, name)
                    V.tensor_copy(dst[:, b, :], mix_of(name)[:, :]).then_inc(free_sem(name), 1)
                    dve.drain().then_inc(out_copied, 1)

                def gated(src, heads, y0, col):
                    for b in range(NB):
                        for n in heads:
                            i = b * H + n
                            yv = y[:, b, y0 + n * DV:y0 + (n + 1) * DV]
                            V.scalar_tensor_tensor(yv, src[:, b, n * DV:(n + 1) * DV], stat[:, col + i:col + i + 1], yv, ALU.mult, ALU.mult)

                def dve_slot(s):
                    if s in (3, 5, 7):
                        small_steps((s - 3) // 2)
                    if s == 4:
                        clear_scores_and_make_masks()
                    if s in (9, 10, 11):
                        log_decays(s - 9)
                    if s == L0 + 2:
                        take_level("lvd", LEVELS)
                    r = s - L0
                    if r >= 0 and r % 2 == 0:
                        n = r // 2
                        if n <= LEVELS:
                            differences(n)
                        if 1 <= n <= LEVELS + 1:
                            decayed(n - 1)
                    if r >= 0 and r % 2 == 1 and 2 <= r // 2 <= LEVELS + 2:
                        take_level(f"lv{r // 2 - 2}", r // 2 - 2)
                        if r // 2 == LEVELS + 2:
                            dve.drain().then_inc(st_ready, 1)
                    if s == L0 + 3:
                        wait_mix(dve, "cols")
                        V.tensor_copy(stat[:, 40:56], mix_of("cols")[:, 0:16]).then_inc(free_sem("cols"), 1)
                        wait_mix(dve, "mbc")
                        mb = mix_of("mbc")[:, :].rearrange("p (h b t) -> p h b t", h=H, b=NB)
                        for b in range(NB):
                            V.tensor_tensor(st2[:, b, :, :], mb[:, :, b, :], cbias[:, :].unsqueeze(1).to_broadcast([P, H, P]), ALU.add)
                        V.tensor_copy(stx2[:, :, :], mb[:, :, 1, :]).then_inc(free_sem("mbc"), 1)
                        dve.drain().then_inc(expo_ready, 1)
                    if s in range(20, 32, 2):
                        conv_tap(1 + (s - 20) // 4, (s - 20) // 2 % 2)
                    if s == 30:
                        dve.drain().then_inc(conv_ready, 1)
                    if s == 33:
                        wait_mix(dve, "go1")
                        copy_heads("go0", gv)
                        copy_heads("go1", gv)
                    if s == 35:
                        dve.wait_ge(wexp_ready, 3)
                        wait_mix(dve, "ps")
                        sv = st2[:, :, :, :].rearrange("p b h t -> p (b h t)")
                        V.scalar_tensor_tensor(sv, mix_of("ps")[:, :], KSC, sv, ALU.mult, ALU.mult).then_inc(free_sem("ps"), 1)
                        wait_mix(dve, "psx")
                        sv = stx2[:, :, :].rearrange("p h t -> p (h t)")
                        V.scalar_tensor_tensor(sv, mix_of("psx")[:, 0:H * P], KSC, sv, ALU.mult, ALU.mult).then_inc(free_sem("psx"), 1)
                        dve.drain().then_inc(st_ready, 1)
                    if s == 36:
                        head_var(1, 24)
                    if s == 37:
                        dn = small[:, 16:24]
                        wait_mix(dve, "den")
                        V.tensor_copy(dn, mix_of("den")[:, 0:8]).then_inc(free_sem("den"), 1)
                        dve.drain()
                        V.scalar_tensor_tensor(stat[:, 56:64], dn, -1.0, dn, ALU.mult, ALU.max)
                        dve.drain()
                        dve.wait_ge(wexp_ready, 4)
                        V.tensor_tensor(stat[:, 56:64], stat[:, 56:64], stat[:, 48:56], ALU.max)
                        dve.drain()
                        V.reciprocal(stat[:, 56:64], stat[:, 56:64])
                        dve.drain().then_inc(denr_ready, 1)
                        copy_heads("mo0", mo)
                    if s == 38:
                        head_scale(1, 24)
                    if s == 39:
                        copy_heads("mo1", mo)
                    if s == 41:
                        head_var(2, 32)
                    if s == 42:
                        dve.wait_ge(acc_free[1], 5)
                        gated(gv, range(H), 0, 24)
                        dve.drain().then_inc(src_ready, 1)
                    if s == 43:
                        head_scale(2, 32)
                        V.tensor_tensor(stat[:, 32:40], stat[:, 32:40], stat[:, 56:64], ALU.mult)
                        dve.drain()
                    if s == 45:
                        t_scale("B", pG, 0)
                    if s == 46:
                        t_scale("B", pG, 1)
                        dve.wait_ge(acc_free[0], 6)
                        gated(mo, range(H // 2), W2, 32)
                    if s == 47:
                        t_lo_part("B", 0)
                        t_lo_part("B", 1)

                for g in range(NA):
                    for q in range(NQ):
                        if g * NQ + q >= 2:
                            split_lo(g * NQ + q)
                        dve_slot(g * NQ + q)
                split_lo(NQ * gB)
                dve.wait_ge(acc_free[1], 6)
                gated(mo, range(H // 2, H), W2, 32)
                dve.drain().then_inc(src_ready, 1)
                split_lo(NQ * gB + 1)
                t_scale("B", pG, 2)
                t_scale("B", pG, 3)
                t_lo_part("B", 2)
                t_lo_part("B", 3)
                def add_chunk(c):
                    g = gB + c
                    dve.wait_ge(slice_used, NQ * (g + 1))
                    hv = h[:, :, c * CW:(c + 1) * CW]
                    V.tensor_tensor(hv, hv, acc[g % 2][:, :].rearrange("p (b n) -> p b n", n=CW), ALU.add).then_inc(acc_free[g % 2], 1)
                    dve.drain().then_inc(h_chunk, 1)

                def take_keys(i):
                    wait_mix(dve, f"key{i}")
                    V.tensor_copy(keyst[:, i * 8:i * 8 + 8, :], mix_of(f"key{i}")[:, :].rearrange("p (k t) -> p k t", t=P)).then_inc(free_sem(f"key{i}"), 1)

                for g in range(gB, gQ):
                    for q in range(NQ):
                        c = g - gB
                        if g * NQ + q >= NQ * gB + 2:
                            split_lo(g * NQ + q)
                        if q == 1 and c > 0:
                            add_chunk(c - 1)
                        if q == 3 and c in (1, 2):
                            t_scale("Q", pF, c - 1)
                        if (c, q) == (2, 1):
                            take_keys(0)
                        if (c, q) == (2, 2):
                            take_keys(1)
                        if (c, q) == (ND - 1, 2):
                            t_lo_part("Q", 0)
                        if (c, q) == (ND - 1, 3):
                            t_scale("Q", pF, 2)
                            t_lo_part("Q", 1)
                split_lo(NQ * gQ)
                add_chunk(ND - 1)
                dve.drain().then_inc(h_ready, NB)
                t_lo_part("Q", 2)
                split_lo(NQ * gQ + 1)
                t_scale("Q", pF, 3)
                t_lo_part("Q", 3)
                dve.drain().then_inc(keyst_ready, 1)

                def take_scores(c):
                    wait_mix(dve, f"sc{c}")
                    for b in range(NB):
                        dst = sc[:, :, :].rearrange("p (b h) n -> p b (h n)", b=NB)[:, b, c * CW:(c + 1) * CW]
                        ins = V.tensor_scalar(dst, mix_of(f"sc{c}")[:, b * CW:(b + 1) * CW], stat[:, 18 + b:19 + b], None, ALU.mult)
                    ins.then_inc(free_sem(f"sc{c}"), 1)

                def top_k(g):
                    V.tensor_copy(s2[:, :, :].rearrange("p a n -> p (a n)").unsqueeze(1), sc[:, bass.ds(g, 1), :])
                    dve.drain()
                    for a in range(2):
                        V.max(tv[:, a, 0:8], s2[:, a, :])
                    dve.drain()
                    for a in range(2):
                        V.max_index(ti[:, a, 0:8], tv[:, a, 0:8], s2[:, a, :])
                        V.match_replace(wk[:, a, :], tv[:, a, 0:8], s2[:, a, :], NEG)
                    dve.drain()
                    for a in range(2):
                        V.max(tv[:, a, 8:16], wk[:, a, :])
                    dve.drain()
                    for a in range(2):
                        V.max_index(ti[:, a, 8:16], tv[:, a, 8:16], wk[:, a, :])
                    V.tensor_tensor(cand[:, :, :], tv[:, 0, :].unsqueeze(2).to_broadcast([P, TOPK, TOPK]),
                                    tv[:, 1, :].unsqueeze(1).to_broadcast([P, TOPK, TOPK]), ALU.add)
                    dve.drain()
                    V.tensor_copy(tif[:, :, :], ti[:, :, :])
                    cf, wf = cand[:, :, :].rearrange("p a n -> p (a n)"), wk[:, :, :].rearrange("p a n -> p (a n)")
                    V.max(cv[:, 0:8], cf)
                    dve.drain()
                    V.max_index(ci[:, 0:8], cv[:, 0:8], cf)
                    V.match_replace(wf, cv[:, 0:8], cf, NEG)
                    dve.drain()
                    V.max(cv[:, 8:16], wf)
                    dve.drain()
                    V.max_index(ci[:, 8:16], cv[:, 8:16], wf)
                    dve.drain()
                    V.tensor_scalar(cij[:, 0, :], ci[:, :], 4, None, ALU.logical_shift_right)
                    V.tensor_scalar(cij[:, 1, :], ci[:, :], TOPK - 1, None, ALU.bitwise_and)
                    dve.drain()
                    V.tensor_copy(cijf[:, :, :], cij[:, :, :])
                    dve.drain()
                    for a in range(2):
                        V.tensor_tensor(oh[:, :, :], cijf[:, a, :].unsqueeze(2).to_broadcast([P, TOPK, TOPK]),
                                        i16[:, :].unsqueeze(1).to_broadcast([P, TOPK, TOPK]), ALU.is_equal)
                        dve.drain()
                        V.tensor_tensor(oh[:, :, :], oh[:, :, :], tif[:, a, :].unsqueeze(1).to_broadcast([P, TOPK, TOPK]), ALU.mult)
                        dve.drain()
                        V.tensor_reduce(pick[:, a, :], oh[:, :, :], AXX, ALU.add)
                        dve.drain()
                    V.scalar_tensor_tensor(pick[:, 0, :], pick[:, 0, :], float(NK), pick[:, 1, :], ALU.mult, ALU.add)
                    dve.drain()
                    if not (isinstance(g, int) and g == 0):
                        dve.wait_ge(idx_taken, g)
                    V.tensor_copy(idxn[:, :], pick[:, 0, :]).then_inc(idx_ready, 1)

                def current_top(g):
                    V.tensor_copy(topc[:, :], cv[:, :])
                    V.tensor_scalar(esm[:, 0:1], cv[:, 0:1], -1.0, None, ALU.mult)
                    dve.drain().then_inc(top_ready, 1)

                def products(g, b, picks=range(TOPK)):
                    for k in picks:
                        dve.wait_ge(u_in[k % DEEP], 16 * (TOPK // DEEP) * g + 16 * (k // DEEP + 1))
                        V.tensor_tensor_reduce(out=u_ring[:, k % DEEP, :], in0=u_ring[:, k % DEEP, :], in1=xn2[:, b, :],
                                               scale=1.0, scalar=0.0, op0=ALU.mult, op1=ALU.add,
                                               accum_out=dots[:, k:k + 1]).then_inc(u_free, 1)

                def weights(g):
                    dve.wait_ge(exp_ready, g + 1)
                    V.reciprocal(esm[:, 2:3], esm[:, 1:2])
                    dve.drain()
                    dve.wait_ge(gelu_ready, g + 1)
                    V.scalar_tensor_tensor(wgt[:, :], ex[:, :], esm[:, 2:3], act_a[:, :], ALU.mult, ALU.mult).then_inc(w_ready, 1)

                dve.wait_ge(const_ready, 2)
                per_slice = {(2, 2): range(0, 2), (2, 3): range(2, 4), (3, 0): range(4, 6), (3, 1): range(6, 9),
                             (3, 2): range(9, 12), (3, 3): range(12, 16)}
                for c in range(ND):
                    for q in range(NQ):
                        if (c, q) >= (0, 2):
                            split_lo((gQ + c) * NQ + q)
                        if (c, q) == (0, 3):
                            rms_scale(3, 4, 2, 4)
                            dve.wait_ge(nffn_in, 16)
                        if (c, q) in ((1, 0), (1, 1)):
                            V.scalar_tensor_tensor(xn2[:, q, :], h[:, q, :], stat[:, 18 + q:19 + q], nrow[:, :],
                                                   ALU.mult, ALU.mult).then_inc(xn2_ready, 1)
                        if q == 3 and c > 0:
                            take_scores(c - 1)
                        if (c, q) == (2, 0):
                            dve.drain()
                            top_k(0)
                            dve.drain()
                            current_top(0)
                        if (c, q) == (3, 0):
                            top_k(1)
                        if (c, q) in per_slice:
                            products(0, 0, per_slice[c, q])
                take_scores(ND - 1)
                weights(0)

                def add_half(b, pairs, i):
                    dve.wait_ge(peer_ready, b + 1)
                    hv = h[:, b, i * 2 * CW:(i + 1) * 2 * CW]
                    V.tensor_tensor(hv, hv, pairs[i][:, :], ALU.add)
                    dve.drain().then_inc(src_ready, 1)

                for b in range(NB):
                    with dve.Fori(max(b * PH, 1), (b + 1) * PH - 2 * (b == NB - 1)) as g:
                        dve.drain()
                        current_top(g)
                        top_k(g + 1)
                        products(g, b)
                        weights(g)
                dve.drain()
                current_top(G - 2)
                top_k(G - 1)
                add_half(0, mix, 0)
                add_half(0, mix, 1)
                dve.drain().then_inc(h_ready, 1)
                dve.drain().then_inc(peer_taken, 1)
                products(G - 2, NB - 1)
                weights(G - 2)
                dve.drain()
                current_top(G - 1)
                wait_mix(dve, "pt")
                V.tensor_copy(pt[:, :, :], mix_of("pt")[:, 0:2 * S].rearrange("p (k t) -> p k t", t=S)).then_inc(free_sem("pt"), 1)
                dve.drain().then_inc(pt_ready, 1)
                products(G - 1, NB - 1)
                weights(G - 1)

                def add_row(k):
                    dve.wait_ge(v_in[k % DEEP], 16 * (TOPK // DEEP) * (G - 1) + 16 * (k // DEEP + 1))
                    V.scalar_tensor_tensor(h[:, 1, :], v_ring[:, k % DEEP, :], wgt[:, k:k + 1], h[:, 1, :],
                                           ALU.mult, ALU.add).then_inc(v_free_dve, 1)
                    dve.drain()

                dve.drain()
                for k in dve_picks:
                    if k == dve_picks[-2]:
                        t_scale("G", pP, 0)
                        t_scale("G", pP, 1)
                    if k == dve_picks[-1]:
                        split_lo(NQ * gG)
                        split_lo(NQ * gG + 1)
                    add_row(k)
                add_half(1, acc, 0)
                t_lo_part("G", 0)
                add_half(1, acc, 1)
                dve.drain().then_inc(h_ready, 1)
                dve.drain().then_inc(peer_taken, 1)
                t_lo_part("G", 1)
                t_scale("G", pP, 2)
                t_scale("G", pP, 3)
                t_lo_part("G", 2)
                t_lo_part("G", 3)

                def gain_of(c):
                    cols = slice(c * CW, (c + 1) * CW)
                    if c == 0:
                        dve.wait_ge(nfin_in, 16)
                    dve.drain()
                    V.tensor_tensor(hn[:, :, cols], h[:, :, cols], nrow[:, cols].unsqueeze(1).to_broadcast([P, NB, CW]), ALU.mult)

                def add_ple(c):
                    dve.wait_ge(gate_ready, c + 1)
                    dve.wait_ge(ple_ready, c + 1)
                    gv_ = gt[:, c % 2, :, :]
                    V.tensor_tensor(gv_, gv_, ple_tile(c), ALU.mult)
                    dve.drain()
                    hv = h[:, :, c * CW:(c + 1) * CW]
                    V.tensor_tensor(hv, hv, gv_, ALU.add).then_inc(h_ready, 1)

                for g in range(gG, gG + ND):
                    for q in range(NQ):
                        if g * NQ + q >= NQ * gG + 2:
                            split_lo(g * NQ + q)
                        if (g, q) == (gG, 3):
                            rms_scale(4, 6, 4, 6)
                            dve.drain().then_inc(rs_ready, 1)
                        if q == 2 and g > gG:
                            add_ple(g - gG - 1)
                            gain_of(g - gG - 1)
                cols = slice((ND - 1) * CW, D)
                for b in range(NB):
                    dve.wait_ge(gate_last, b + 1)
                    gb = gt[:, (ND - 1) % 2, b, :]
                    V.tensor_tensor(gb, gb, ple_tile(ND - 1)[:, b, :], ALU.mult)
                    dve.drain()
                    V.tensor_tensor(h[:, b, cols], h[:, b, cols], gb, ALU.add).then_inc(h_ready, 1)
                gain_of(ND - 1)
                dve.wait_ge(ssq_ready, 10)
                V.tensor_tensor(stat[:, 6:8], stat[:, 6:8], stat[:, 24:26], ALU.add)
                dve.drain()
                rms_scale(5, 10, 6, 8)
                dve.drain().then_inc(rs_ready, 1)
                V.tensor_scalar(hn[:, 0, :], hn[:, 0, :], stat[:, 22:23], None, ALU.mult).then_inc(out_ready[0], 1)

            @block.tensor
            def _(pe):
                T = nc.tensor

                def transposes(phase, items=range(4)):
                    src = src_blocks(phase)
                    for i in items:
                        name = f"t{phase}{i}"
                        b, kh = item(phase, i)
                        pe.wait_ge(src_ready, {"A": b, "B": NB + kh, "G": 2 * NB + 2 * b + kh}[phase] + 1)
                        take_mix(pe, name)
                        for k in range(8):
                            kt = kh * 8 + k
                            o = mix_of(name)[:, k * P:(k + 1) * P]
                            if phase == "A":
                                ins = T.matmul(o, src[:, b, kt * P:(kt + 1) * P], diag[:, b, :], start=True, stop=True)
                            else:
                                ins = T.transpose(o, src[:, b, kt * P:(kt + 1) * P], ident[:, :])
                        ins.then_inc(mix_ready, 1)

                def begin_chunk(set_no, uses):
                    if uses is not None:
                        pe.wait_ge(acc_free[set_no], uses)

                def token_slice(set_no, s_slot, q, lo_count, blocks=range(NB)):
                    pe.wait_ge(lo_done, lo_count)
                    for k in range(KQ):
                        kt = q * KQ + k
                        for b in blocks:
                            tok = slice(b * P, (b + 1) * P)
                            for n, (a, w) in enumerate(((t_hi, w_hi), (t_hi, w_lo), (t_lo, w_hi))):
                                ins = T.matmul(acc[set_no][:, b * CW:(b + 1) * CW], a[:, kt, tok], w[:, s_slot, k, :],
                                               start=(kt == 0 and n == 0), stop=(kt == KT - 1 and n == 2))
                    if blocks[-1] == NB - 1:
                        ins.then_inc(slice_used, 1)

                def column_slice(set_no, s_slot, q, lo_count):
                    pe.wait_ge(lo_done, lo_count)
                    for k in range(KQ):
                        kt = q * KQ + k
                        for c in range(CW // P):
                            for n, (w, a) in enumerate(((w_hi, t_hi), (w_hi, t_lo), (w_lo, t_hi))):
                                ins = T.matmul(acc[set_no][:, c * S:(c + 1) * S], w[:, s_slot, k, c * P:(c + 1) * P], a[:, kt, :],
                                               start=(kt == 0 and n == 0 and c % 2 == 0), stop=(kt == KT - 1 and n == 2),
                                               skip_group_check=True)
                    ins.then_inc(slice_used, 1)

                def chunk(g, kind, after=None):
                    begin_chunk(g % 2, g // 2 if g >= 2 else None)
                    for q in range(NQ):
                        kind(g % 2, (g * NQ + q) % 2, q, g * NQ + q + 1)
                        if after is not None:
                            after(g * NQ + q)

                pe.wait_ge(const_ready, 1)
                pe.wait_ge(par_in, 16 * 8)
                T.transpose(mix_of("par")[:, 0:NPAR], stack[:, :], ident[0:NPAR, 0:NPAR]).then_inc(mix_ready, 1)
                transposes("A")
                pe.wait_ge(tlo_done, 2)

                def small_products():
                    take_mix(pe, "sm")
                    pe.wait_ge(smw_lo, 1)
                    m = mix_of("sm")
                    for kt in range(KT):
                        T.matmul(m[0:2 * NSM, 0:S], wsm_hl[:, kt, :], t_hi[:, kt, :], start=(kt == 0), stop=False, skip_group_check=True)
                        ins = T.matmul(m[0:NSM, 0:S], wsm_hl[:, kt, 0:NSM], t_lo[:, kt, :], start=False, stop=(kt == KT - 1), skip_group_check=True)
                    ins.then_inc(mix_ready, 1)

                def level_item(name, lv):
                    take_mix(pe, name)
                    m = mix_of(name)
                    if name == "lvd":
                        pe.wait_ge(acc_free[1], 1)
                        kk, qq = gk[:, :, :], gq[:, :, :]
                    else:
                        pe.wait_ge(qk_ready, lv + 1)
                        kk = qq = tfp[:, lv % 2, :, :].rearrange("p k t -> p (k t)").rearrange("p (h t) -> p h t", t=S)
                    if lv == LEVELS and name != "lvd":
                        for n in range(H):
                            ins = T.matmul(m[:, n * P:(n + 1) * P], kk[:, n, 0:P], qq[:, n, P:2 * P], start=True, stop=True)
                    else:
                        for b in range(NB):
                            for n in range(H):
                                ins = T.matmul(m[:, (b * H + n) * P:(b * H + n + 1) * P], kk[:, n, b * P:(b + 1) * P],
                                               qq[:, n, b * P:(b + 1) * P], start=True, stop=True)
                    ins.then_inc(mix_ready, 1)

                def attend(name, within, across, values):
                    b = int(name[-1])
                    take_mix(pe, name)
                    for n in range(H):
                        o, cols = mix_of(name)[:, n * DV:(n + 1) * DV], slice(n * DV, (n + 1) * DV)
                        ins = T.matmul(o, within[:, b, n, :], values[:, b, cols], start=True, stop=(b == 0))
                        if b == 1:
                            ins = T.matmul(o, across[:, n, :], values[:, 0, cols], start=False, stop=True)
                    ins.then_inc(mix_ready, 1)

                def pe_slot(s):
                    if s == 1:
                        pe.wait_ge(tlo_done, 4)
                        small_products()
                    if s == 3:
                        take_mix(pe, "smt")
                        pe.wait_ge(sm_ready, 1)
                        m = mix_of("smt")
                        T.matmul(m[0:RANK, 0:S], sm_sum[:, 0:RANK], small_t, start=True, stop=True)
                        T.matmul(m[0:H, S:2 * S], sm_sum[:, RANK:RANK + H], small_t, start=True, stop=True)
                        T.matmul(m[0:H, 2 * S:3 * S], sm_sum[:, RANK + H:NSM], small_t, start=True, stop=True).then_inc(mix_ready, 1)
                    if s == 5:
                        take_mix(pe, "z")
                        pe.wait_ge(smt_ready, 1)
                        pe.wait_ge(gup_in, 16)
                        for n in range(H):
                            ins = T.matmul(mix_of("z")[:, n * S:(n + 1) * S], gup[:, n * DK:(n + 1) * DK], glr[:, :], start=True, stop=True)
                        ins.then_inc(mix_ready, 1)
                    if s == L0:
                        level_item("lvd", LEVELS)
                    if s == L0 + 1:
                        take_mix(pe, "cols")
                        pe.wait_ge(rows_ready, 1)
                        for i, row in enumerate((0, 4)):
                            for b in range(NB):
                                c = i * 8 + b * H
                                ins = T.transpose(mix_of("cols")[:, c:c + H], rowm[0:H, row, b * P:(b + 1) * P], ident[0:H, 0:H])
                        ins.then_inc(mix_ready, 1)
                        take_mix(pe, "mbc")
                        for n in range(H):
                            ins = T.matmul(mix_of("mbc")[:, n * S:(n + 1) * S], sel[:, n, :], rowm[0:H, 3, :], start=True, stop=True)
                        ins.then_inc(mix_ready, 1)
                    r = s - L0
                    if r >= 2 and r % 2 == 0 and r // 2 <= LEVELS + 1:
                        level_item(f"lv{r // 2 - 1}", r // 2 - 1)
                    if s == 31:
                        pe.wait_ge(st_ready, 1)
                        pe.wait_ge(acc_free[1], 3)
                        attend("go0", st, stx, gv)
                        attend("go1", st, stx, gv)
                    if s == 33:
                        take_mix(pe, "ps")
                        pe.wait_ge(silu_ready, 1)
                        for b in range(NB):
                            for n in range(H):
                                ins = T.matmul(mix_of("ps")[:, (b * H + n) * P:(b * H + n + 1) * P], conv[:, H + n, b * P:(b + 1) * P],
                                               conv[:, n, b * P:(b + 1) * P], start=True, stop=True)
                        ins.then_inc(mix_ready, 1)
                        take_mix(pe, "psx")
                        for n in range(H):
                            ins = T.matmul(mix_of("psx")[:, n * P:(n + 1) * P], conv[:, H + n, 0:P], conv[:, n, P:2 * P], start=True, stop=True)
                        ins.then_inc(mix_ready, 1)
                    if s == 35:
                        pe.wait_ge(st_ready, 2)
                        take_mix(pe, "den")
                        for b in range(NB):
                            for n in range(H):
                                o = mix_of("den")[:, b * H + n:b * H + n + 1]
                                ins = T.matmul(o, st2[:, b, n, :], ones[:, :], start=True, stop=(b == 0))
                                if b == 1:
                                    ins = T.matmul(o, stx2[:, n, :], ones[:, :], start=False, stop=True)
                        ins.then_inc(mix_ready, 1)
                        pe.wait_ge(acc_free[1], 4)
                        attend("mo0", st2, stx2, mv)
                    if s == 37:
                        attend("mo1", st2, stx2, mv)
                    if s == 44:
                        transposes("B", (0, 1))

                for g in range(NA):
                    chunk(g, column_slice if g < 4 else token_slice, pe_slot)
                pe.wait_ge(tlo_done, 6)

                def transpose_h(c):
                    pe.wait_ge(h_chunk, c + 1)
                    take_mix(pe, f"tQ{c}")
                    for k in range(4):
                        for b in range(NB):
                            ins = T.transpose(mix_of(f"tQ{c}")[:, (k * NB + b) * P:(k * NB + b + 1) * P],
                                              h[:, b, (4 * c + k) * P:(4 * c + k + 1) * P], ident[:, :])
                    ins.then_inc(mix_ready, 1)

                def after_b(s):
                    r = s - NQ * gB
                    if r == 0:
                        transposes("B", (2, 3))
                    if r == 1:
                        pe.wait_ge(tlo_done, 8)
                    if r in (5, 9, 13):
                        transpose_h(r // 4 - 1)
                    if r == 7:
                        for i in range(2):
                            take_mix(pe, f"key{i}")
                            pe.wait_ge(keys_in, 16)
                            for k in range(8):
                                ins = T.transpose(mix_of(f"key{i}")[:, k * P:(k + 1) * P], keys[:, i * 8 + k, :], ident[:, :])
                            ins.then_inc(mix_ready, 1)

                for g in range(gB, gQ):
                    chunk(g, token_slice, after_b)

                def scores(c):
                    name = f"sc{c}"
                    g = gQ + c
                    take_mix(pe, name)
                    pe.wait_ge(keyst_ready, 1)
                    pe.wait_ge(acc_free[g % 2], g // 2 + 1)
                    for b in range(NB):
                        for a in range(4):
                            ins = T.matmul(mix_of(name)[:, (b * 4 + a) * P:(b * 4 + a + 1) * P], qt[:, a, b * P:(b + 1) * P],
                                           keyst[:, c * 4 + a, :], start=True, stop=True)
                    ins.then_inc(mix_ready, 1)

                for c in range(ND):
                    g = gQ + c
                    begin_chunk(g % 2, g // 2)
                    for q in range(NQ):
                        if c == 0:
                            pe.wait_ge(tlo_done, 8 + q + 1)
                        column_slice(g % 2, q % 2, q, g * NQ + q + 1)
                        if (c, q) == (0, 0):
                            transpose_h(ND - 1)
                        if q == 2 and c >= 1:
                            scores(c - 1)
                scores(ND - 1)

                for b, pairs in enumerate((mix, acc)):
                    if b == 0:
                        for i in range(2):
                            last = max(m for m in range(n_before_peer) if m % 2 == i)
                            pe.wait_ge(mix_free[i], last // 2 + 1)
                    for i in range(2):
                        for j in range(2):
                            T.matmul(pairs[i][:, j * CW:(j + 1) * CW], zero16[:, 0:P], zero16[:, :], start=True, stop=False, skip_group_check=True)

                    def down(g, picks, last=False):
                        for k in picks:
                            pe.wait_ge(diag_ready, g * TOPK + (pe_picks.index(k) if last else k) + 1)
                            pe.wait_ge(v_in[k % DEEP], 16 * (TOPK // DEEP) * g + 16 * (k // DEEP + 1))
                            for j in range(4):
                                ins = T.matmul(pairs[j // 2][:, (j % 2) * CW:(j % 2 + 1) * CW], diag[:, k % DEEP, :],
                                               v_ring[:, k % DEEP, j * CW:(j + 1) * CW], start=False, stop=False, skip_group_check=True)
                            ins.then_inc(v_free, 1)

                    with pe.Fori(b * PH, (b + 1) * PH - 2 * (b == NB - 1)) as g:
                        down(g, range(TOPK))
                    if b == NB - 1:
                        take_mix(pe, "pt")
                        pe.wait_ge(p_in, 16)
                        for bb in range(NB):
                            for k in range(PLE // P):
                                ins = T.transpose(mix_of("pt")[:, k * S + bb * P:k * S + (bb + 1) * P], pin[:, bb, k * P:(k + 1) * P], ident[:, :])
                        ins.then_inc(mix_ready, 1)
                        for c in range(ND):
                            down(G - 2, range(4 * c, 4 * c + 4))
                            take_mix(pe, f"pl{c}")
                            if c == 0:
                                pe.wait_ge(pt_ready, 1)
                                pe.wait_ge(wple_in, 16)
                            for bb in range(NB):
                                for k in range(PLE // P):
                                    ins = T.matmul(mix_of(f"pl{c}")[:, bb * CW:(bb + 1) * CW], pt[:, k, bb * P:(bb + 1) * P],
                                                   wple[:, k, c * CW:(c + 1) * CW], start=(k == 0), stop=(k == PLE // P - 1))
                            ins.then_inc(mix_ready, 1)
                        down(G - 1, pe_picks[:6], last=True)
                        transposes("G", (0, 1))
                        down(G - 1, pe_picks[6:], last=True)
                    for i in range(2):
                        for j in range(2):
                            ins = T.matmul(pairs[i][:, j * CW:(j + 1) * CW], zero16[:, 0:P], zero16[:, :], start=False, stop=True, skip_group_check=True)
                    ins.then_inc(peer_ready, 1)

                for q in range(2):
                    pe.wait_ge(tlo_done, 13)
                    pe.wait_ge(src_ready, 2 * NB + 3)
                    token_slice(gG % 2, q, q, gG * NQ + q + 1, blocks=(0,))
                    transposes("G", (2 + q,))
                pe.wait_ge(tlo_done, 15)
                for q in range(2):
                    token_slice(gG % 2, q, q, gG * NQ + q + 1, blocks=(1,))
                pe.wait_ge(tlo_done, 16)
                for q in range(2, NQ):
                    token_slice(gG % 2, q % 2, q, gG * NQ + q + 1)
                pe.wait_ge(peer_taken, 2)
                for c in range(1, ND):
                    g = gG + c
                    if c >= 2:
                        begin_chunk(g % 2, g // 2)
                    for q in range(NQ):
                        token_slice(g % 2, q % 2, q, g * NQ + q + 1)


_INS = ['x', 'p', 'norm_mix', 'w_in', 'gla_gate_up', 'gla_gate_bias', 'gla_norm', 'mlstm_conv_w', 'mlstm_conv_b',
        'mlstm_igate_bias', 'mlstm_fgate_bias', 'mlstm_norm', 'w_out', 'norm_ffn', 'peer_query', 'peer_sub_keys',
        'peer_u', 'peer_v', 'norm_ple', 'w_ple', 'w_ple_gate', 'norm_final']


def kernel(**inputs):
    import numpy as _np
    import concourse.bacc as _bacc
    from concourse import mybir as _mybir
    from concourse.bass_utils import run_bass_kernel_spmd as _run

    nc = _bacc.Bacc("TRN2", target_bir_lowering=False, num_devices=1)
    arrays, args = {}, []
    for name in _INS:
        a = _np.ascontiguousarray(inputs[name])
        arrays[f"in_{name}_dram"] = a
        args.append(nc.dram_tensor(f"in_{name}_dram", a.shape, _mybir.dt.from_np(a.dtype), kind="ExternalInput").ap())
    shape = tuple(inputs['x'].shape)
    args.append(nc.dram_tensor("out_0_dram", shape, _mybir.dt.float32, kind="ExternalOutput").ap())
    build(nc, *args)
    r = _run(nc, [arrays], core_ids=[0])
    return r.results[0]["out_0_dram"]
```
